# Optimizing a Trainium2 kernel written in Bass

```python
import jax
import jax.numpy as jnp
from jax import lax
import numpy as np

D_MODEL = 1024
BATCH = 1
SEQ = 1024
DEPTH = 1

N_META = 16
D_MIX = D_MODEL
POOL_WIDTH = D_MIX // 2
POOL_WINDOWS = (2, 4, 8, 16)
N_POOL_GROUPS = len(POOL_WINDOWS)
POOL_GROUP_DIM = POOL_WIDTH // N_POOL_GROUPS
MLA_HEADS = 8
QK_NOPE_DIM = 64
QK_ROPE_DIM = 32
QK_HEAD_DIM = QK_NOPE_DIM + QK_ROPE_DIM
V_HEAD_DIM = (D_MIX - POOL_WIDTH) // MLA_HEADS
Q_LORA_RANK = 384
KV_LORA_RANK = 256
IN_WIDTH = POOL_WIDTH + Q_LORA_RANK + KV_LORA_RANK + QK_ROPE_DIM
D_FF = -(-8 * D_MODEL // (3 * 256)) * 256
ROPE_THETA = 10000.0
RMS_EPS = 1e-6
Q_BLOCK = 128

kernel_name = "hymba_pool_mla_hybrid"

def rms_norm(x, g):
    xf = x.astype(jnp.float32)
    y = xf * lax.rsqrt(jnp.mean(xf * xf, axis=-1, keepdims=True) + RMS_EPS)
    return (y * g.astype(jnp.float32)).astype(x.dtype)

def rope_tables(length):
    inv = 1.0 / (ROPE_THETA ** (jnp.arange(0, QK_ROPE_DIM, 2, dtype=jnp.float32) / QK_ROPE_DIM))
    ang = jnp.arange(length, dtype=jnp.float32)[:, None] * inv[None, :]
    return jnp.cos(ang), jnp.sin(ang)

def apply_rope(x, cos, sin):
    x1, x2 = jnp.split(x, 2, axis=-1)
    c = cos.astype(x.dtype)
    s = sin.astype(x.dtype)
    return jnp.concatenate([x1 * c - x2 * s, x1 * s + x2 * c], axis=-1)

def multiscale_pool(u, w_pool, pool_scale):
    B, L, _ = u.shape
    uf = u.astype(jnp.float32)
    cs = jnp.concatenate([jnp.zeros((B, 1, POOL_WIDTH), jnp.float32), lax.cumsum(uf, axis=1)], axis=1)
    t = jnp.arange(L)
    outs = []
    for g, w in enumerate(POOL_WINDOWS):
        sl = slice(g * POOL_GROUP_DIM, (g + 1) * POOL_GROUP_DIM)
        csg = cs[:, :, sl]
        start = jnp.maximum(t + 1 - w, 0)
        count = (t + 1 - start).astype(jnp.float32)
        mean = (csg[:, 1:] - csg[:, start]) / count[None, :, None]
        outs.append(mean - uf[:, :, sl])
    p = jnp.stack(outs, axis=2).astype(u.dtype)
    y = jnp.einsum('blgc,gcd->blgd', p, w_pool).reshape(B, L, POOL_WIDTH)
    return y * pool_scale.astype(y.dtype)

def causal_mla_attention(q_nope, q_rope, k_nope, k_rope, v):
    B, L, H, _ = q_nope.shape
    n_blocks = -(-L // Q_BLOCK)
    Lp = n_blocks * Q_BLOCK
    pad = Lp - L

    def padl(a):
        return jnp.pad(a, [(0, 0), (0, pad)] + [(0, 0)] * (a.ndim - 2))

    q_nope, q_rope, k_nope, k_rope, v = (padl(a) for a in (q_nope, q_rope, k_nope, k_rope, v))

    def blocks(a):
        return jnp.moveaxis(a.reshape(B, n_blocks, Q_BLOCK, *a.shape[2:]), 1, 0)

    qn_b, qr_b = blocks(q_nope), blocks(q_rope)
    key_pos = jnp.arange(Lp)
    scale = QK_HEAD_DIM ** -0.5

    def one_block(args):
        i, qn, qr = args
        s = (jnp.einsum('bqhd,bkhd->bhqk', qn, k_nope)
             + jnp.einsum('bqhr,bkr->bhqk', qr, k_rope)).astype(jnp.float32) * scale
        q_pos = i * Q_BLOCK + jnp.arange(Q_BLOCK)
        mask = key_pos[None, :] <= q_pos[:, None]
        s = jnp.where(mask[None, None], s, -jnp.inf)
        p = jax.nn.softmax(s, axis=-1).astype(v.dtype)
        return jnp.einsum('bhqk,bkhd->bqhd', p, v)

    out = lax.map(one_block, (jnp.arange(n_blocks), qn_b, qr_b))
    return jnp.moveaxis(out, 0, 1).reshape(B, Lp, H, V_HEAD_DIM)[:, :L]

def mla_group(c_q, c_kv, k_rope_raw, cos, sin, q_a_norm_g, w_q_b, kv_a_norm_g, w_kv_b, q_norm_g, k_norm_g):
    B, L, _ = c_q.shape
    q = (rms_norm(c_q, q_a_norm_g) @ w_q_b).reshape(B, L, MLA_HEADS, QK_HEAD_DIM)
    kv = (rms_norm(c_kv, kv_a_norm_g) @ w_kv_b).reshape(B, L, MLA_HEADS, QK_NOPE_DIM + V_HEAD_DIM)
    q_nope, q_rope = q[..., :QK_NOPE_DIM], q[..., QK_NOPE_DIM:]
    k_nope, v = kv[..., :QK_NOPE_DIM], kv[..., QK_NOPE_DIM:]
    q_nope = rms_norm(q_nope, q_norm_g[:QK_NOPE_DIM])
    q_rope = rms_norm(q_rope, q_norm_g[QK_NOPE_DIM:])
    k_nope = rms_norm(k_nope, k_norm_g[:QK_NOPE_DIM])
    k_rope = rms_norm(k_rope_raw, k_norm_g[QK_NOPE_DIM:])
    q_rope = apply_rope(q_rope, cos[:, None, :], sin[:, None, :])
    k_rope = apply_rope(k_rope, cos, sin)
    o = causal_mla_attention(q_nope, q_rope, k_nope, k_rope, v)
    return o.reshape(B, L, MLA_HEADS * V_HEAD_DIM)

def setup_inputs(seed: int = 0) -> dict:
    key = jax.random.key(seed)
    ks = jax.random.split(key, 18)
    f32 = jnp.float32
    nl = DEPTH

    def nrm(k, shape, scale):
        return jax.random.normal(k, shape, f32) * scale

    def gain(k, shape):
        return 1.0 + 0.05 * jax.random.normal(k, shape, f32)

    return {
        'x': nrm(ks[0], (BATCH, SEQ, D_MODEL), 1.0),
        'meta_tokens': nrm(ks[1], (N_META, D_MODEL), 1.0),
        'attn_norm_g': gain(ks[2], (nl, D_MODEL)),
        'w_in': nrm(ks[3], (nl, D_MODEL, IN_WIDTH), D_MODEL ** -0.5),
        'w_pool': nrm(ks[4], (nl, N_POOL_GROUPS, POOL_GROUP_DIM, POOL_GROUP_DIM), POOL_GROUP_DIM ** -0.5),
        'pool_scale': gain(ks[5], (nl, POOL_WIDTH)),
        'q_a_norm_g': gain(ks[6], (nl, Q_LORA_RANK)),
        'w_q_b': nrm(ks[7], (nl, Q_LORA_RANK, MLA_HEADS * QK_HEAD_DIM), Q_LORA_RANK ** -0.5),
        'kv_a_norm_g': gain(ks[8], (nl, KV_LORA_RANK)),
        'w_kv_b': nrm(ks[9], (nl, KV_LORA_RANK, MLA_HEADS * (QK_NOPE_DIM + V_HEAD_DIM)), KV_LORA_RANK ** -0.5),
        'q_norm_g': gain(ks[10], (nl, QK_HEAD_DIM)),
        'k_norm_g': gain(ks[11], (nl, QK_HEAD_DIM)),
        'w_out': nrm(ks[12], (nl, D_MIX, D_MODEL), D_MIX ** -0.5),
        'ffn_norm_g': gain(ks[13], (nl, D_MODEL)),
        'w_gate': nrm(ks[14], (nl, D_MODEL, D_FF), D_MODEL ** -0.5),
        'w_up': nrm(ks[15], (nl, D_MODEL, D_FF), D_MODEL ** -0.5),
        'w_down': nrm(ks[16], (nl, D_FF, D_MODEL), D_FF ** -0.5),
    }

def reference(x, meta_tokens, attn_norm_g, w_in, w_pool, pool_scale, q_a_norm_g, w_q_b,
              kv_a_norm_g, w_kv_b, q_norm_g, k_norm_g, w_out, ffn_norm_g, w_gate, w_up, w_down):
    B = x.shape[0]
    meta = jnp.broadcast_to(meta_tokens.astype(x.dtype)[None], (B, N_META, D_MODEL))
    h = jnp.concatenate([meta, x], axis=1)
    L = h.shape[1]
    cos, sin = rope_tables(L)
    s1 = POOL_WIDTH
    s2 = s1 + Q_LORA_RANK
    s3 = s2 + KV_LORA_RANK
    for l in range(DEPTH):
        z = rms_norm(h, attn_norm_g[l]) @ w_in[l]
        u_pool, c_q, c_kv, k_rope = jnp.split(z, [s1, s2, s3], axis=-1)
        y_pool = multiscale_pool(u_pool, w_pool[l], pool_scale[l])
        y_mla = mla_group(c_q, c_kv, k_rope, cos, sin, q_a_norm_g[l], w_q_b[l],
                          kv_a_norm_g[l], w_kv_b[l], q_norm_g[l], k_norm_g[l])
        h = h + jnp.concatenate([y_pool, y_mla], axis=-1) @ w_out[l]
        g = rms_norm(h, ffn_norm_g[l])
        h = h + (jax.nn.silu(g @ w_gate[l]) * (g @ w_up[l])) @ w_down[l]
    return h[:, N_META:]


_drawn_inputs = setup_inputs


def setup_inputs(seed=0):
    import zlib

    import numpy as np

    out = dict(_drawn_inputs(seed))
    spreads = {}
    factors = {'q_a_norm_g': 8.0,
     'kv_a_norm_g': 8.0,
     'q_norm_g': 8.0,
     'k_norm_g': 8.0,
     'pool_scale': 8.0,
     'ffn_norm_g': 7.23}
    for name, (base, spread) in spreads.items():
        noise = np.random.default_rng([zlib.crc32(name.encode()), seed]).standard_normal(out[name].shape)
        drawn = base * np.exp(spread * noise) if base else spread * noise
        out[name] = jnp.asarray(drawn.astype(out[name].dtype))
    for name, factor in factors.items():
        out[name] = (out[name] * factor).astype(out[name].dtype)
    return out
```

```python
from contextlib import ExitStack

import concourse.bass as bass
from concourse import mybir

F32 = mybir.dt.float32
F32R = mybir.dt.float32r
ALU = mybir.AluOpType
ACT = mybir.ActivationFunctionType
AX = mybir.AxisListType

P = 128
META = 16
EPS = 1e-6
MASKED = -1e30
N_RAW, N_SPLIT = 2, 3
POOL_GROUPS = 4
HEADS = 8
NOPE, ROPE, VDIM = 64, 32, 64
HD = NOPE + ROPE
C_ATTN, C_FFN, C_Z, C_POOL, C_QN, C_KN = 0, 8, 16, 21, 25, 26
N_COLS = 27


def token0(t):
    return 0 if t == 0 else META + P * (t - 1)


def attention_jobs(last):
    jobs, used = [], {"act": 0, "dve": 0}

    def add(kind, e, i, blocks, engine):
        used[engine] += 1
        jobs.append((kind, e, i, blocks, len(jobs), engine, used[engine]))

    for e in range(2):
        for i in range(8):
            blocks = list(range(i + 2))
            for n, b in enumerate(range(0, len(blocks), 4)):
                add("T", e, i, blocks[b:b + 4], "dve" if n == 1 else "act")
            if not (last and e == 1):
                if i == 2:
                    add("q", e, i, [0, 1, 2, 3], "act")
                if i == 3:
                    add("q", e, i, [4, 5, 6, 7], "dve")
                if i == 4:
                    add("k", e, i, [0, 1, 2, 3], "act")
                    add("k", e, i, [4, 5, 6], "dve")
                if i == 5:
                    add("k", e, i, [7, 8], "act")
    return jobs, dict(used)


FIRST_JOBS = [("q", [0, 1, 2, 3], "act"), ("q", [4, 5, 6, 7], "dve"), ("k", [0, 1, 2, 3], "act"),
              ("k", [4, 5, 6], "dve"), ("k", [7, 8], "act")]
S_BANKS = [(0, 1), (1, 1), (2, 1), (3, 2), (0, 2), (2, 2), (0, 2), (2, 3)]
T_PER_HEAD, PREP_PER_HEAD = 14, 5


def build(nc, xT, w_in, w_pool, w_q_b, w_kv_b, w_out, w_gate, w_up, w_down, columns, rows, rope_cos,
          rope_sin, outT):
    D = w_in.shape[1]
    L = xT.shape[1]
    SEQ = L - META
    KT = D // P
    ZW = (L + 2) // 3 + ((L + 2) // 3) % 2
    LP = 3 * ZW
    NT = SEQ // P
    N_FFN = w_gate.shape[2]
    FT = N_FFN // P
    GROUPS = FT // 2
    LOOPS = (GROUPS - 1) // 2
    QW, KVW = w_q_b.shape[2], w_kv_b.shape[2]
    POOLW = POOL_GROUPS * P
    SCALE = float(HD) ** -0.5
    assert GROUPS % 2 == 1 and KT == 8 and NT == 8 and SEQ == 1024 and HEADS == 8

    Q0, KV0 = POOLW, POOLW + 3 * P
    R0 = KV0 + 2 * P
    IN_COLS = [(KV0, P), (KV0 + P, P), (R0, ROPE), (Q0, P), (Q0 + P, P), (Q0 + 2 * P, P)] + \
              [(g * P, P) for g in range(POOL_GROUPS)]
    in_cols = w_in[0].rearrange("(k p) c -> p k c", p=P)
    early = [(in_cols[:, :, c:c + w], KT, w) for c, w in IN_COLS]
    N_KV = len(early)
    early += [(w_kv_b[0, k * P:(k + 1) * P, :], 1, KVW) for k in range(2)]
    N_POOL = len(early)
    early += [(w_pool[0].rearrange("g c d -> c g d"), POOL_GROUPS, P)]
    N_Q = len(early)
    early += [(w_q_b[0, k * P:(k + 1) * P, :], 1, QW) for k in range(3)]
    N_OUT = len(early)
    out_cols = w_out[0].rearrange("(k p) c -> p k c", p=P)
    early += [(out_cols[:, :, d * P:(d + 1) * P], KT, P) for d in range(KT)]
    N_F = len(early)
    assert N_F % N_SPLIT == 0 and N_F % N_RAW == 0
    gate_t = w_gate[0].rearrange("(k p) (f c) -> f p k c", p=P, c=P)
    up_t = w_up[0].rearrange("(k p) (f c) -> f p k c", p=P, c=P)
    down_t = w_down[0].rearrange("(f p) c -> f p c", p=P)
    N_ALL = N_F + 3 * FT
    PER = 12
    N_L = N_F + 4

    with ExitStack() as ctx:
        def sem(name):
            return ctx.enter_context(nc.semaphore(name))

        cursor = [nc.sbuf_base + (-nc.sbuf_base) % 32]

        def size(shape):
            n = 4
            for s in shape[1:]:
                n *= s
            return n + (-n) % 32

        def take(name, shape, dt=F32):
            t = nc.alloc_sbuf_tensor_at(name, shape, dt, offset=cursor[0])
            cursor[0] += size(shape)
            assert cursor[0] <= nc.sbuf_top, (name, cursor[0] - nc.sbuf_top)
            return t

        w_raw = [take(f"w_raw{i}", [P, 1024]) for i in range(N_RAW)]
        w_hi = [take(f"w_hi{i}", [P, 1024], F32R) for i in range(N_SPLIT)]
        w_lo = [take(f"w_lo{i}", [P, 1024], F32R) for i in range(N_SPLIT)]
        ident = take("ident", [P, P])
        ones = take("ones", [P, P])
        causal = take("causal", [P, P])
        cols = take("cols", [P, N_COLS])
        gains = take("gains", [P, 2 * ROPE])
        q_cos = take("q_cos", [P, NT, ROPE])
        q_sin = take("q_sin", [P, NT, ROPE])
        eps = take("eps", [P, 1])
        meta_rows = take("meta_rows", [P, 1])
        q_scale_col = take("q_scale_col", [P, 1])
        h_ms = take("h_ms", [P, NT + 1])
        h_root = take("h_root", [P, NT + 1])
        r_h = take("r_h", [P, NT + 1])
        r_h2 = take("r_h2", [P, NT + 1])
        kv_sum = take("kv_sum", [P, NT + 1])
        q_sum = take("q_sum", [P, NT])
        kv_ms = take("kv_ms", [P, NT + 1])
        kv_root = take("kv_root", [P, NT + 1])
        kv_inv = take("kv_inv", [P, NT + 1])
        s_kv = take("s_kv", [P, NT + 1])
        q_ms = take("q_ms", [P, NT])
        q_root = take("q_root", [P, NT])
        q_inv = take("q_inv", [P, NT])
        s_q = take("s_q", [P, NT])
        nmax = take("nmax", [P, 2])
        nmax2 = take("nmax2", [P, 2, 2])
        denom = take("denom", [P, 2])
        denom2 = take("denom2", [P, 2, 2])
        rdenom = take("rdenom", [P, 2])
        QN, KN, QR, KR = 0, NT * HEADS, (2 * NT + 1) * HEADS, (3 * NT + 1) * HEADS
        N_SS = KR + NT + 1
        krn = take("krn", [P, NT + 1, ROPE])
        ssq = take("ssq", [P, N_SS])
        rs = take("rs", [P, N_SS])
        yp_at = cursor[0]
        yp_hi = take("yp_hi", [P, POOL_GROUPS, SEQ], F32R)
        yp_lo = take("yp_lo", [P, POOL_GROUPS, SEQ], F32R)
        base = cursor[0]

        h_hi = [take(f"h_hi{k}", [P, LP], F32R) for k in range(KT)]
        h_lo = [take(f"h_lo{k}", [P, LP], F32R) for k in range(KT)]
        z_hi = [take(f"z_hi{k}", [P, LP], F32R) for k in range(5)]
        z_lo = [take(f"z_lo{k}", [P, LP], F32R) for k in range(5)]
        late = cursor[0]
        h_raw = [take(f"h_raw{i}", [P, LP]) for i in range(2)]
        square = take("square", [P, LP])
        h_sq = take("h_sq", [P, LP])
        z_sq = take("z_sq", [P, LP])
        r_bcast = take("r_bcast", [P, LP])
        zr = take("zr", [ROPE, LP])
        u, win = h_raw[0], [h_raw[1], square]

        cursor[0] = base
        kvn = take("kvn", [P, NT + 1, KVW])
        qn = take("qn", [P, NT, QW])
        attn_at = cursor[0]
        cos2 = take("cos2", [P, NT + 1, ROPE])
        sin2 = take("sin2", [P, NT + 1, ROPE])
        cursor[0] = late
        sq_tmp = [take(f"sq_tmp{i}", [P, QW]) for i in range(2)]
        kr_b = take("kr_b", [P, NT + 1, ROPE])
        k_cos = take("k_cos", [P, NT + 1, ROPE])
        k_sin = take("k_sin", [P, NT + 1, ROPE])
        kr_a = take("kr_a", [P, NT + 1, ROPE])
        assert cursor[0] <= late + 3 * size([P, LP])

        cursor[0] = attn_at
        qs = take("qs", [P, NT, HD])
        ks = take("ks", [P, NT + 1, HD])
        vs = [take(f"vs{b}", [P, NT + 1, VDIM]) for b in range(2)]
        qT = [take(f"qT{b}", [HD, SEQ]) for b in range(2)]
        kT = [take(f"kT{b}", [HD, L]) for b in range(2)]
        rope_v = take("rope_v", [P, NT, ROPE])
        rope_a = take("rope_a", [P, NT, ROPE])
        rope_b = take("rope_b", [P, NT, ROPE])
        assert cursor[0] <= late
        prob = [take(f"prob{b}", [P, L]) for b in range(2)]
        probT = take("probT", [P, NT + 1, P])
        assert cursor[0] <= nc.sbuf_top - 2 * size([P, HEADS // 2, SEQ])
        ya_at = nc.sbuf_top - 2 * size([P, HEADS // 2, SEQ]) - 32
        ya_at -= ya_at % 32
        cursor[0] = ya_at
        ya_hi = take("ya_hi", [P, HEADS // 2, SEQ], F32R)
        ya_lo = take("ya_lo", [P, HEADS // 2, SEQ], F32R)

        cursor[0] = base
        resid = take("resid", [P, KT, SEQ])
        g_hi = take("g_hi", [P, KT, SEQ], F32R)
        g_lo = take("g_lo", [P, KT, SEQ], F32R)
        r_sq = take("r_sq", [P, SEQ])
        r_sq_tmp = take("r_sq_tmp", [P, SEQ])
        assert cursor[0] <= ya_at

        cursor[0] = yp_at
        r2 = take("r2", [P, SEQ])
        r2_root = take("r2_root", [P, SEQ])
        gate_in = take("gate_in", [P, SEQ])
        gate = take("gate", [P, SEQ])
        up = take("up", [P, SEQ])
        act = take("act", [P, SEQ])
        assert cursor[0] <= base
        cursor[0] = ya_at
        act_hi = [[take(f"act_hi{s}{j}", [P, SEQ], F32R) for j in range(2)] for s in range(2)]
        act_lo = [[take(f"act_lo{s}{j}", [P, SEQ], F32R) for j in range(2)] for s in range(2)]

        ps = ctx.enter_context(nc.psum_tensor("ps", [P, 8, 512], F32))
        psf = ps[:, :, :].rearrange("p b c -> p (b c)")

        columns_landed = sem("columns_landed")
        rope_landed = sem("rope_landed")
        raw_landed = [sem(f"raw_landed{i}") for i in range(N_RAW)]
        w_hi_ready = sem("w_hi_ready")
        w_lo_ready = sem("w_lo_ready")
        w_used = sem("w_used")
        h_landed = [sem(f"h_landed{i}") for i in range(2)]
        pad_ready = sem("pad_ready")
        h_hi_ready = sem("h_hi_ready")
        h_sq_ready = sem("h_sq_ready")
        h_lo_ready = sem("h_lo_ready")
        h_sq_added = sem("h_sq_added")
        const_ready = sem("const_ready")
        z_hi_ready = sem("z_hi_ready")
        z_act_done = sem("z_act_done")
        z_dve_done = sem("z_dve_done")
        z_sq_added = sem("z_sq_added")
        aux_done = sem("aux_done")
        aux_act = sem("aux_act")
        aux_dve = sem("aux_dve")
        dve_step = sem("dve_step")
        pool_step = sem("pool_step")
        h_ms_ready = sem("h_ms_ready")
        h_root_ready = sem("h_root_ready")
        r_h_ready = sem("r_h_ready")
        kv_ms_ready = sem("kv_ms_ready")
        kv_root_ready = sem("kv_root_ready")
        s_kv_ready = sem("s_kv_ready")
        q_ms_ready = sem("q_ms_ready")
        q_root_ready = sem("q_root_ready")
        s_q_ready = sem("s_q_ready")
        p_ready = sem("p_ready")
        p_hi_ready = sem("p_hi_ready")
        p_lo_ready = sem("p_lo_ready")
        proj_done = sem("proj_done")
        proj_act = sem("proj_act")
        yp_lo_ready = sem("yp_lo_ready")
        sq_ready = sem("sq_ready")
        ssq_added = sem("ssq_added")
        root_ready = sem("root_ready")
        rs_ready = sem("rs_ready")
        q_scale_ready = sem("q_scale_ready")
        qs_ready = sem("qs_ready")
        ks_ready = sem("ks_ready")
        vs_ready = sem("vs_ready")
        prepT_done = sem("prepT_done")
        probT_done = sem("probT_done")
        bank_act = sem("bank_act")
        bank_dve = sem("bank_dve")
        s_done = sem("s_done")
        mask_done = sem("mask_done")
        max2_done = sem("max2_done")
        max_done = sem("max_done")
        exp_done = sem("exp_done")
        denom_done = sem("denom_done")
        rdenom_done = sem("rdenom_done")
        prob_ready = sem("prob_ready")
        pv_done = sem("pv_done")
        y_hi_ready = sem("y_hi_ready")
        y_taken = sem("y_taken")
        resid_landed = sem("resid_landed")
        h2_ready = sem("h2_ready")
        g_hi_ready = sem("g_hi_ready")
        g_sq_ready = sem("g_sq_ready")
        g_lo_ready = sem("g_lo_ready")
        g_sq_added = sem("g_sq_added")
        ms2_done = sem("ms2_done")
        r2_root_ready = sem("r2_root_ready")
        r2_ready = sem("r2_ready")
        gate_in_ready = sem("gate_in_ready")
        silu_ready = sem("silu_ready")
        up_ready = sem("up_ready")
        act_ready = sem("act_ready")
        act_hi_ready = sem("act_hi_ready")
        act_lo_ready = sem("act_lo_ready")
        down_done = sem("down_done")
        down_bank_free = sem("down_bank_free")
        out_landed = sem("out_landed")

        Z_OF_STEP = {0: 0, 1: 1, 3: 2, 4: 3, 5: 4}
        ACT_READS = [1, 2, 3, 4, 5, 6, 6, 6, 6, 6]
        DVE_READS = [1, 2, 2, 3, 4, 5, 6, 7, 8, 9]
        N_STEPS = len(IN_COLS)
        J_POOL, J_Q, N_JOBS = NT + 1, NT + 1 + POOL_GROUPS, 2 * NT + 1 + POOL_GROUPS

        JOB_ENDS = {J_POOL - 1: N_POOL, J_Q - 1: N_Q, N_JOBS - 1: N_OUT}

        def z_banks(step):
            return 3 * (step % 2)

        def job_bank(job):
            return 2 * ((job + 3) % 4)

        def wait_for_job(engine, j):
            if j in JOB_ENDS:
                engine.wait_ge(w_used, JOB_ENDS[j])
            else:
                engine.wait_ge(proj_done, j + 1 - sum(1 for e in JOB_ENDS if e < j))

        def in_loop(i, per, c):
            return c if i is None else i * per + c

        def raw_count(n):
            return 16 * (n // N_RAW + 1)

        block = ctx.enter_context(nc.Block())

        @block.sync
        def _(sp):
            def load_weights(n):
                src, k, w = early[n]
                if n >= N_RAW:
                    sp.wait_ge(w_lo_ready, n - N_RAW + 1)
                dst = w_raw[n % N_RAW][:, 0:k * w]
                if k > 1:
                    dst = dst.rearrange("p (k c) -> p k c", k=k)
                sp.dma_start(dst, src).then_inc(raw_landed[n % N_RAW], 16)

            def load_h(k):
                if k >= 2:
                    sp.wait_ge(h_sq_ready, k - 1)
                    sp.wait_ge(h_lo_ready, k - 1)
                sp.dma_start(h_raw[k % 2][:, 0:L], xT[k * P:(k + 1) * P, :])\
                  .then_inc(h_landed[k % 2], 16)

            sp.dma_start(cols[:, :], columns).then_inc(columns_landed, 16)
            load_weights(0)
            load_h(0)
            load_weights(1)
            sp.dma_start(gains[:, :], rows).then_inc(columns_landed, 16)
            for k in range(1, KT):
                load_h(k)
            for n in range(2, N_STEPS + 2):
                load_weights(n)
            sp.wait_ge(w_used, N_STEPS)
            sp.dma_start(cos2[:, :, :], rope_cos).then_inc(rope_landed, 16)
            sp.dma_start(sin2[:, :, :], rope_sin).then_inc(rope_landed, 16)
            for n in range(N_STEPS + 2, N_OUT + 2):
                load_weights(n)
            sp.wait_ge(qs_ready, HEADS)
            sp.wait_ge(ks_ready, HEADS)
            sp.wait_ge(vs_ready, HEADS)
            for d in range(KT):
                sp.dma_start(resid[:, d, :], xT[d * P:(d + 1) * P, META:L]).then_inc(resid_landed, 16)
                sp.wait_ge(resid_landed, 16 * (d + 1))
            for n in range(N_OUT + 2, N_F):
                load_weights(n)

            def load_ffn(src, c, i):
                sp.wait_ge(w_lo_ready, in_loop(i, PER, c - N_RAW + 1))
                dst = w_raw[c % N_RAW][:, :]
                if len(src.shape) == 3:
                    dst = dst.rearrange("p (k c) -> p k c", k=KT)
                sp.dma_start(dst, src).then_inc(raw_landed[c % N_RAW], 16)

            def load_gate_up(f, c, i):
                for j in range(2):
                    load_ffn(gate_t[f + j], c + 2 * j, i)
                    load_ffn(up_t[f + j], c + 2 * j + 1, i)

            def load_down(f, c, i):
                for j in range(2):
                    load_ffn(down_t[f + j], c + j, i)

            load_gate_up(0, N_F, None)
            with sp.Fori(0, LOOPS) as i:
                load_gate_up(i * 4 + 2, N_L, i)
                load_down(i * 4, N_L + 4, i)
                load_gate_up(i * 4 + 4, N_L + 6, i)
                load_down(i * 4 + 2, N_L + 10, i)
            load_down(FT - 2, N_ALL - 2, None)
            for d in range(KT):
                sp.wait_ge(down_bank_free, 4 + 16 * (GROUPS - 1) + 2 * (d + 1))
                sp.dma_start(outT[d * P:(d + 1) * P, :], resid[:, d, :]).then_inc(out_landed, 16)
            sp.wait_ge(out_landed, 16 * KT)

        @block.gpsimd
        def _(pool):
            steps = [0]

            def link(ins):
                steps[0] += 1
                ins.then_inc(pool_step, 1)
                pool.wait_ge(pool_step, steps[0])

            pool.memset(ident[:, :], 0.0).then_inc(pool_step, 1)
            pool.memset(causal[:, :], 0.0).then_inc(pool_step, 1)
            pool.memset(ones[:, :], 1.0).then_inc(const_ready, 1)
            pool.memset(eps[:, :], EPS).then_inc(const_ready, 1)
            pool.memset(meta_rows[:, :], 1.0).then_inc(pool_step, 1)
            steps[0] = 3
            pool.wait_ge(pool_step, 3)
            pool.affine_select(out=ident[:, :], in_=ident[:, :], compare_op=ALU.not_equal, fill=1.0,
                               base=0, pattern=[[-1, P]], channel_multiplier=1).then_inc(const_ready, 1)
            pool.affine_select(out=causal[:, :], in_=causal[:, :], compare_op=ALU.is_ge, fill=MASKED,
                               base=0, pattern=[[-1, P]], channel_multiplier=1).then_inc(const_ready, 1)
            pool.affine_select(out=meta_rows[:, :], in_=meta_rows[:, :], compare_op=ALU.is_ge, fill=0.0,
                               base=META - 1, pattern=[[0, 1]], channel_multiplier=-1)\
                .then_inc(const_ready, 1)

            pool.wait_ge(columns_landed, 32)
            pool.wait_ge(rope_landed, 32)
            pool.wait_ge(p_lo_ready, POOL_GROUPS)
            H = ROPE // 2

            def table(out, trig, n, g, swapped):
                for a in range(2):
                    b = 1 - a if swapped else a
                    last = pool.tensor_tensor(
                        out[:, :, a * H:(a + 1) * H], trig[:, NT + 1 - n:, a * H:(a + 1) * H],
                        gains[:, None, g + b * H:g + (b + 1) * H].to_broadcast([P, n, H]), ALU.mult)
                return last

            table(q_cos, cos2, NT, 0, False)
            table(q_sin, sin2, NT, 0, True)
            table(k_cos, cos2, NT + 1, ROPE, False)
            link(table(k_sin, sin2, NT + 1, ROPE, True))

            def squares(job, src, out):
                pool.wait_ge(proj_act, job + 1)
                pool.tensor_tensor(out, src, src, ALU.mult).then_inc(sq_ready, 1)

            for t in range(NT + 1):
                if t >= 2:
                    pool.wait_ge(ssq_added, t - 1)
                squares(t, kvn[:, t, :].rearrange("p (h c) -> p h c", h=HEADS)[:, :, 0:NOPE],
                        sq_tmp[t % 2][:, 0:HEADS * NOPE].rearrange("p (h c) -> p h c", h=HEADS))
            for t in range(NT):
                pool.wait_ge(ssq_added, NT + t)
                squares(J_Q + t, qn[:, t, :], sq_tmp[(NT + 1 + t) % 2][:, :])

            def rope(v, cos, sin, a, b, out, n):
                pool.tensor_tensor(a, v, cos[:, :, :], ALU.mult)
                pool.tensor_tensor(b[:, :, 0:H], v[:, :, H:ROPE], sin[:, :, 0:H], ALU.mult)
                return pool.tensor_tensor(b[:, :, H:ROPE], v[:, :, 0:H], sin[:, :, H:ROPE], ALU.mult)

            pool.wait_ge(rs_ready, 1)
            link(pool.tensor_tensor(krn[:, :, :], krn[:, :, :],
                                    rs[:, KR:KR + NT + 1, None].to_broadcast([P, NT + 1, ROPE]), ALU.mult))
            link(rope(krn[:, :, :], k_cos, k_sin, kr_a[:, :, :], kr_b[:, :, :], None, NT + 1))
            link(pool.tensor_tensor(ks[:, :, NOPE:HD], kr_a[:, :, :], kr_b[:, :, :], ALU.add))
            before = steps[0]

            def stat(at, n, h):
                return rs[:, at:at + n * HEADS].rearrange("p (t h) -> p t h", h=HEADS)[:, :, bass.ds(h, 1)]

            def prepare(h):
                if not (isinstance(h, int) and h == 0):
                    pool.wait_ge(prepT_done, h * PREP_PER_HEAD)
                pool.tensor_tensor(rope_v[:, :, :], qn[:, :, bass.ds(h * HD + NOPE, ROPE)],
                                   stat(QR, NT, h).to_broadcast([P, NT, ROPE]), ALU.mult)\
                    .then_inc(pool_step, 1)
                pool.tensor_tensor(qs[:, :, 0:NOPE], qn[:, :, bass.ds(h * HD, NOPE)],
                                   stat(QN, NT, h).to_broadcast([P, NT, NOPE]), ALU.mult)
                pool.wait_ge(pool_step, h * 2 + before + 1)
                rope(rope_v[:, :, :], q_cos, q_sin, rope_a[:, :, :], rope_b[:, :, :], None, NT)\
                    .then_inc(pool_step, 1)
                pool.wait_ge(pool_step, h * 2 + before + 2)
                pool.tensor_tensor(qs[:, :, NOPE:HD], rope_a[:, :, :], rope_b[:, :, :], ALU.add)\
                    .then_inc(qs_ready, 1)
                pool.tensor_tensor(ks[:, :, 0:NOPE], kvn[:, :, bass.ds(h * (NOPE + VDIM), NOPE)],
                                   stat(KN, NT + 1, h).to_broadcast([P, NT + 1, NOPE]), ALU.mult)\
                    .then_inc(ks_ready, 1)

            prepare(0)
            with pool.Fori(1, HEADS) as h:
                prepare(h)

        @block.scalar
        def _(act_e):
            a = act_e

            def split_hi(c, i=None):
                w = 1024 if c >= N_F else early[c][1] * early[c][2]
                a.wait_ge(raw_landed[c % N_RAW], in_loop(i, 16 * PER // N_RAW, raw_count(c)))
                if c >= N_SPLIT:
                    a.wait_ge(w_used, in_loop(i, PER, c - N_SPLIT + 1))
                a.activation(w_hi[c % N_SPLIT][:, 0:w], w_raw[c % N_RAW][:, 0:w], ACT.Copy)\
                    .then_inc(w_hi_ready, 1)

            a.wait_ge(columns_landed, 16)
            a.wait_ge(pad_ready, 2)
            split_hi(0)
            for k in range(KT):
                a.wait_ge(h_landed[k % 2], 16 * (k // 2 + 1))
                a.activation(h_hi[k][:, :], h_raw[k % 2][:, :], ACT.Identity,
                             scale=cols[:, C_ATTN + k:C_ATTN + k + 1]).then_inc(h_hi_ready, 1)
                if k == 0:
                    split_hi(1)
                if k >= 2:
                    a.wait_ge(h_sq_added, k - 1)
                a.activation((square if k else h_sq)[:, :], h_raw[k % 2][:, :], ACT.Square)\
                    .then_inc(h_sq_ready, 1)

            def z_view(step, rows=P):
                b = z_banks(step)
                return ps[0:rows, b:b + 3, 0:ZW]

            def tiles3(t, rows=P):
                return t[0:rows, :].rearrange("p (b c) -> p b c", b=3)

            for s in range(N_STEPS):
                split_hi(s + 2)
                if s in Z_OF_STEP:
                    z = Z_OF_STEP[s]
                    a.wait_ge(w_used, s + 1)
                    a.activation(tiles3(z_hi[z]), z_view(s), ACT.Identity,
                                 scale=cols[:, C_Z + z:C_Z + z + 1]).then_inc(z_hi_ready, 1)
                    if s == 1:
                        a.wait_ge(h_sq_added, KT - 1)
                    if s == 3:
                        a.wait_ge(aux_done, 2)
                    if s == 4:
                        a.wait_ge(z_sq_added, 1)
                    if s == 5:
                        a.wait_ge(z_sq_added, 2)
                    dst = {0: z_sq, 1: square, 3: h_sq, 4: square, 5: square}[s]
                    a.activation(tiles3(dst), z_view(s), ACT.Square).then_inc(z_act_done, 1)
                if s == 2:
                    a.wait_ge(w_used, 3)
                    a.activation(tiles3(zr, ROPE), z_view(2, ROPE), ACT.Copy).then_inc(z_act_done, 1)
                if s == 3:
                    a.wait_ge(h_ms_ready, 1)
                    a.wait_ge(const_ready, 5)
                    a.activation(h_root[:, :], h_ms[:, :], ACT.Sqrt, bias=eps[:, :], scale=1.0 / D)\
                        .then_inc(h_root_ready, 1)
                if s == 4:
                    a.wait_ge(aux_done, 3)
                    a.activation(r_bcast[:, 0:400], ps[:, 6, 0:400], ACT.Copy).then_inc(aux_act, 1)
                    a.activation(r_bcast[:, 400:784], ps[:, 7, 0:384], ACT.Copy).then_inc(aux_act, 1)
                if s == 5:
                    a.wait_ge(aux_done, 4)
                    a.activation(r_bcast[:, 784:1040], ps[:, 6, 0:256], ACT.Copy).then_inc(aux_act, 1)
                if s == 6:
                    a.wait_ge(kv_ms_ready, 1)
                    a.activation(kv_root[:, :], kv_ms[:, :], ACT.Sqrt, bias=eps[:, :])\
                        .then_inc(kv_root_ready, 1)
                if s == 7:
                    a.wait_ge(q_ms_ready, 1)
                    a.activation(q_root[:, :], q_ms[:, :], ACT.Sqrt, bias=eps[:, :])\
                        .then_inc(q_root_ready, 1)
                if s >= 6:
                    g = s - 6
                    a.wait_ge(p_ready, g + 1)
                    a.activation(yp_hi[:, g, :], win[g % 2][:, META:L], ACT.Copy).then_inc(p_hi_ready, 1)

            for j in range(N_JOBS):
                b = job_bank(j)
                if j == 0:
                    split_hi(N_POOL)
                    a.wait_ge(s_kv_ready, 1)
                if j == J_POOL:
                    split_hi(N_Q)
                    split_hi(N_Q + 1)
                if j == J_Q:
                    split_hi(N_Q + 2)
                    a.wait_ge(s_q_ready, 1)
                wait_for_job(a, j)
                if j < J_POOL:
                    a.activation(kvn[:, j, :], psf[:, b * 512:b * 512 + KVW], ACT.Copy,
                                 scale=s_kv[:, j:j + 1]).then_inc(proj_act, 1)
                elif j < J_Q:
                    g = j - J_POOL
                    a.activation(yp_hi[:, g, :], psf[:, b * 512:b * 512 + SEQ], ACT.Copy,
                                 scale=cols[:, C_POOL + g:C_POOL + g + 1]).then_inc(proj_act, 1)
                else:
                    t = j - J_Q
                    a.activation(qn[:, t, :].rearrange("p (b c) -> p b c", b=2),
                                 ps[:, b:b + 2, 0:QW // 2], ACT.Copy,
                                 scale=s_q[:, t:t + 1]).then_inc(proj_act, 1)
            split_hi(N_OUT)
            split_hi(N_OUT + 1)
            a.wait_ge(ssq_added, 2 * NT + 2)
            a.activation(ssq[:, 0:QR], ssq[:, 0:QR], ACT.Sqrt, bias=eps[:, :], scale=1.0 / NOPE)\
                .then_inc(root_ready, 1)
            a.activation(ssq[:, QR:N_SS], ssq[:, QR:N_SS], ACT.Sqrt, bias=eps[:, :], scale=1.0 / ROPE)\
                .then_inc(root_ready, 1)

            def take_values(h, b):
                a.activation(vs[b][:, :, :], kvn[:, :, bass.ds(h * (NOPE + VDIM) + NOPE, VDIM)],
                             ACT.Copy).then_inc(vs_ready, 1)

            def prep_out(kind, blocks, b):
                if kind == "q":
                    return qT[b][:, blocks[0] * P:(blocks[-1] + 1) * P], q_scale_col
                return kT[b][:, token0(blocks[0]):token0(blocks[-1]) + (META if blocks[-1] == 0 else P)], \
                    cols[:, C_KN:C_KN + 1]

            def prep_evac(kind, blocks, idx, b):
                out, gain = prep_out(kind, blocks, b)
                a.activation(out, ps[0:HD, 5 + idx % 2, 0:out.shape[1]], ACT.Copy, scale=gain[0:HD, :])\
                    .then_inc(bank_act, 1)

            def exponentials(p, u):
                a.wait_ge(max_done, p * 16 + u + 1)
                i, x = u % 8, u % 2
                bank, nb = S_BANKS[i]
                n = META + P * (i + 1)
                m = nmax[:, x:x + 1]
                if nb < 3:
                    a.activation(prob[x][:, 0:n].rearrange("p (b c) -> p b c", b=nb),
                                 ps[:, bank:bank + nb, 0:n // nb], ACT.Exp, bias=m,
                                 accum_out=denom[:, x:x + 1]).then_inc(exp_done, 1)
                else:
                    a.activation(prob[x][:, 0:704].rearrange("p (b c) -> p b c", b=2),
                                 ps[:, bank:bank + 2, 0:352], ACT.Exp, bias=m,
                                 accum_out=denom2[:, x, 0:1])
                    a.activation(prob[x][:, 704:n], ps[:, bank + 2, 0:n - 704], ACT.Exp, bias=m,
                                 accum_out=denom2[:, x, 1:2]).then_inc(exp_done, 1)

            take_values(0, 0)
            for idx, (kind, blocks, engine) in enumerate(FIRST_JOBS):
                if engine == "act":
                    a.wait_ge(prepT_done, idx + 1)
                    if idx == 0:
                        a.wait_ge(q_scale_ready, 1)
                    prep_evac(kind, blocks, idx + 1, 0)
            exponentials(0, 0)
            exponentials(0, 1)

            def pair(p, last):
                jobs, _ = attention_jobs(last)
                for e in range(2):
                    for i in range(8):
                        un = 8 * e + i
                        mine = [j for j in jobs if j[1] == e and j[2] == i]
                        for kind, _, _, blocks, idx, engine, _ in mine:
                            if kind == "T" and engine == "act":
                                n_t = sum(1 for x in jobs[:idx + 1] if x[0] == "T")
                                a.wait_ge(probT_done, p * 2 * T_PER_HEAD + n_t)
                                n = len(blocks)
                                a.activation(probT[:, blocks[0]:blocks[0] + n, :].rearrange("p b c -> p (b c)"),
                                             ps[:, 5 + idx % 2, 0:n * P], ACT.Copy).then_inc(bank_act, 1)
                        if not (last and un + 2 >= 16):
                            exponentials(p, un + 2)
                        if i % 4 == 3:
                            a.wait_ge(pv_done, p * 16 + un + 1)
                            a.activation(ya_hi[VDIM * e:VDIM * (e + 1), bass.ds(p, 1),
                                               512 * (i // 4):512 * (i // 4 + 1)].rearrange("p a c -> p (a c)"),
                                         ps[0:VDIM, 7, :], ACT.Copy).then_inc(y_hi_ready, 1)
                        if i == 3 and not (last and e == 1):
                            take_values(p * 2 + e + 1, 1 - e)
                        for kind, _, _, blocks, idx, engine, _ in mine:
                            if kind != "T" and engine == "act":
                                n_p = sum(1 for x in jobs[:idx + 1] if x[0] != "T")
                                a.wait_ge(prepT_done, p * 2 * PREP_PER_HEAD + PREP_PER_HEAD + n_p)
                                prep_evac(kind, blocks, idx, 1 - e)

            with a.Fori(0, HEADS // 2 - 1) as p:
                pair(p, False)
            pair(HEADS // 2 - 1, True)

            for d in range(KT):
                split_hi(N_OUT + d + 2)
                a.wait_ge(h2_ready, d + 1)
                a.activation(g_hi[:, d, :], resid[:, d, :], ACT.Copy,
                             scale=cols[:, C_FFN + d:C_FFN + d + 1]).then_inc(g_hi_ready, 1)
                if d >= 2:
                    a.wait_ge(g_sq_added, d - 1)
                a.activation((r_sq_tmp if d else r_sq)[:, :], resid[:, d, :], ACT.Square)\
                    .then_inc(g_sq_ready, 1)

            def gate_up(g, c, i, s):
                for j in range(2):
                    t = in_loop(i, 4, 2 * g + j)
                    split_hi(c + 2 * j + 2, i)
                    if i is None and g == 0 and j == 0:
                        a.wait_ge(ms2_done, 1)
                        a.activation(r2_root[:, :], psf[:, 4 * 512:4 * 512 + SEQ], ACT.Sqrt,
                                     bias=eps[:, :], scale=1.0 / D).then_inc(r2_root_ready, 1)
                    a.wait_ge(gate_in_ready, t + 1)
                    if not (i is None and g == 0 and j == 0):
                        a.wait_ge(act_ready, t)
                    a.activation(gate[:, :], gate_in[:, :], ACT.Silu).then_inc(silu_ready, 1)
                    split_hi(c + 2 * j + 3, i)
                    a.wait_ge(act_ready, t + 1)
                    a.activation(act_hi[s][j][:, :], act[:, :], ACT.Copy).then_inc(act_hi_ready, 1)

            def down(c, i):
                for j in range(2):
                    if c + j + 2 < N_ALL:
                        split_hi(c + j + 2, i)

            gate_up(0, N_F, None, 0)
            with a.Fori(0, LOOPS) as i:
                gate_up(1, N_L, i, 1)
                down(N_L + 4, i)
                gate_up(2, N_L + 6, i, 0)
                down(N_L + 10, i)

        @block.vector
        def _(v):
            steps = [0]

            def link(ins):
                steps[0] += 1
                ins.then_inc(dve_step, 1)
                v.wait_ge(dve_step, steps[0])

            def split_lo(c, i=None):
                w = 1024 if c >= N_F else early[c][1] * early[c][2]
                v.wait_ge(w_hi_ready, in_loop(i, PER, c + 1))
                v.tensor_tensor(w_lo[c % N_SPLIT][:, 0:w], w_raw[c % N_RAW][:, 0:w],
                                w_hi[c % N_SPLIT][:, 0:w].bitcast(F32), ALU.subtract)\
                    .then_inc(w_lo_ready, 1)

            for t in (*h_raw, r_bcast):
                v.memset(t[:, L:LP], 0.0).then_inc(pad_ready, 1)
            v.wait_ge(columns_landed, 16)
            split_lo(0)
            for k in range(KT):
                v.wait_ge(h_hi_ready, k + 1)
                v.scalar_tensor_tensor(out=h_lo[k][:, :], in0=h_raw[k % 2][:, :],
                                       scalar=cols[:, C_ATTN + k:C_ATTN + k + 1],
                                       in1=h_hi[k][:, :].bitcast(F32), op0=ALU.mult, op1=ALU.subtract)\
                    .then_inc(h_lo_ready, 1)
                if k == 0:
                    split_lo(1)
                else:
                    v.wait_ge(h_sq_ready, k + 1)
                    if k >= 2:
                        v.wait_ge(h_sq_added, k - 1)
                    v.tensor_tensor(h_sq[:, :], h_sq[:, :], square[:, :], ALU.add).then_inc(h_sq_added, 1)

            def z_view(step):
                b = z_banks(step)
                return ps[:, b:b + 3, 0:ZW]

            def tiles3(t):
                return t[:, :].rearrange("p (b c) -> p b c", b=3)

            def column_sums(out, col, n):
                return v.tensor_reduce(out, psf[:, col:col + n * P].rearrange("p (t c) -> p t c", c=P),
                                       AX.X, ALU.add)

            for s in range(N_STEPS):
                split_lo(s + 2)
                if s in Z_OF_STEP:
                    z = Z_OF_STEP[s]
                    v.wait_ge(z_hi_ready, z + 1)
                    v.wait_ge(z_act_done, ACT_READS[s])
                    v.scalar_tensor_tensor(out=tiles3(z_lo[z]), in0=z_view(s),
                                           scalar=cols[:, C_Z + z:C_Z + z + 1],
                                           in1=tiles3(z_hi[z]).bitcast(F32), op0=ALU.mult,
                                           op1=ALU.subtract).then_inc(z_dve_done, 1)
                    if s in (1, 4, 5):
                        acc = z_sq if s == 1 else h_sq
                        if s == 5:
                            v.wait_ge(z_sq_added, 2)
                        v.tensor_tensor(acc[:, :], acc[:, :], square[:, :], ALU.add)\
                            .then_inc(z_sq_added, 1)
                if s == 2:
                    v.wait_ge(aux_done, 1)
                    column_sums(h_ms[:, 0:NT], 6 * 512, NT).then_inc(aux_dve, 1)
                if s == 3:
                    v.wait_ge(aux_done, 2)
                    column_sums(h_ms[:, NT:NT + 1], 6 * 512, 1).then_inc(h_ms_ready, 1)
                    v.tensor_reduce(kv_sum[:, 0:4], ps[:, 7, :].rearrange("p (t c) -> p t c", c=P),
                                    AX.X, ALU.add)
                    v.wait_ge(h_root_ready, 1)
                    v.reciprocal(r_h[:, :], h_root[:, :]).then_inc(r_h_ready, 1)
                    v.wait_ge(r_h_ready, 1)
                    v.tensor_tensor(krn[:, :, :],
                                    ps[:, 6, P:P + (NT + 1) * ROPE].rearrange("p (t c) -> p t c", c=ROPE),
                                    r_h[:, :, None].to_broadcast([P, NT + 1, ROPE]), ALU.mult)\
                        .then_inc(aux_dve, 1)
                if s == 5:
                    v.wait_ge(aux_done, 4)
                    v.wait_ge(aux_act, 3)
                    column_sums(kv_sum[:, NT:NT + 1], 6 * 512 + 2 * P, 1)
                    link(column_sums(kv_sum[:, 4:NT], 7 * 512, 4))
                    aux_read = v.tensor_tensor(r_h2[:, :], r_h[:, :], r_h[:, :], ALU.mult)
                    aux_read.then_inc(aux_dve, 1)
                    v.wait_ge(aux_dve, 3)
                    v.scalar_tensor_tensor(out=kv_ms[:, :], in0=kv_sum[:, :], scalar=1.0 / (2 * P),
                                           in1=r_h2[:, :], op0=ALU.mult, op1=ALU.mult)\
                        .then_inc(kv_ms_ready, 1)
                if s >= 6:
                    g = s - 6
                    v.wait_ge(w_used, s + 1)
                    if g == 0:
                        v.wait_ge(aux_act, 3)
                        v.wait_ge(pad_ready, 3)
                    else:
                        v.wait_ge(p_hi_ready, g)
                    ub = u[:, :].rearrange("p (b c) -> p b c", b=3)
                    rb = r_bcast[:, :].rearrange("p (b c) -> p b c", b=3)
                    v.tensor_tensor(ub, z_view(s), rb, ALU.mult).then_inc(z_dve_done, 1)
                    v.wait_ge(z_dve_done, DVE_READS[s])
                    src, start = u, 0
                    for j in range(g + 1):
                        shift = 2 ** j
                        dst = win[(1 + g + g - j) % 2]
                        start += shift
                        link(v.tensor_tensor(dst[:, start:L], src[:, start:L],
                                             src[:, start - shift:L - shift], ALU.add))
                        src = dst
                    v.scalar_tensor_tensor(out=win[g % 2][:, META:L], in0=src[:, META:L],
                                           scalar=1.0 / 2 ** (g + 1), in1=u[:, META:L],
                                           op0=ALU.mult, op1=ALU.subtract).then_inc(p_ready, 1)
                    v.wait_ge(p_hi_ready, g + 1)
                    v.tensor_tensor(yp_lo[:, g, :], win[g % 2][:, META:L],
                                    yp_hi[:, g, :].bitcast(F32), ALU.subtract).then_inc(p_lo_ready, 1)
                if s == 6:
                    v.wait_ge(kv_root_ready, 1)
                    link(v.reciprocal(kv_inv[:, :], kv_root[:, :]))
                    link(v.tensor_tensor(s_kv[:, :], kv_inv[:, :], r_h[:, :], ALU.mult))
                    v.tensor_tensor(s_kv[:, 0:1], s_kv[:, 0:1], meta_rows[:, :], ALU.mult)\
                        .then_inc(s_kv_ready, 1)
                    v.wait_ge(aux_done, 5)
                    link(column_sums(q_sum[:, :], 6 * 512, NT))
                    v.scalar_tensor_tensor(out=q_ms[:, :], in0=q_sum[:, :], scalar=1.0 / (3 * P),
                                           in1=r_h2[:, 1:NT + 1], op0=ALU.mult, op1=ALU.mult)\
                        .then_inc(q_ms_ready, 1)
                if s == 7:
                    v.wait_ge(q_root_ready, 1)
                    link(v.reciprocal(q_inv[:, :], q_root[:, :]))
                    v.tensor_tensor(s_q[:, :], q_inv[:, :], r_h[:, 1:NT + 1], ALU.mult)\
                        .then_inc(s_q_ready, 1)
                    v.tensor_scalar(q_scale_col[:, :], cols[:, C_QN:C_QN + 1], SCALE, None, ALU.mult)\
                        .then_inc(q_scale_ready, 1)

            for j in range(N_JOBS):
                b = job_bank(j)
                if j == 0:
                    split_lo(N_POOL)
                if j == J_POOL:
                    split_lo(N_Q)
                    split_lo(N_Q + 1)
                if j == J_Q:
                    split_lo(N_Q + 2)
                if j < J_POOL:
                    v.wait_ge(sq_ready, j + 1)
                    v.tensor_reduce(ssq[:, KN + j * HEADS:KN + (j + 1) * HEADS],
                                    sq_tmp[j % 2][:, 0:HEADS * NOPE].rearrange("p (h c) -> p h c", h=HEADS),
                                    AX.X, ALU.add).then_inc(ssq_added, 1)
                elif j < J_Q:
                    g = j - J_POOL
                    v.wait_ge(proj_act, j + 1)
                    v.scalar_tensor_tensor(out=yp_lo[:, g, :], in0=psf[:, b * 512:b * 512 + SEQ],
                                           scalar=cols[:, C_POOL + g:C_POOL + g + 1],
                                           in1=yp_hi[:, g, :].bitcast(F32), op0=ALU.mult,
                                           op1=ALU.subtract).then_inc(yp_lo_ready, 1)
                else:
                    t = j - J_Q
                    v.wait_ge(sq_ready, NT + 2 + t)
                    squares = sq_tmp[(NT + 1 + t) % 2][:, :].rearrange("p (h c) -> p h c", h=HEADS)
                    v.tensor_reduce(ssq[:, QN + t * HEADS:QN + (t + 1) * HEADS], squares[:, :, 0:NOPE],
                                    AX.X, ALU.add)
                    v.tensor_reduce(ssq[:, QR + t * HEADS:QR + (t + 1) * HEADS], squares[:, :, NOPE:HD],
                                    AX.X, ALU.add).then_inc(ssq_added, 1)
            v.wait_ge(aux_dve, 3)
            link(v.tensor_tensor(kr_b[:, :, :], krn[:, :, :], krn[:, :, :], ALU.mult))
            v.tensor_reduce(ssq[:, KR:N_SS], kr_b[:, :, :], AX.X, ALU.add).then_inc(ssq_added, 1)
            v.wait_ge(root_ready, 2)
            v.reciprocal(rs[:, :], ssq[:, :]).then_inc(rs_ready, 1)
            split_lo(N_OUT)
            split_lo(N_OUT + 1)

            def prep_evac(kind, blocks, idx, b):
                if kind == "q":
                    out, gain = qT[b][:, blocks[0] * P:(blocks[-1] + 1) * P], q_scale_col[0:HD, :]
                else:
                    out, gain = kT[b][:, token0(blocks[0]):token0(blocks[-1]) + P], cols[0:HD, C_KN:C_KN + 1]
                v.tensor_scalar(out, ps[0:HD, 5 + idx % 2, 0:out.shape[1]], gain, None, ALU.mult)\
                    .then_inc(bank_dve, 1)

            def maximum(p, un):
                i, x = un % 8, un % 2
                bank, nb = S_BANKS[i]
                n = META + P * (i + 1)
                width = [n, n // 2, n - 704][nb - 1]
                diagonal = ps[:, bank + nb - 1, width - P:width]
                v.wait_ge(s_done, p * 16 + (un + 1))
                v.tensor_tensor(diagonal, diagonal, causal[:, :], ALU.add).then_inc(mask_done, 1)
                v.wait_ge(mask_done, p * 16 + (un + 1))
                if nb < 3:
                    v.tensor_reduce(nmax[:, x:x + 1], ps[:, bank:bank + nb, 0:width], AX.XY, ALU.max,
                                    negate=True).then_inc(max_done, 1)
                else:
                    v.tensor_reduce(nmax2[:, x, 0:1], ps[:, bank:bank + 2, 0:352], AX.XY, ALU.max)
                    v.tensor_reduce(nmax2[:, x, 1:2], ps[:, bank + 2, 0:width], AX.X, ALU.max)\
                        .then_inc(max2_done, 1)
                    v.wait_ge(max2_done, p * 2 + (1 + un // 8))
                    v.tensor_reduce(nmax[:, x:x + 1], nmax2[:, x, :], AX.X, ALU.max, negate=True)\
                        .then_inc(max_done, 1)

            def normalise(p, un):
                i, x = un % 8, un % 2
                n = META + P * (i + 1)
                v.wait_ge(exp_done, p * 16 + (un + 1))
                if i == 7:
                    v.tensor_reduce(denom[:, x:x + 1], denom2[:, x, :], AX.X, ALU.add)\
                        .then_inc(denom_done, 1)
                    v.wait_ge(denom_done, p * 2 + (1 + un // 8))
                v.reciprocal(rdenom[:, x:x + 1], denom[:, x:x + 1]).then_inc(rdenom_done, 1)
                v.wait_ge(rdenom_done, p * 16 + (un + 1))
                v.tensor_scalar(prob[x][:, 0:n], prob[x][:, 0:n], rdenom[:, x:x + 1], None, ALU.mult)\
                    .then_inc(prob_ready, 1)

            v.sem_inc(y_taken, 1)
            for idx, (kind, blocks, engine) in enumerate(FIRST_JOBS):
                if engine == "dve":
                    v.wait_ge(prepT_done, idx + 1)
                    prep_evac(kind, blocks, idx + 1, 0)
            maximum(0, 0)
            maximum(0, 1)
            normalise(0, 0)

            def pair(p, last):
                jobs, _ = attention_jobs(last)
                for e in range(2):
                    for i in range(8):
                        un = 8 * e + i
                        mine = [j for j in jobs if j[1] == e and j[2] == i]
                        for kind, _, _, blocks, idx, engine, _ in mine:
                            if kind == "T" and engine == "dve":
                                n_t = sum(1 for x in jobs[:idx + 1] if x[0] == "T")
                                v.wait_ge(probT_done, p * (2 * T_PER_HEAD) + n_t)
                                n = len(blocks)
                                v.tensor_copy(probT[:, blocks[0]:blocks[0] + n, :].rearrange("p b c -> p (b c)"),
                                              ps[:, 5 + idx % 2, 0:n * P]).then_inc(bank_dve, 1)
                        if not (last and un + 1 >= 16):
                            normalise(p, un + 1)
                        if not (last and un + 2 >= 16):
                            maximum(p, un + 2)
                        if i % 4 == 3:
                            half = i // 4
                            v.wait_ge(y_hi_ready, p * 4 + (2 * e + half + 1))
                            rows_ = slice(VDIM * e, VDIM * (e + 1))
                            cols_ = slice(512 * half, 512 * (half + 1))
                            v.tensor_tensor(ya_lo[rows_, bass.ds(p, 1), cols_].rearrange("p a c -> p (a c)"),
                                            ps[0:VDIM, 7, :],
                                            ya_hi[rows_, bass.ds(p, 1), cols_].rearrange("p a c -> p (a c)")
                                            .bitcast(F32), ALU.subtract).then_inc(y_taken, 1)
                        for kind, _, _, blocks, idx, engine, _ in mine:
                            if kind != "T" and engine == "dve":
                                n_p = sum(1 for x in jobs[:idx + 1] if x[0] != "T")
                                v.wait_ge(prepT_done, p * (2 * PREP_PER_HEAD) + (PREP_PER_HEAD + n_p))
                                prep_evac(kind, blocks, idx, 1 - e)

            with v.Fori(0, HEADS // 2 - 1) as p:
                pair(p, False)
            pair(HEADS // 2 - 1, True)

            for d in range(KT):
                split_lo(N_OUT + d + 2)
                v.wait_ge(w_used, N_OUT + d + 1)
                v.wait_ge(resid_landed, 16 * (d + 1))
                b = 2 * (d % 2)
                v.tensor_tensor(resid[:, d, :], psf[:, b * 512:b * 512 + SEQ], resid[:, d, :], ALU.add)\
                    .then_inc(h2_ready, 1)
                v.wait_ge(g_hi_ready, d + 1)
                v.scalar_tensor_tensor(out=g_lo[:, d, :], in0=resid[:, d, :],
                                       scalar=cols[:, C_FFN + d:C_FFN + d + 1],
                                       in1=g_hi[:, d, :].bitcast(F32), op0=ALU.mult, op1=ALU.subtract)\
                    .then_inc(g_lo_ready, 1)
                if d >= 1:
                    v.wait_ge(g_sq_ready, d + 1)
                    if d >= 2:
                        v.wait_ge(g_sq_added, d - 1)
                    v.tensor_tensor(r_sq[:, :], r_sq[:, :], r_sq_tmp[:, :], ALU.add)\
                        .then_inc(g_sq_added, 1)

            def gate_up(g, c, i, s):
                for j in range(2):
                    first = i is None and g == 0 and j == 0
                    t = in_loop(i, 4, 2 * g + j)
                    after = in_loop(i, 4, 2 * g + j + 1)
                    split_lo(c + 2 * j + 2, i)
                    if first:
                        v.wait_ge(r2_root_ready, 1)
                        v.reciprocal(r2[:, :], r2_root[:, :]).then_inc(r2_ready, 1)
                        v.wait_ge(r2_ready, 1)
                        v.sem_inc(down_bank_free, 4)
                    else:
                        v.wait_ge(silu_ready, t)
                    v.wait_ge(w_used, in_loop(i, PER, c + 2 * j + 1))
                    v.tensor_tensor(gate_in[:, :], psf[:, 0:SEQ], r2[:, :], ALU.mult)\
                        .then_inc(gate_in_ready, 1)
                    split_lo(c + 2 * j + 3, i)
                    v.wait_ge(w_used, in_loop(i, PER, c + 2 * j + 2))
                    v.tensor_tensor(up[:, :], psf[:, SEQ:2 * SEQ], r2[:, :], ALU.mult).then_inc(up_ready, 1)
                    v.wait_ge(up_ready, after)
                    v.wait_ge(silu_ready, after)
                    v.tensor_tensor(act[:, :], gate[:, :], up[:, :], ALU.mult).then_inc(act_ready, 1)
                    v.wait_ge(act_hi_ready, after)
                    v.tensor_tensor(act_lo[s][j][:, :], act[:, :], act_hi[s][j][:, :].bitcast(F32),
                                    ALU.subtract).then_inc(act_lo_ready, 1)

            def down(g, c, i):
                if c + 2 < N_ALL:
                    split_lo(c + 2, i)
                for x in range(2 * KT):
                    d, half = x // 2, x % 2
                    out = resid[:, d, 512 * half:512 * (half + 1)]
                    if x < 2 * KT - 1:
                        v.wait_ge(down_done, in_loop(i, 2 * (2 * KT - 1), (2 * KT - 1) * g + x + 1))
                    else:
                        v.wait_ge(w_used, in_loop(i, PER, c + 2))
                    v.tensor_tensor(out, ps[:, 4 + x % 4, :], out, ALU.add).then_inc(down_bank_free, 1)
                if c + 3 < N_ALL:
                    split_lo(c + 3, i)

            gate_up(0, N_F, None, 0)
            with v.Fori(0, LOOPS) as i:
                gate_up(1, N_L, i, 1)
                down(0, N_L + 4, i)
                gate_up(2, N_L + 6, i, 0)
                down(1, N_L + 10, i)
            down(GROUPS - 1, N_ALL - 2, None)

        @block.tensor
        def _(pe):
            def passes(out, w_h, w_l, x_h, x_l, first, last):
                pe.matmul(out, w_h, x_h, start=first, stop=False)
                pe.matmul(out, w_h, x_l, start=False, stop=False)
                return pe.matmul(out, w_l, x_h, start=False, stop=last)

            def weights(c, k, width, m):
                s = c % N_SPLIT
                return (w_hi[s][:, k * width:k * width + m], w_lo[s][:, k * width:k * width + m])

            def z_step(s, k):
                w = IN_COLS[s][1]
                w_h, w_l = weights(s, k, w, w)
                for b in range(3):
                    x = slice(b * ZW, (b + 1) * ZW)
                    last = passes(ps[0:w, z_banks(s) + b, 0:ZW], w_h, w_l, h_hi[k][:, x], h_lo[k][:, x],
                                  k == 0, k == KT - 1)
                return last

            def transpose_tiles(src, tiles, col):
                for n, t in enumerate(tiles):
                    last = pe.transpose(psf[:, col + n * P:col + (n + 1) * P],
                                        src[:, token0(t):token0(t) + P], ident[:, :])
                return last

            pe.wait_ge(w_lo_ready, 2)
            for k in range(KT):
                pe.wait_ge(h_lo_ready, k + 1)
                for s in range(2):
                    last = z_step(s, k)
                    if k == KT - 1:
                        last.then_inc(w_used, 1)
            for s in range(2, N_STEPS):
                pe.wait_ge(w_lo_ready, s + 1)
                pe.wait_ge(z_act_done, ACT_READS[s - 2])
                pe.wait_ge(z_dve_done, DVE_READS[s - 2])
                for k in range(KT):
                    last = z_step(s, k)
                last.then_inc(w_used, 1)
                if s == 2:
                    pe.wait_ge(const_ready, 5)
                    pe.wait_ge(h_sq_added, KT - 1)
                    transpose_tiles(h_sq, range(NT), 6 * 512).then_inc(aux_done, 1)
                if s == 3:
                    pe.wait_ge(aux_dve, 1)
                    transpose_tiles(h_sq, [NT], 6 * 512)
                    pe.wait_ge(z_act_done, 3)
                    for t in range(NT + 1):
                        pe.transpose(psf[:, 6 * 512 + P + t * ROPE:6 * 512 + P + (t + 1) * ROPE],
                                     zr[:, token0(t):token0(t) + P], ident[0:ROPE, 0:ROPE])
                    pe.wait_ge(z_sq_added, 1)
                    transpose_tiles(z_sq, range(4), 7 * 512).then_inc(aux_done, 1)
                if s == 4:
                    pe.wait_ge(r_h_ready, 1)
                    pe.wait_ge(aux_dve, 2)
                    pe.matmul(ps[:, 6, 0:META], r_h[0:META, 0:1].to_broadcast([META, P]),
                              ident[0:META, 0:META], start=True, stop=True)
                    for t in range(1, 7):
                        b, at_col = (6, META + (t - 1) * P) if t < 4 else (7, (t - 4) * P)
                        last = pe.matmul(ps[:, b, at_col:at_col + P], r_h[:, t:t + 1].to_broadcast([P, P]),
                                         ident[:, :], start=True, stop=True)
                    last.then_inc(aux_done, 1)
                if s == 5:
                    pe.wait_ge(aux_act, 2)
                    for t in range(7, NT + 1):
                        pe.matmul(ps[:, 6, (t - 7) * P:(t - 6) * P], r_h[:, t:t + 1].to_broadcast([P, P]),
                                  ident[:, :], start=True, stop=True)
                    transpose_tiles(z_sq, [NT], 6 * 512 + 2 * P)
                    transpose_tiles(z_sq, range(4, NT), 7 * 512).then_inc(aux_done, 1)
                if s == 6:
                    pe.wait_ge(aux_dve, 3)
                    pe.wait_ge(z_sq_added, 3)
                    transpose_tiles(h_sq, range(1, NT + 1), 6 * 512).then_inc(aux_done, 1)

            def open_job(j):
                if j == 0:
                    pe.wait_ge(q_ms_ready, 1)
                elif j <= 3:
                    pe.wait_ge(z_dve_done, DVE_READS[-1])
                if j >= 4:
                    pe.wait_ge(proj_act, j - 3)
                    if J_POOL <= j - 4 < J_Q:
                        pe.wait_ge(yp_lo_ready, j - 4 - J_POOL + 1)
                return job_bank(j)

            def token_major(j, t, z0, n_k, tile, width):
                b = open_job(j)
                x = slice(token0(t), token0(t) + P)
                for k in range(n_k):
                    pe.wait_ge(w_lo_ready, tile + k + 1)
                    w_h, w_l = w_hi[(tile + k) % N_SPLIT], w_lo[(tile + k) % N_SPLIT]
                    z_h, z_l = z_hi[z0 + k], z_lo[z0 + k]
                    for half in range(2):
                        c = slice(half * width, (half + 1) * width)
                        last = passes(ps[:, b + half, 0:width], z_h[:, x], z_l[:, x], w_h[:, c], w_l[:, c],
                                      k == 0, k == n_k - 1)
                    if k < n_k - 1 and j in JOB_ENDS:
                        last.then_inc(w_used, 1)
                return last.then_inc(w_used if j in JOB_ENDS else proj_done, 1)

            pe.wait_ge(z_dve_done, DVE_READS[5])
            for t in range(NT + 1):
                token_major(t, t, 0, 2, N_KV, KVW // 2)
            pe.wait_ge(w_lo_ready, N_POOL + 1)
            for g in range(POOL_GROUPS):
                j = J_POOL + g
                b = open_job(j)
                pe.wait_ge(p_lo_ready, g + 1)
                w_h, w_l = weights(N_POOL, g, P, P)
                for half in range(2):
                    x = slice(512 * half, 512 * (half + 1))
                    last = passes(ps[:, b + half, :], w_h, w_l, yp_hi[:, g, x], yp_lo[:, g, x], True, True)
                last.then_inc(w_used if j in JOB_ENDS else proj_done, 1)
            for t in range(NT):
                token_major(J_Q + t, t + 1, 2, 3, N_Q, QW // 2)

            def wait_banks(p, act_n, dve_n):
                pe.wait_ge(bank_act, p * PAIR_USED["act"] + (FIRST_USED["act"] + act_n))
                pe.wait_ge(bank_dve, p * PAIR_USED["dve"] + (FIRST_USED["dve"] + dve_n))

            FIRST_USED = {e: sum(1 for j in FIRST_JOBS if j[2] == e) for e in ("act", "dve")}
            PAIR_USED = attention_jobs(False)[1]

            def prep_transposes(kind, blocks, bank):
                for b in sorted(blocks, key=lambda b: kind == "k" and b == 0):
                    if kind == "q":
                        out, src, n = (b - blocks[0]) * P, qs, P
                    else:
                        out, src, n = token0(b) - token0(blocks[0]), ks, P if b else META
                    last = pe.transpose(ps[0:HD, bank, out:out + n], src[0:n, b, :], ident[0:n, 0:n])
                last.then_inc(prepT_done, 1)

            def scores(p, un, b):
                i = un % 8
                bank, nb = S_BANKS[i]
                n = META + P * (i + 1)
                width = [n, n // 2, 352][nb - 1]
                for m in range(nb):
                    c = slice(m * width, min((m + 1) * width, n))
                    last = pe.matmul(ps[:, bank + m, 0:c.stop - c.start], qT[b][:, i * P:(i + 1) * P],
                                     kT[b][:, c], start=True, stop=True)
                last.then_inc(s_done, 1)

            pe.wait_ge(proj_act, N_JOBS)
            pe.wait_ge(yp_lo_ready, POOL_GROUPS)
            pe.wait_ge(qs_ready, 1)
            pe.wait_ge(ks_ready, 1)
            for idx, (kind, blocks, engine) in enumerate(FIRST_JOBS):
                if idx >= 2:
                    before = [j[2] for j in FIRST_JOBS[:idx - 1]]
                    pe.wait_ge(bank_act if before[-1] == "act" else bank_dve, before.count(before[-1]))
                prep_transposes(kind, blocks, 5 + (idx + 1) % 2)
            pe.wait_ge(bank_act, FIRST_USED["act"])
            pe.wait_ge(bank_dve, FIRST_USED["dve"])
            scores(0, 0, 0)
            scores(0, 1, 0)

            def pair(p, last_pair):
                jobs, _ = attention_jobs(last_pair)

                def open_bank(idx):
                    if idx < 2:
                        engine, count = ("dve", 0) if idx == 0 else ("act", 0)
                    else:
                        engine, count = jobs[idx - 2][5], jobs[idx - 2][6]
                    done = bank_act if engine == "act" else bank_dve
                    pe.wait_ge(done, p * PAIR_USED[engine] + (FIRST_USED[engine] + count))
                    return 5 + idx % 2

                for e in range(2):
                    for i in range(8):
                        un = 8 * e + i
                        mine = [j for j in jobs if j[1] == e and j[2] == i]
                        pe.wait_ge(prob_ready, p * 16 + (un + 1))
                        for kind, _, _, blocks, idx, _, _ in mine:
                            if kind == "T":
                                bank = open_bank(idx)
                                for n, b in enumerate(blocks):
                                    c = token0(b)
                                    last = pe.transpose(ps[:, bank, n * P:(n + 1) * P],
                                                        prob[un % 2][:, c:c + P], ident[:, :])
                                last.then_inc(probT_done, 1)
                        if not (last_pair and un + 2 >= 16):
                            if i == 6:
                                preps = [j for j in jobs if j[1] == e and j[0] != "T"]
                                wait_banks(p, max(j[6] for j in preps if j[5] == "act"),
                                           max(j[6] for j in preps if j[5] == "dve"))
                            pe.wait_ge(exp_done, p * 16 + (un + 1))
                            scores(p, un + 2, e if i < 6 else 1 - e)
                        if i == 0:
                            pe.wait_ge(vs_ready, p * 2 + (e + 1))
                        if i % 4 == 0:
                            pe.wait_ge(y_taken, p * 4 + (2 * e + i // 4 + 1))
                        for kind, _, _, blocks, idx, engine, count in mine:
                            if kind == "T":
                                done = bank_act if engine == "act" else bank_dve
                                pe.wait_ge(done, p * PAIR_USED[engine] + (FIRST_USED[engine] + count))
                                for b in blocks:
                                    last = pe.matmul(ps[0:VDIM, 7, (i % 4) * P:(i % 4 + 1) * P],
                                                     vs[e][:, b, :], probT[:, b, :],
                                                     start=b == 0, stop=b == i + 1)
                        last.then_inc(pv_done, 1)
                        for kind, _, _, blocks, idx, _, _ in mine:
                            if kind != "T":
                                pe.wait_ge(qs_ready if kind == "q" else ks_ready, p * 2 + (e + 2))
                                prep_transposes(kind, blocks, open_bank(idx))

            with pe.Fori(0, HEADS // 2 - 1) as p:
                pair(p, False)
            pair(HEADS // 2 - 1, True)

            y_of = [(yp_hi, yp_lo, k) for k in range(POOL_GROUPS)] + \
                   [(ya_hi, ya_lo, k) for k in range(HEADS // 2)]
            pe.wait_ge(y_taken, 2 * HEADS + 1)
            for d in range(KT):
                n = N_OUT + d
                pe.wait_ge(w_lo_ready, n + 1)
                if d >= 2:
                    pe.wait_ge(h2_ready, d - 1)
                for k, (y_h, y_l, at_k) in enumerate(y_of):
                    w_h, w_l = weights(n, k, P, P)
                    for half in range(2):
                        x = slice(512 * half, 512 * (half + 1))
                        last = passes(ps[:, 2 * (d % 2) + half, :], w_h, w_l, y_h[:, at_k, x],
                                      y_l[:, at_k, x], k == 0, k == KT - 1)
                last.then_inc(w_used, 1)

            def ffn_in(c, i, bank, t, first):
                pe.wait_ge(w_lo_ready, in_loop(i, PER, c + 1))
                for k in range(KT):
                    if first:
                        pe.wait_ge(g_lo_ready, k + 1)
                    w_h, w_l = weights(c, k, P, P)
                    for half in range(2):
                        x = slice(512 * half, 512 * (half + 1))
                        last = passes(ps[:, bank + half, :], w_h, w_l, g_hi[:, k, x], g_lo[:, k, x],
                                      k == 0, k == KT - 1)
                last.then_inc(w_used, 1)

            def gate_up(g, c, i):
                for j in range(2):
                    first = i is None and g == 0 and j == 0
                    t = in_loop(i, 4, 2 * g + j)
                    if first:
                        pe.wait_ge(h2_ready, KT - 1)
                    else:
                        pe.wait_ge(gate_in_ready, t)
                    ffn_in(c + 2 * j, i, 0, t, first)
                    if first:
                        pe.wait_ge(g_sq_added, KT - 1)
                        for half in range(2):
                            last = pe.matmul(ps[:, 4 + half, :], ones[:, :],
                                             r_sq[:, 512 * half:512 * (half + 1)], start=True, stop=True)
                        last.then_inc(ms2_done, 1)
                        pe.wait_ge(h2_ready, KT)
                    else:
                        pe.wait_ge(up_ready, t)
                    ffn_in(c + 2 * j + 1, i, 2, t, False)

            def down(g, c, i, s):
                pe.wait_ge(w_lo_ready, in_loop(i, PER, c + 2))
                pe.wait_ge(act_lo_ready, in_loop(i, 4, 2 * g + 2))
                for x in range(2 * KT):
                    d, half = x // 2, x % 2
                    pe.wait_ge(down_bank_free, in_loop(i, 4 * KT, 2 * KT * g + x + 1))
                    tok = slice(512 * half, 512 * (half + 1))
                    for j in range(2):
                        w_h, w_l = weights(c + j, d, P, P)
                        last = passes(ps[:, 4 + x % 4, :], w_h, w_l, act_hi[s][j][:, tok],
                                      act_lo[s][j][:, tok], j == 0, j == 1)
                        if j == 0 and x == 2 * KT - 1:
                            last.then_inc(w_used, 1)
                    last.then_inc(down_done if x < 2 * KT - 1 else w_used, 1)

            gate_up(0, N_F, None)
            with pe.Fori(0, LOOPS) as i:
                gate_up(1, N_L, i)
                down(0, N_L + 4, i, 0)
                gate_up(2, N_L + 6, i)
                down(1, N_L + 10, i, 1)
            down(GROUPS - 1, N_ALL - 2, None, 0)


def kernel(x, meta_tokens, attn_norm_g, w_in, w_pool, pool_scale, q_a_norm_g, w_q_b, kv_a_norm_g, w_kv_b,
           q_norm_g, k_norm_g, w_out, ffn_norm_g, w_gate, w_up, w_down):
    import numpy as np
    from concourse import bacc
    from concourse.bass_utils import run_bass_kernel_spmd

    x, meta_tokens = np.asarray(x), np.asarray(meta_tokens)
    length = meta_tokens.shape[0] + x.shape[1]
    n_tiles = x.shape[1] // P

    xT = np.ascontiguousarray(np.concatenate([meta_tokens, x[0]], axis=0).T)

    def blocks(g):
        return np.asarray(g)[0].reshape(-1, P).T

    def head_gain(g):
        return np.concatenate([np.asarray(g)[0, :NOPE], np.ones(P - NOPE, np.float32)])[:, None]

    columns = np.ascontiguousarray(np.concatenate(
        [blocks(attn_norm_g), blocks(ffn_norm_g), blocks(kv_a_norm_g), blocks(q_a_norm_g),
         blocks(pool_scale), head_gain(q_norm_g), head_gain(k_norm_g)], axis=1))
    rows = np.ascontiguousarray(np.broadcast_to(
        np.concatenate([np.asarray(q_norm_g)[0, NOPE:], np.asarray(k_norm_g)[0, NOPE:]]), (P, 2 * ROPE)))

    inv = 1.0 / (np.float32(10000.0) ** (np.arange(0, ROPE, 2, dtype=np.float32) / np.float32(ROPE)))
    token = np.stack([token0(t) + np.arange(P) for t in range(n_tiles + 1)], axis=1)
    angle = token.astype(np.float32)[:, :, None] * inv[None, None, :].astype(np.float32)
    cos, sin = np.cos(angle).astype(np.float32), np.sin(angle).astype(np.float32)
    rope_cos = np.ascontiguousarray(np.concatenate([cos, cos], axis=2))
    rope_sin = np.ascontiguousarray(np.concatenate([-sin, sin], axis=2))

    nc = bacc.Bacc("TRN2", target_bir_lowering=False, num_devices=1)
    arrays, args = {}, []
    for name, a in [("xT", xT), ("w_in", w_in), ("w_pool", w_pool), ("w_q_b", w_q_b), ("w_kv_b", w_kv_b),
                    ("w_out", w_out), ("w_gate", w_gate), ("w_up", w_up), ("w_down", w_down),
                    ("columns", columns), ("rows", rows), ("rope_cos", rope_cos), ("rope_sin", rope_sin)]:
        arrays[f"in_{name}"] = np.ascontiguousarray(a)
        args.append(nc.dram_tensor(f"in_{name}", arrays[f"in_{name}"].shape, F32, kind="ExternalInput").ap())
    outT = nc.dram_tensor("outT", (x.shape[2], x.shape[1]), F32, kind="ExternalOutput").ap()
    build(nc, *args, outT)
    got = run_bass_kernel_spmd(nc, [arrays], core_ids=[0]).results[0]["outT"]
    return np.ascontiguousarray(np.asarray(got).T)[None]
```

```python
from contextlib import ExitStack

import concourse.bass as bass
from concourse import mybir

F32 = mybir.dt.float32
F32R = mybir.dt.float32r
ALU = mybir.AluOpType
ACT = mybir.ActivationFunctionType
AX = mybir.AxisListType

P = 128
META = 16
EPS = 1e-6
MASKED = -1e30
N_RAW, N_SPLIT = 2, 3
POOL_GROUPS = 4
HEADS = 8
NOPE, ROPE, VDIM = 64, 32, 64
HD = NOPE + ROPE
C_ATTN, C_FFN, C_Z, C_POOL, C_QN, C_KN = 0, 8, 16, 21, 25, 26
N_COLS = 27


def token0(t):
    return 0 if t == 0 else META + P * (t - 1)


def key0(t):
    return P * t


def misc_fills():
    fills = [("q", [0, 1, 2, 3]), ("q", [4, 5, 6, 7]), ("k", [0, 1, 2, 3]), ("k", [4, 5, 6]), ("k", [7, 8])]
    for i in range(8):
        n = META + P * (i + 1)
        parts = -(-n // 512)
        width = n // parts if parts < 3 else 352
        fills += [("n", i, m, parts, min(width, n - m * width)) for m in range(parts)]
    return fills + [("m",)]


FILLS = misc_fills()
N_FILLS = len(FILLS)
N_PREP = 5
FILL_AT = [(7, 0), (7, 1), (8, 1), (8, 3), (0, 1), (0, 2), (0, 3), (0, 3), (1, 1), (1, 2), (1, 3), (1, 3),
           (2, 1), (2, 2), (2, 3), (2, 3), (3, 1), (3, 2), (3, 3), (4, 1)]
TAIL = 7
KEY_TILES = 9
S_FROM = [0, 112, 240, 368, 416, 624, 752, 768, 768]
AHEAD = 80
P_FROM = [0, 112, 240, 368, 416, 624, 752, 880, 928]


def build(nc, xT, w_in, w_pool, w_q_b, w_kv_b, w_out, w_gate, w_up, w_down, columns, rows, rope_cos,
          rope_sin, inverses, outT):
    D = w_in.shape[1]
    L = xT.shape[1]
    SEQ = L - META
    KT = D // P
    ZW = (L + 2) // 3 + ((L + 2) // 3) % 2
    LP = 3 * ZW
    NT = SEQ // P
    N_FFN = w_gate.shape[2]
    FT = N_FFN // P
    GROUPS = FT // 2
    LOOPS = (GROUPS - 1) // 2
    QW, KVW = w_q_b.shape[2], w_kv_b.shape[2]
    POOLW = POOL_GROUPS * P
    SCALE = float(HD) ** -0.5
    assert len(FILL_AT) == N_FILLS == 20 and SEQ + META == P * (KEY_TILES - 1) + META
    assert GROUPS % 2 == 1 and KT == 8 and NT == 8 and SEQ == 1024 and HEADS == 8

    Q0, KV0 = POOLW, POOLW + 3 * P
    R0 = KV0 + 2 * P
    IN_COLS = [(KV0, P), (KV0 + P, P), (R0, ROPE), (Q0, P), (Q0 + P, P), (Q0 + 2 * P, P)] + \
              [(g * P, P) for g in range(POOL_GROUPS)]
    in_cols = w_in[0].rearrange("(k p) c -> p k c", p=P)
    early = [(in_cols[:, :, c:c + w], KT, w) for c, w in IN_COLS]
    N_KV = len(early)
    early += [(w_kv_b[0, k * P:(k + 1) * P, :], 1, KVW) for k in range(2)]
    N_POOL = len(early)
    early += [(w_pool[0].rearrange("g c d -> c g d"), POOL_GROUPS, P)]
    N_Q = len(early)
    early += [(w_q_b[0, k * P:(k + 1) * P, :], 1, QW) for k in range(3)]
    N_OUT = len(early)
    out_cols = w_out[0].rearrange("(k p) c -> p k c", p=P)
    early += [(out_cols[:, :, d * P:(d + 1) * P], KT, P) for d in range(KT)]
    N_F = len(early)
    assert N_F % N_SPLIT == 0 and N_F % N_RAW == 0
    gate_t = w_gate[0].rearrange("(k p) (f c) -> f p k c", p=P, c=P)
    up_t = w_up[0].rearrange("(k p) (f c) -> f p k c", p=P, c=P)
    down_t = w_down[0].rearrange("(f p) c -> f p c", p=P)
    N_ALL = N_F + 3 * FT
    PER = 12
    N_L = N_F + 4

    with ExitStack() as ctx:
        def sem(name):
            return ctx.enter_context(nc.semaphore(name))

        cursor = [nc.sbuf_base + (-nc.sbuf_base) % 32]

        def size(shape):
            n = 4
            for s in shape[1:]:
                n *= s
            return n + (-n) % 32

        def take(name, shape, dt=F32):
            t = nc.alloc_sbuf_tensor_at(name, shape, dt, offset=cursor[0])
            cursor[0] += size(shape)
            assert cursor[0] <= nc.sbuf_top, (name, cursor[0] - nc.sbuf_top)
            return t

        w_raw = [take(f"w_raw{i}", [P, 1024]) for i in range(N_RAW)]
        w_hi = [take(f"w_hi{i}", [P, 1024], F32R) for i in range(N_SPLIT)]
        w_lo = [take(f"w_lo{i}", [P, 1024], F32R) for i in range(N_SPLIT)]
        ident = take("ident", [P, P])
        ones = take("ones", [P, P])
        causal = take("causal", [P, P])
        causal_t = take("causal_t", [P, AHEAD + P])
        cols = take("cols", [P, N_COLS])
        gains = take("gains", [P, 2 * ROPE])
        eps = take("eps", [P, 1])
        q_scale_col = take("q_scale_col", [P, 1])
        h_ms = take("h_ms", [P, NT + 1])
        h_root = take("h_root", [P, NT + 1])
        r_h = take("r_h", [P, NT + 1])
        r_h2 = take("r_h2", [P, NT + 1])
        r_hq = take("r_hq", [P, NT])
        r_hq2 = take("r_hq2", [P, NT])
        kv_sum = take("kv_sum", [P, NT + 1])
        q_sum = take("q_sum", [P, NT])
        kv_ms = take("kv_ms", [P, NT + 1])
        kv_root = take("kv_root", [P, NT + 1])
        kv_inv = take("kv_inv", [P, NT + 1])
        s_kv = take("s_kv", [P, NT + 1])
        q_ms = take("q_ms", [P, NT])
        q_root = take("q_root", [P, NT])
        q_inv = take("q_inv", [P, NT])
        s_q = take("s_q", [P, NT])
        max_parts = take("max_parts", [P, NT, 3])
        neg_max = take("neg_max", [P, NT])
        KN, KR = 0, (NT + 1) * HEADS
        QN = KR + NT + 1
        QR = QN + NT * HEADS
        N_SS = QR + NT * HEADS
        scratch_at = cursor[0]
        q_cos = take("q_cos", [P, NT, ROPE])
        q_sin = take("q_sin", [P, NT, ROPE])
        krn = take("krn", [P, NT + 1, ROPE])
        ssq = take("ssq", [P, N_SS])
        rs = take("rs", [P, N_SS])
        yp_at = cursor[0]
        p_hi = take("p_hi", [P, POOL_GROUPS, SEQ], F32R)
        r1_at = cursor[0]
        p_lo = take("p_lo", [P, POOL_GROUPS, SEQ], F32R)
        base = cursor[0]

        h_hi = [take(f"h_hi{k}", [P, LP], F32R) for k in range(KT)]
        h_lo = [take(f"h_lo{k}", [P, LP], F32R) for k in range(KT)]
        z_hi = [take(f"z_hi{k}", [P, LP], F32R) for k in range(5)]
        z_lo = [take(f"z_lo{k}", [P, LP], F32R) for k in range(5)]
        late = cursor[0]
        h_raw = [take(f"h_raw{i}", [P, LP]) for i in range(2)]
        square = take("square", [P, LP])
        h_sq = take("h_sq", [P, LP])
        z_sq = take("z_sq", [P, LP])
        r_bcast = take("r_bcast", [P, LP])
        zr = take("zr", [ROPE, LP])
        u, win = h_raw[0], [h_raw[1], square]

        cursor[0] = base
        kvn = take("kvn", [P, NT + 1, KVW])
        qn = take("qn", [P, NT, QW])
        attn_at = cursor[0]
        cos2 = take("cos2", [P, 2 * NT + 1, ROPE])
        sin2 = take("sin2", [P, 2 * NT + 1, ROPE])
        cursor[0] = late
        sq_tmp = [take(f"sq_tmp{i}", [P, QW]) for i in range(2)]
        kr_b = take("kr_b", [P, NT + 1, ROPE])
        k_cos = take("k_cos", [P, NT + 1, ROPE])
        k_sin = take("k_sin", [P, NT + 1, ROPE])
        kr_a = take("kr_a", [P, NT + 1, ROPE])
        assert cursor[0] <= late + 3 * size([P, LP])

        y_space = HEADS // 2 * size([P, SEQ])
        ya_at = nc.sbuf_top - y_space - 32
        ya_at -= ya_at % 32
        ya_hi_at = ya_at - y_space
        yp = nc.alloc_sbuf_tensor_at("yp", [P, POOL_GROUPS, SEQ], F32, offset=yp_at)
        yp_lo = nc.alloc_sbuf_tensor_at("yp_lo", [P, POOL_GROUPS, SEQ], F32R, offset=yp_at)
        yp_hi = nc.alloc_sbuf_tensor_at("yp_hi", [P, POOL_GROUPS, SEQ], F32R, offset=r1_at)
        ya = nc.alloc_sbuf_tensor_at("ya", [P, HEADS // 2, SEQ], F32, offset=ya_at)
        ya_lo = nc.alloc_sbuf_tensor_at("ya_lo", [P, HEADS // 2, SEQ], F32R, offset=ya_at)
        ya_hi = nc.alloc_sbuf_tensor_at("ya_hi", [P, HEADS // 2, SEQ], F32R, offset=ya_hi_at)

        qT_hi, qT_lo, kT_hi, kT_lo = [None, None], [None, None], [None, None], [None, None]
        cursor[0] = r1_at
        qs = take("qs", [P, NT, HD])
        ks = take("ks", [P, NT + 1, HD])
        rope_v = take("rope_v", [P, NT, ROPE])
        rope_a = take("rope_a", [P, NT, ROPE])
        rope_b = take("rope_b", [P, NT, ROPE])
        assert cursor[0] <= r1_at + 3 * size([P, SEQ])
        cursor[0] = r1_at + 3 * size([P, SEQ])
        y_raw = [take("y_raw0", [P, SEQ]), None]
        assert cursor[0] <= base
        cursor[0] = ya_hi_at
        qT_hi[0] = take("qT_hi0", [P, SEQ], F32R)
        kT_hi[0] = take("kT_hi0", [P, L], F32R)
        kT_lo[0] = take("kT_lo0", [P, L], F32R)
        vs = [take("vs0", [P, NT + 1, VDIM + 1]), None]
        neg_max8 = take("neg_max8", [NT, P], F32R)
        denom = take("denom", [SEQ // 16, 16])
        inv_denom = take("inv_denom", [SEQ // 16, 16])
        assert cursor[0] <= ya_at
        cursor[0] = attn_at
        qT_lo[0] = take("qT_lo0", [P, SEQ], F32R)
        qT_hi[1] = take("qT_hi1", [P, SEQ], F32R)
        qT_lo[1] = take("qT_lo1", [P, SEQ], F32R)
        kT_hi[1] = take("kT_hi1", [P, L], F32R)
        kT_lo[1] = take("kT_lo1", [P, L], F32R)
        probT = [take(f"probT{j}", [P, SEQ - P_FROM[j]]) for j in range(3)]
        vs[1] = take("vs1", [P, NT + 1, VDIM + 1])
        y_raw[1] = take("y_raw1", [P, SEQ])
        inv_l = take("inv_l", [P, SEQ])
        assert cursor[0] <= ya_hi_at

        cursor[0] = base
        resid = take("resid", [P, KT, SEQ])
        g_hi = take("g_hi", [P, KT, SEQ], F32R)
        g_lo = take("g_lo", [P, KT, SEQ], F32R)
        r_sq = take("r_sq", [P, SEQ])
        r_sq_tmp = nc.alloc_sbuf_tensor_at("r_sq_tmp", [P, SEQ], F32, offset=scratch_at)
        assert scratch_at + size([P, SEQ]) <= yp_at
        assert cursor[0] <= ya_hi_at

        cursor[0] = yp_at
        r2 = take("r2", [P, SEQ])
        r2_root = take("r2_root", [P, SEQ])
        gate_in = take("gate_in", [P, SEQ])
        gate = take("gate", [P, SEQ])
        up = take("up", [P, SEQ])
        act = take("act", [P, SEQ])
        assert cursor[0] <= base
        cursor[0] = ya_hi_at
        act_hi = [[take(f"act_hi{s}{j}", [P, SEQ], F32R) for j in range(2)] for s in range(2)]
        act_lo = [[take(f"act_lo{s}{j}", [P, SEQ], F32R) for j in range(2)] for s in range(2)]

        ps = ctx.enter_context(nc.psum_tensor("ps", [P, 8, 512], F32))
        psf = ps[:, :, :].rearrange("p b c -> p (b c)")

        columns_landed = sem("columns_landed")
        rope_landed = sem("rope_landed")
        raw_landed = [sem(f"raw_landed{i}") for i in range(N_RAW)]
        w_hi_ready = sem("w_hi_ready")
        w_lo_ready = sem("w_lo_ready")
        w_used = sem("w_used")
        h_landed = [sem(f"h_landed{i}") for i in range(2)]
        pad_ready = sem("pad_ready")
        h_hi_ready = sem("h_hi_ready")
        h_sq_ready = sem("h_sq_ready")
        h_lo_ready = sem("h_lo_ready")
        h_sq_added = sem("h_sq_added")
        const_ready = sem("const_ready")
        z_hi_ready = sem("z_hi_ready")
        z_act_done = sem("z_act_done")
        z_dve_done = sem("z_dve_done")
        z_sq_added = sem("z_sq_added")
        aux_done = sem("aux_done")
        aux_act = sem("aux_act")
        aux_dve = sem("aux_dve")
        dve_step = sem("dve_step")
        pool_step = sem("pool_step")
        h_ms_ready = sem("h_ms_ready")
        h_root_ready = sem("h_root_ready")
        r_h_ready = sem("r_h_ready")
        kv_ms_ready = sem("kv_ms_ready")
        kv_root_ready = sem("kv_root_ready")
        s_kv_ready = sem("s_kv_ready")
        q_ms_ready = sem("q_ms_ready")
        q_root_ready = sem("q_root_ready")
        s_q_ready = sem("s_q_ready")
        p_ready = sem("p_ready")
        p_hi_ready = sem("p_hi_ready")
        p_lo_ready = sem("p_lo_ready")
        proj_done = sem("proj_done")
        proj_act = sem("proj_act")
        kv_pad_ready = sem("kv_pad_ready")
        sq_ready = sem("sq_ready")
        ssq_added = sem("ssq_added")
        root_ready = sem("root_ready")
        rs_k_ready = sem("rs_k_ready")
        rs_ready = sem("rs_ready")
        q_sq_ready = sem("q_sq_ready")
        q_scale_ready = sem("q_scale_ready")
        tables_ready = sem("tables_ready")
        kr_ready = sem("kr_ready")
        head0_ready = sem("head0_ready")
        qs_ready = sem("qs_ready")
        ks_ready = sem("ks_ready")
        vs_ready = sem("vs_ready")
        ones_ready = sem("ones_ready")
        misc_filled = sem("misc_filled")
        prep_hi_ready = sem("prep_hi_ready")
        misc_free = sem("misc_free")
        nat_masked = sem("nat_masked")
        neg_max_ready = sem("neg_max_ready")
        m_landed = sem("m_landed")
        st_done = sem("st_done")
        st_masked = sem("st_masked")
        exp_done = sem("exp_done")
        pv_done = sem("pv_done")
        y_taken = sem("y_taken")
        l_landed = sem("l_landed")
        inv_denom_ready = sem("inv_denom_ready")
        inv_row_landed = sem("inv_row_landed")
        inv_l_landed = sem("inv_l_landed")
        ya_ready = sem("ya_ready")
        y_hi_ready = sem("y_hi_ready")
        y_lo_ready = sem("y_lo_ready")
        resid_landed = sem("resid_landed")
        h2_ready = sem("h2_ready")
        g_hi_ready = sem("g_hi_ready")
        g_sq_ready = sem("g_sq_ready")
        g_lo_ready = sem("g_lo_ready")
        g_sq_added = sem("g_sq_added")
        ms2_done = sem("ms2_done")
        r2_root_ready = sem("r2_root_ready")
        r2_ready = sem("r2_ready")
        gate_in_ready = sem("gate_in_ready")
        silu_ready = sem("silu_ready")
        up_ready = sem("up_ready")
        act_ready = sem("act_ready")
        act_hi_ready = sem("act_hi_ready")
        act_lo_ready = sem("act_lo_ready")
        down_done = sem("down_done")
        down_bank_free = sem("down_bank_free")
        out_landed = sem("out_landed")

        Z_OF_STEP = {0: 0, 1: 1, 3: 2, 4: 3, 5: 4}
        ACT_READS = [1, 2, 3, 4, 5, 6, 6, 6, 6, 6]
        DVE_READS = [1, 2, 2, 3, 4, 5, 6, 7, 8, 9]
        N_STEPS = len(IN_COLS)
        J_POOL, J_Q, N_JOBS = NT + 1, NT + 1 + POOL_GROUPS, 2 * NT + 1 + POOL_GROUPS

        JOB_ENDS = {J_POOL - 1: N_POOL, J_Q - 1: N_Q, N_JOBS - 1: N_OUT}

        def z_banks(step):
            return 3 * (step % 2)

        def job_bank(job):
            return 2 * ((job + 3) % 4)

        def wait_for_job(engine, j):
            if j in JOB_ENDS:
                engine.wait_ge(w_used, JOB_ENDS[j])
            else:
                engine.wait_ge(proj_done, j + 1 - sum(1 for e in JOB_ENDS if e < j))

        def count(head, per, c):
            i, n = head
            return n * per + c if i is None else i * (2 * per) + (n * per + c)

        def next_head(head):
            return head[0], head[1] + 1

        Y_ORDER = [0, 1, 2, 4, 5, 3, 6, 7]

        def is_first(head):
            return head[0] is None and head[1] == 0

        def fills_at(j, *places):
            return [(x, FILLS[x]) for x in range(N_FILLS) for place in places if FILL_AT[x] == (j, place)]

        FILLS_AHEAD = [(x, FILLS[x]) for x in range(N_FILLS) if FILL_AT[x][0] >= TAIL]
        BODY, END = range(TAIL), range(TAIL, KEY_TILES)

        def divide(engine, head):
            i, n = head
            e, pair = n % 2, (n // 2 if i is None else i + n // 2)
            rows_ = slice(VDIM * e, VDIM * (e + 1))
            engine.wait_ge(inv_l_landed, count(head, 16, 16))
            engine.tensor_tensor(ya[rows_, bass.ds(pair, 1), :].rearrange("p a c -> p (a c)"),
                                 y_raw[e][0:VDIM, :], inv_l[0:VDIM, :], ALU.mult).then_inc(ya_ready, 1)

        def filled_in(head, j):
            return next_head(next_head(head)) if j >= TAIL else next_head(head)

        def in_loop(i, per, c):
            return c if i is None else i * per + c

        def raw_count(n):
            return 16 * (n // N_RAW + 1)

        def prep_out(q, k, b, kind, tiles):
            if kind == "q":
                return q[b][0:HD, tiles[0] * P:(tiles[-1] + 1) * P], q_scale_col
            return k[b][0:HD, key0(tiles[0]):min(key0(tiles[-1] + 1), L)], cols[:, C_KN:C_KN + 1]

        def st_bank(head, j):
            return 2 * ((KEY_TILES * head[1] + j) % 2)

        block = ctx.enter_context(nc.Block())

        @block.sync
        def _(sp):
            def load_weights(n):
                src, k, w = early[n]
                if n >= N_RAW:
                    sp.wait_ge(w_lo_ready, n - N_RAW + 1)
                dst = w_raw[n % N_RAW][:, 0:k * w]
                if k > 1:
                    dst = dst.rearrange("p (k c) -> p k c", k=k)
                sp.dma_start(dst, src).then_inc(raw_landed[n % N_RAW], 16)

            def load_h(k):
                if k >= 2:
                    sp.wait_ge(h_sq_ready, k - 1)
                    sp.wait_ge(h_lo_ready, k - 1)
                sp.dma_start(h_raw[k % 2][:, 0:L], xT[k * P:(k + 1) * P, :])\
                  .then_inc(h_landed[k % 2], 16)

            sp.dma_start(cols[:, :], columns).then_inc(columns_landed, 16)
            load_weights(0)
            load_h(0)
            load_weights(1)
            sp.dma_start(gains[:, :], rows).then_inc(columns_landed, 16)
            for k in range(1, KT):
                load_h(k)
            for n in range(2, N_STEPS + 2):
                load_weights(n)
            sp.wait_ge(w_used, N_STEPS)
            sp.dma_start(cos2[:, :, :], rope_cos).then_inc(rope_landed, 16)
            sp.dma_start(sin2[:, :, :], rope_sin).then_inc(rope_landed, 16)
            for n in range(N_STEPS + 2, N_OUT + 2):
                load_weights(n)

            def send_max(head):
                sp.wait_ge(misc_free, count(head, N_FILLS, N_FILLS))
                sp.dma_start(qT_hi[head[1] % 2][HD:HD + 1, :].bitcast(F32), neg_max8[:, :].bitcast(F32)).then_inc(m_landed, 16)

            def send_sums(head):
                sp.wait_ge(y_taken, count(head, 2, 3))
                sp.dma_start(denom[:, :], y_raw[head[1] % 2][VDIM:VDIM + 1, :]).then_inc(l_landed, 16)

            def send_inverses(head):
                sp.wait_ge(inv_denom_ready, count(head, 1, 1))
                sp.dma_start(inverses, inv_denom[:, :]).then_inc(inv_row_landed, 16)
                sp.wait_ge(inv_row_landed, count(head, 16, 16))
                sp.wait_ge(ya_ready, count(head, 1, 1))
                sp.dma_start(inv_l[0:VDIM, :].rearrange("p (r c) -> p r c", r=SEQ // 16),
                             inverses[None, :, :].to_broadcast([VDIM, SEQ // 16, 16])).then_inc(inv_l_landed, 16)

            def send(head):
                send_sums(head)
                send_inverses(head)
                send_max(next_head(next_head(head)))

            send_max((None, 0))
            send_max((None, 1))
            send((None, 0))
            with sp.Fori(0, HEADS // 2 - 2) as i:
                send((i, 1))
                send((i, 2))
            send((None, HEADS - 3))
            sp.wait_ge(ks_ready, HEADS)
            sp.wait_ge(vs_ready, HEADS)
            for d in range(KT):
                sp.dma_start(resid[:, d, :], xT[d * P:(d + 1) * P, META:L]).then_inc(resid_landed, 16)
            for h in (HEADS - 2, HEADS - 1):
                send_sums((None, h))
                send_inverses((None, h))
            for n in range(N_OUT + 2, N_F):
                load_weights(n)

            def load_ffn(src, c, i):
                sp.wait_ge(w_lo_ready, in_loop(i, PER, c - N_RAW + 1))
                dst = w_raw[c % N_RAW][:, :]
                if len(src.shape) == 3:
                    dst = dst.rearrange("p (k c) -> p k c", k=KT)
                sp.dma_start(dst, src).then_inc(raw_landed[c % N_RAW], 16)

            def load_gate_up(f, c, i):
                for j in range(2):
                    load_ffn(gate_t[f + j], c + 2 * j, i)
                    load_ffn(up_t[f + j], c + 2 * j + 1, i)

            def load_down(f, c, i):
                for j in range(2):
                    load_ffn(down_t[f + j], c + j, i)

            load_gate_up(0, N_F, None)
            with sp.Fori(0, LOOPS) as i:
                load_gate_up(i * 4 + 2, N_L, i)
                load_down(i * 4, N_L + 4, i)
                load_gate_up(i * 4 + 4, N_L + 6, i)
                load_down(i * 4 + 2, N_L + 10, i)
            load_down(FT - 2, N_ALL - 2, None)
            for d in range(KT):
                sp.wait_ge(down_bank_free, 4 + 16 * (GROUPS - 1) + 2 * (d + 1))
                sp.dma_start(outT[d * P:(d + 1) * P, :], resid[:, d, :]).then_inc(out_landed, 16)
            sp.wait_ge(out_landed, 16 * KT)

        @block.gpsimd
        def _(pool):
            steps = [0]

            def link(ins):
                steps[0] += 1
                ins.then_inc(pool_step, 1)
                pool.wait_ge(pool_step, steps[0])

            pool.memset(ident[:, :], 0.0).then_inc(pool_step, 1)
            pool.memset(causal[:, :], 0.0).then_inc(pool_step, 1)
            pool.memset(causal_t[:, :], 0.0).then_inc(pool_step, 1)
            pool.memset(ones[:, :], 1.0).then_inc(const_ready, 1)
            pool.memset(eps[:, :], EPS).then_inc(const_ready, 1)
            steps[0] = 3
            pool.wait_ge(pool_step, 3)
            pool.affine_select(out=ident[:, :], in_=ident[:, :], compare_op=ALU.not_equal, fill=1.0,
                               base=0, pattern=[[-1, P]], channel_multiplier=1).then_inc(const_ready, 1)
            pool.affine_select(out=causal[:, :], in_=causal[:, :], compare_op=ALU.is_ge, fill=MASKED,
                               base=0, pattern=[[-1, P]], channel_multiplier=1).then_inc(const_ready, 1)
            pool.affine_select(out=causal_t[:, :], in_=causal_t[:, :], compare_op=ALU.is_ge, fill=MASKED,
                               base=-AHEAD, pattern=[[1, AHEAD + P]], channel_multiplier=-1)\
                .then_inc(const_ready, 1)

            pool.wait_ge(columns_landed, 32)
            pool.wait_ge(rope_landed, 32)
            pool.wait_ge(p_lo_ready, POOL_GROUPS)
            H = ROPE // 2

            def table(out, trig, n, g, swapped):
                for a in range(2):
                    b = 1 - a if swapped else a
                    last = pool.tensor_tensor(
                        out[:, :, a * H:(a + 1) * H],
                        trig[:, 0 if n == NT else NT:n if n == NT else NT + n, a * H:(a + 1) * H],
                        gains[:, None, g + b * H:g + (b + 1) * H].to_broadcast([P, n, H]), ALU.mult)
                return last

            table(q_cos, cos2, NT, 0, False)
            table(q_sin, sin2, NT, 0, True).then_inc(tables_ready, 1)
            table(k_cos, cos2, NT + 1, ROPE, False)
            link(table(k_sin, sin2, NT + 1, ROPE, True))

            def squares(job, src, out):
                pool.wait_ge(proj_act, job + 1)
                pool.tensor_tensor(out, src, src, ALU.mult).then_inc(sq_ready, 1)

            for t in range(NT + 1):
                if t >= 2:
                    pool.wait_ge(ssq_added, t - 1)
                squares(t, kvn[:, t, :].rearrange("p (h c) -> p h c", h=HEADS)[:, :, 0:NOPE],
                        sq_tmp[t % 2][:, 0:HEADS * NOPE].rearrange("p (h c) -> p h c", h=HEADS))
            def rope(v, cos, sin, a, b, n):
                pool.tensor_tensor(a, v, cos[:, :, :], ALU.mult)
                pool.tensor_tensor(b[:, :, 0:H], v[:, :, H:ROPE], sin[:, :, 0:H], ALU.mult)
                return pool.tensor_tensor(b[:, :, H:ROPE], v[:, :, 0:H], sin[:, :, H:ROPE], ALU.mult)

            pool.wait_ge(rs_k_ready, 1)
            pool.wait_ge(w_used, N_POOL + 1)
            link(pool.tensor_tensor(krn[:, :, :], krn[:, :, :],
                                    rs[:, KR:KR + NT + 1, None].to_broadcast([P, NT + 1, ROPE]), ALU.mult))
            link(rope(krn[:, :, :], k_cos, k_sin, kr_a[:, :, :], kr_b[:, :, :], NT + 1))
            pool.tensor_tensor(ks[:, :, NOPE:HD], kr_a[:, :, :], kr_b[:, :, :], ALU.add).then_inc(kr_ready, 1)
            before = steps[0]

            def stat(at, n, h):
                return rs[:, at:at + n * HEADS].rearrange("p (t h) -> p t h", h=HEADS)[:, :, bass.ds(h, 1)]

            def queries(h):
                pool.tensor_tensor(rope_v[:, :, :], qn[:, :, bass.ds(h * HD + NOPE, ROPE)],
                                   stat(QR, NT, h).to_broadcast([P, NT, ROPE]), ALU.mult)\
                    .then_inc(pool_step, 1)
                pool.tensor_tensor(qs[:, :, 0:NOPE], qn[:, :, bass.ds(h * HD, NOPE)],
                                   stat(QN, NT, h).to_broadcast([P, NT, NOPE]), ALU.mult)
                pool.wait_ge(pool_step, h * 2 + (before - 1))
                rope(rope_v[:, :, :], q_cos, q_sin, rope_a[:, :, :], rope_b[:, :, :], NT)\
                    .then_inc(pool_step, 1)
                pool.wait_ge(pool_step, h * 2 + before)
                pool.tensor_tensor(qs[:, :, NOPE:HD], rope_a[:, :, :], rope_b[:, :, :], ALU.add)\
                    .then_inc(qs_ready, 1)

            def keys(h):
                pool.tensor_tensor(ks[:, :, 0:NOPE], kvn[:, :, bass.ds(h * (NOPE + VDIM), NOPE)],
                                   stat(KN, NT + 1, h).to_broadcast([P, NT + 1, NOPE]), ALU.mult)\
                    .then_inc(ks_ready, 1)

            def prepare(head):
                i, n = head
                h = n if i is None else i * 2 + n
                pool.wait_ge(misc_filled, count(head, N_FILLS, N_PREP - N_FILLS))
                queries(h)
                keys(h)

            def divide_after(head, ahead):
                pool.wait_ge(ks_ready, count(head, 1, ahead + 1))
                divide(pool, head)
                pool.wait_ge(ya_ready, count(head, 1, 2))

            keys(0)
            pool.wait_ge(rs_ready, 1)
            pool.sem_inc(ya_ready, 1)
            prepare((None, 1))
            prepare((None, 2))
            prepare((None, 3))
            with pool.Fori(0, HEADS // 2 - 2) as i:
                for n in (0, 1):
                    divide_after((i, n), 3)
                    prepare((i, n + 4))
            for h in range(HEADS - 4, HEADS - 1):
                divide_after((None, h), HEADS - 1 - h)

        @block.scalar
        def _(act_e):
            a = act_e

            def split_hi(c, i=None):
                w = 1024 if c >= N_F else early[c][1] * early[c][2]
                a.wait_ge(raw_landed[c % N_RAW], in_loop(i, 16 * PER // N_RAW, raw_count(c)))
                if c >= N_SPLIT:
                    a.wait_ge(w_used, in_loop(i, PER, c - N_SPLIT + 1))
                a.activation(w_hi[c % N_SPLIT][:, 0:w], w_raw[c % N_RAW][:, 0:w], ACT.Copy)\
                    .then_inc(w_hi_ready, 1)

            a.wait_ge(columns_landed, 16)
            a.wait_ge(pad_ready, 2)
            split_hi(0)
            for k in range(KT):
                a.wait_ge(h_landed[k % 2], 16 * (k // 2 + 1))
                a.activation(h_hi[k][:, :], h_raw[k % 2][:, :], ACT.Identity,
                             scale=cols[:, C_ATTN + k:C_ATTN + k + 1]).then_inc(h_hi_ready, 1)
                if k == 0:
                    split_hi(1)
                if k >= 2:
                    a.wait_ge(h_sq_added, k - 1)
                a.activation((square if k else h_sq)[:, :], h_raw[k % 2][:, :], ACT.Square)\
                    .then_inc(h_sq_ready, 1)

            def z_view(step, rows=P):
                b = z_banks(step)
                return ps[0:rows, b:b + 3, 0:ZW]

            def tiles3(t, rows=P):
                return t[0:rows, :].rearrange("p (b c) -> p b c", b=3)

            for s in range(N_STEPS):
                split_hi(s + 2)
                if s in Z_OF_STEP:
                    z = Z_OF_STEP[s]
                    a.wait_ge(w_used, s + 1)
                    a.activation(tiles3(z_hi[z]), z_view(s), ACT.Identity,
                                 scale=cols[:, C_Z + z:C_Z + z + 1]).then_inc(z_hi_ready, 1)
                    if s == 1:
                        a.wait_ge(h_sq_added, KT - 1)
                    if s == 3:
                        a.wait_ge(aux_done, 2)
                    if s == 4:
                        a.wait_ge(z_sq_added, 1)
                    if s == 5:
                        a.wait_ge(z_sq_added, 2)
                    dst = {0: z_sq, 1: square, 3: h_sq, 4: square, 5: square}[s]
                    a.activation(tiles3(dst), z_view(s), ACT.Square).then_inc(z_act_done, 1)
                if s == 2:
                    a.wait_ge(w_used, 3)
                    a.activation(tiles3(zr, ROPE), z_view(2, ROPE), ACT.Copy).then_inc(z_act_done, 1)
                if s == 3:
                    a.wait_ge(h_ms_ready, 1)
                    a.wait_ge(const_ready, 5)
                    a.activation(h_root[:, :], h_ms[:, :], ACT.Sqrt, bias=eps[:, :], scale=1.0 / D)\
                        .then_inc(h_root_ready, 1)
                if s == 4:
                    a.wait_ge(aux_done, 3)
                    a.activation(r_bcast[:, 0:512], ps[:, 6, :], ACT.Copy).then_inc(aux_act, 1)
                    a.activation(r_bcast[:, 512:768], ps[:, 7, 0:256], ACT.Copy).then_inc(aux_act, 1)
                if s == 5:
                    a.wait_ge(aux_done, 4)
                    a.activation(r_bcast[:, 768:L], ps[:, 6, 0:L - 768], ACT.Copy).then_inc(aux_act, 1)
                if s == 6:
                    a.wait_ge(kv_ms_ready, 1)
                    a.activation(kv_root[:, :], kv_ms[:, :], ACT.Sqrt, bias=eps[:, :])\
                        .then_inc(kv_root_ready, 1)
                if s == 8:
                    a.wait_ge(q_ms_ready, 1)
                    a.activation(q_root[:, :], q_ms[:, :], ACT.Sqrt, bias=eps[:, :])\
                        .then_inc(q_root_ready, 1)
                if s >= 6:
                    g = s - 6
                    a.wait_ge(p_ready, g + 1)
                    a.activation(p_hi[:, g, :], win[g % 2][:, META:L], ACT.Copy).then_inc(p_hi_ready, 1)

            def roots(lo, hi, n):
                a.activation(ssq[:, lo:hi], ssq[:, lo:hi], ACT.Sqrt, bias=eps[:, :], scale=1.0 / n)\
                    .then_inc(root_ready, 1)

            for j in range(N_JOBS):
                b = job_bank(j)
                if j == 0:
                    split_hi(N_POOL)
                    a.wait_ge(s_kv_ready, 1)
                if j == J_POOL:
                    split_hi(N_Q)
                    split_hi(N_Q + 1)
                if j == J_Q:
                    split_hi(N_Q + 2)
                    a.wait_ge(ssq_added, NT + 2)
                    roots(KN, KR, NOPE)
                    roots(KR, QN, ROPE)
                    a.wait_ge(s_q_ready, 1)
                wait_for_job(a, j)
                if j < J_POOL:
                    n = min(P, L - key0(j))
                    if n < P:
                        a.wait_ge(kv_pad_ready, 1)
                    a.activation(kvn[0:n, j, :], psf[0:n, b * 512:b * 512 + KVW], ACT.Copy,
                                 scale=s_kv[0:n, j:j + 1]).then_inc(proj_act, 1)
                elif j < J_Q:
                    g = j - J_POOL
                    a.activation(yp[:, g, :], psf[:, b * 512:b * 512 + SEQ], ACT.Copy,
                                 scale=cols[:, C_POOL + g:C_POOL + g + 1]).then_inc(proj_act, 1)
                else:
                    t = j - J_Q
                    a.wait_ge(ssq_added, NT + 2 + max(t - 1, 0))
                    a.activation(sq_tmp[t % 2][:, :].rearrange("p (b c) -> p b c", b=2),
                                 ps[:, b:b + 2, 0:QW // 2], ACT.Square, scale=s_q[:, t:t + 1])\
                        .then_inc(q_sq_ready, 1)
                    a.activation(qn[:, t, :].rearrange("p (b c) -> p b c", b=2),
                                 ps[:, b:b + 2, 0:QW // 2], ACT.Copy,
                                 scale=s_q[:, t:t + 1]).then_inc(proj_act, 1)
            a.wait_ge(ssq_added, 2 * NT + 2)
            roots(QN, QR, NOPE)
            roots(QR, N_SS, ROPE)
            split_hi(N_OUT)
            split_hi(N_OUT + 1)

            def take_values(h, b):
                a.activation(vs[b][:, :, 0:VDIM], kvn[:, :, bass.ds(h * (NOPE + VDIM) + NOPE, VDIM)],
                             ACT.Copy).then_inc(vs_ready, 1)

            def prep_hi(b, kind, tiles):
                out, gain = prep_out(qT_hi, kT_hi, b, kind, tiles)
                return out, gain[0:HD, :]

            def exponentials(head, j):
                n = SEQ - P_FROM[j]
                rows_ = min(P, L - key0(j))
                bank = st_bank(head, j)
                a.wait_ge(st_masked, count(head, KEY_TILES, j + 1))
                if not is_first(head) or j >= 3:
                    a.wait_ge(pv_done, count(head, KEY_TILES, j - 2))
                out = probT[j % 3][0:rows_, 0:n]
                skip = P_FROM[j] - S_FROM[j]
                if n > 512:
                    a.activation(out.rearrange("p (b c) -> p b c", b=2), ps[0:rows_, bank:bank + 2, 0:n // 2],
                                 ACT.Exp).then_inc(exp_done, 1)
                else:
                    a.activation(out, ps[0:rows_, bank, skip:skip + n], ACT.Exp).then_inc(exp_done, 1)

            def high_parts(head, fills):
                for x, fill in fills:
                    if fill[0] in "qk":
                        a.wait_ge(misc_filled, count(head, N_FILLS, x + 1))
                        out, gain = prep_hi(head[1] % 2, *fill)
                        a.activation(out, ps[0:HD, 6 + x % 2, 0:out.shape[1]], ACT.Copy, scale=gain)\
                            .then_inc(prep_hi_ready, 1)

            def take_y(head, half):
                a.wait_ge(pv_done, count(head, KEY_TILES, 5 if half == 0 else KEY_TILES))
                if half == 0:
                    a.wait_ge(ya_ready, count(head, 1, 0))
                a.activation(y_raw[head[1] % 2][0:VDIM + 1, 512 * half:512 * (half + 1)], ps[0:VDIM + 1, 4 + half, :],
                             ACT.Copy).then_inc(y_taken, 1)

            def y_high(k):
                src, dst = (yp, yp_hi) if k < POOL_GROUPS else (ya, ya_hi)
                a.activation(dst[:, k % POOL_GROUPS, :], src[:, k % POOL_GROUPS, :], ACT.Copy)\
                    .then_inc(y_hi_ready, 1)

            def attend(head, steps, last=False, fills=True):
                for j in steps:
                    if fills:
                        high_parts(filled_in(head, j), fills_at(j, 0))
                    if j < KEY_TILES - 2:
                        exponentials(head, j + 2)
                    elif not last:
                        exponentials(next_head(head), j + 2 - KEY_TILES)
                    if fills:
                        high_parts(filled_in(head, j), fills_at(j, 1, 2, 3))
                    if j == 3 and not last:
                        n = next_head(head)
                        take_values(n[1] if n[0] is None else n[0] * 2 + n[1], n[1] % 2)
                    if j == 4:
                        take_y(head, 0)
                    if last and j < 5:
                        y_high(Y_ORDER[j])
                    if j == KEY_TILES - 1:
                        take_y(head, 1)
                        if last:
                            a.wait_ge(ya_ready, 1 + HEADS - 1)
                            y_high(Y_ORDER[5])
                            y_high(Y_ORDER[6])

            a.sem_inc(y_taken, 1)
            a.wait_ge(q_scale_ready, 1)
            high_parts((None, 0), list(enumerate(FILLS)))
            take_values(0, 0)
            exponentials((None, 0), 0)
            exponentials((None, 0), 1)
            high_parts((None, 1), FILLS_AHEAD)
            attend((None, 0), BODY)
            with a.Fori(0, HEADS // 2 - 1) as i:
                for n in (1, 2):
                    attend((i, n - 1), END)
                    attend((i, n), BODY)
            attend((None, HEADS - 2), END, fills=False)
            attend((None, HEADS - 1), BODY, last=True, fills=False)
            attend((None, HEADS - 1), END, last=True, fills=False)
            a.wait_ge(ya_ready, 1 + HEADS)
            y_high(Y_ORDER[7])

            for d in range(KT):
                split_hi(N_OUT + d + 2)
                a.wait_ge(h2_ready, d + 1)
                a.activation(g_hi[:, d, :], resid[:, d, :], ACT.Copy,
                             scale=cols[:, C_FFN + d:C_FFN + d + 1]).then_inc(g_hi_ready, 1)
                if d >= 2:
                    a.wait_ge(g_sq_added, d - 1)
                a.activation((r_sq_tmp if d else r_sq)[:, :], resid[:, d, :], ACT.Square)\
                    .then_inc(g_sq_ready, 1)

            def gate_up(g, c, i, s):
                for j in range(2):
                    t = in_loop(i, 4, 2 * g + j)
                    split_hi(c + 2 * j + 2, i)
                    if i is None and g == 0 and j == 0:
                        a.wait_ge(ms2_done, 1)
                        a.activation(r2_root[:, :], psf[:, 4 * 512:4 * 512 + SEQ], ACT.Sqrt,
                                     bias=eps[:, :], scale=1.0 / D).then_inc(r2_root_ready, 1)
                    a.wait_ge(gate_in_ready, t + 1)
                    if not (i is None and g == 0 and j == 0):
                        a.wait_ge(act_ready, t)
                    a.activation(gate[:, :], gate_in[:, :], ACT.Silu).then_inc(silu_ready, 1)
                    split_hi(c + 2 * j + 3, i)
                    a.wait_ge(act_ready, t + 1)
                    a.activation(act_hi[s][j][:, :], act[:, :], ACT.Copy).then_inc(act_hi_ready, 1)

            def down(c, i):
                for j in range(2):
                    if c + j + 2 < N_ALL:
                        split_hi(c + j + 2, i)

            gate_up(0, N_F, None, 0)
            with a.Fori(0, LOOPS) as i:
                gate_up(1, N_L, i, 1)
                down(N_L + 4, i)
                gate_up(2, N_L + 6, i, 0)
                down(N_L + 10, i)

        @block.vector
        def _(v):
            steps = [0]

            def link(ins):
                steps[0] += 1
                ins.then_inc(dve_step, 1)
                v.wait_ge(dve_step, steps[0])

            def split_lo(c, i=None):
                w = 1024 if c >= N_F else early[c][1] * early[c][2]
                v.wait_ge(w_hi_ready, in_loop(i, PER, c + 1))
                v.tensor_tensor(w_lo[c % N_SPLIT][:, 0:w], w_raw[c % N_RAW][:, 0:w],
                                w_hi[c % N_SPLIT][:, 0:w].bitcast(F32), ALU.subtract)\
                    .then_inc(w_lo_ready, 1)

            for t in (*h_raw, r_bcast):
                v.memset(t[:, L:LP], 0.0).then_inc(pad_ready, 1)
            for t in (h_ms[:, NT:], kv_sum[:, NT:], krn[:, NT, :]):
                v.memset(t, 1.0).then_inc(pad_ready, 1)
            v.wait_ge(columns_landed, 16)
            split_lo(0)
            for k in range(KT):
                v.wait_ge(h_hi_ready, k + 1)
                v.scalar_tensor_tensor(out=h_lo[k][:, :], in0=h_raw[k % 2][:, :],
                                       scalar=cols[:, C_ATTN + k:C_ATTN + k + 1],
                                       in1=h_hi[k][:, :].bitcast(F32), op0=ALU.mult, op1=ALU.subtract)\
                    .then_inc(h_lo_ready, 1)
                if k == 0:
                    split_lo(1)
                else:
                    v.wait_ge(h_sq_ready, k + 1)
                    if k >= 2:
                        v.wait_ge(h_sq_added, k - 1)
                    v.tensor_tensor(h_sq[:, :], h_sq[:, :], square[:, :], ALU.add).then_inc(h_sq_added, 1)

            def z_view(step):
                b = z_banks(step)
                return ps[:, b:b + 3, 0:ZW]

            def tiles3(t):
                return t[:, :].rearrange("p (b c) -> p b c", b=3)

            def column_sums(out, col, n):
                return v.tensor_reduce(out, psf[:, col:col + n * P].rearrange("p (t c) -> p t c", c=P),
                                       AX.X, ALU.add)

            def last_sum(out, col):
                return v.tensor_reduce(out[0:META, NT:NT + 1], psf[0:META, col:col + P], AX.X, ALU.add)

            for s in range(N_STEPS):
                split_lo(s + 2)
                if s in Z_OF_STEP:
                    z = Z_OF_STEP[s]
                    v.wait_ge(z_hi_ready, z + 1)
                    v.wait_ge(z_act_done, ACT_READS[s])
                    v.scalar_tensor_tensor(out=tiles3(z_lo[z]), in0=z_view(s),
                                           scalar=cols[:, C_Z + z:C_Z + z + 1],
                                           in1=tiles3(z_hi[z]).bitcast(F32), op0=ALU.mult,
                                           op1=ALU.subtract).then_inc(z_dve_done, 1)
                    if s in (1, 4, 5):
                        acc = z_sq if s == 1 else h_sq
                        if s == 5:
                            v.wait_ge(z_sq_added, 2)
                        v.tensor_tensor(acc[:, :], acc[:, :], square[:, :], ALU.add)\
                            .then_inc(z_sq_added, 1)
                if s == 2:
                    v.wait_ge(aux_done, 1)
                    column_sums(h_ms[:, 0:NT], 6 * 512, NT).then_inc(aux_dve, 1)
                if s == 3:
                    v.wait_ge(aux_done, 2)
                    v.wait_ge(pad_ready, 6)
                    last_sum(h_ms, 6 * 512).then_inc(h_ms_ready, 1)
                    v.tensor_reduce(kv_sum[:, 0:4], ps[:, 7, :].rearrange("p (t c) -> p t c", c=P),
                                    AX.X, ALU.add)
                    v.wait_ge(h_root_ready, 1)
                    v.reciprocal(r_h[:, :], h_root[:, :]).then_inc(r_h_ready, 1)
                    v.wait_ge(r_h_ready, 1)
                    v.tensor_tensor(krn[:, 0:NT, :],
                                    ps[:, 6, P:P + NT * ROPE].rearrange("p (t c) -> p t c", c=ROPE),
                                    r_h[:, 0:NT, None].to_broadcast([P, NT, ROPE]), ALU.mult)
                    v.tensor_tensor(krn[0:META, NT, :], ps[0:META, 6, P + NT * ROPE:P + (NT + 1) * ROPE],
                                    r_h[0:META, NT:NT + 1].to_broadcast([META, ROPE]), ALU.mult)\
                        .then_inc(aux_dve, 1)
                if s == 5:
                    v.wait_ge(aux_done, 4)
                    v.wait_ge(aux_act, 3)
                    last_sum(kv_sum, 6 * 512 + 3 * P)
                    link(column_sums(kv_sum[:, 4:NT], 7 * 512, 4))
                    aux_read = v.tensor_tensor(r_h2[:, :], r_h[:, :], r_h[:, :], ALU.mult)
                    aux_read.then_inc(aux_dve, 1)
                    v.wait_ge(aux_dve, 3)
                    v.scalar_tensor_tensor(out=kv_ms[:, :], in0=kv_sum[:, :], scalar=1.0 / (2 * P),
                                           in1=r_h2[:, :], op0=ALU.mult, op1=ALU.mult)\
                        .then_inc(kv_ms_ready, 1)
                if s >= 6:
                    g = s - 6
                    v.wait_ge(w_used, s + 1)
                    if g == 0:
                        v.wait_ge(aux_act, 3)
                        v.wait_ge(pad_ready, 3)
                    else:
                        v.wait_ge(p_hi_ready, g)
                    ub = u[:, :].rearrange("p (b c) -> p b c", b=3)
                    rb = r_bcast[:, :].rearrange("p (b c) -> p b c", b=3)
                    v.tensor_tensor(ub, z_view(s), rb, ALU.mult).then_inc(z_dve_done, 1)
                    v.wait_ge(z_dve_done, DVE_READS[s])
                    src, start = u, 0
                    for j in range(g + 1):
                        shift = 2 ** j
                        dst = win[(1 + g + g - j) % 2]
                        start += shift
                        link(v.tensor_tensor(dst[:, start:L], src[:, start:L],
                                             src[:, start - shift:L - shift], ALU.add))
                        src = dst
                    v.scalar_tensor_tensor(out=win[g % 2][:, META:L], in0=src[:, META:L],
                                           scalar=1.0 / 2 ** (g + 1), in1=u[:, META:L],
                                           op0=ALU.mult, op1=ALU.subtract).then_inc(p_ready, 1)
                    v.wait_ge(p_hi_ready, g + 1)
                    v.tensor_tensor(p_lo[:, g, :], win[g % 2][:, META:L],
                                    p_hi[:, g, :].bitcast(F32), ALU.subtract).then_inc(p_lo_ready, 1)
                if s == 6:
                    v.wait_ge(kv_root_ready, 1)
                    link(v.reciprocal(kv_inv[:, :], kv_root[:, :]))
                    v.tensor_tensor(s_kv[:, :], kv_inv[:, :], r_h[:, :], ALU.mult).then_inc(s_kv_ready, 1)
                    v.wait_ge(aux_done, 5)
                    column_sums(q_sum[:, :], 6 * 512, NT).then_inc(aux_dve, 1)
                if s == 7:
                    v.wait_ge(aux_done, 6)
                    link(v.tensor_copy(r_hq[:, :], psf[:, 6 * 512:6 * 512 + NT * 32]
                                       .rearrange("p (t c) -> p t c", c=32)[:, :, 0:1]
                                       .rearrange("p t c -> p (t c)")))
                    link(v.tensor_tensor(r_hq2[:, :], r_hq[:, :], r_hq[:, :], ALU.mult))
                    v.wait_ge(aux_dve, 4)
                    v.scalar_tensor_tensor(out=q_ms[:, :], in0=q_sum[:, :], scalar=1.0 / (3 * P),
                                           in1=r_hq2[:, :], op0=ALU.mult, op1=ALU.mult)\
                        .then_inc(q_ms_ready, 1)
                if s == 8:
                    v.wait_ge(q_root_ready, 1)
                    link(v.reciprocal(q_inv[:, :], q_root[:, :]))
                    v.tensor_tensor(s_q[:, :], q_inv[:, :], r_hq[:, :], ALU.mult).then_inc(s_q_ready, 1)
                    v.tensor_scalar(q_scale_col[:, :], cols[:, C_QN:C_QN + 1], SCALE, None, ALU.mult)\
                        .then_inc(q_scale_ready, 1)

            v.wait_ge(w_used, N_STEPS)
            v.memset(kvn[:, NT, :], 0.0).then_inc(kv_pad_ready, 1)

            for j in range(N_JOBS):
                if j == 0:
                    split_lo(N_POOL)
                if j == J_POOL:
                    split_lo(N_Q)
                    split_lo(N_Q + 1)
                if j == J_Q:
                    split_lo(N_Q + 2)
                    v.wait_ge(aux_dve, 3)
                    link(v.tensor_tensor(kr_b[:, :, :], krn[:, :, :], krn[:, :, :], ALU.mult))
                    v.tensor_reduce(ssq[:, KR:QN], kr_b[:, :, :], AX.X, ALU.add).then_inc(ssq_added, 1)
                    v.wait_ge(root_ready, 2)
                    v.reciprocal(rs[:, 0:QN], ssq[:, 0:QN]).then_inc(rs_k_ready, 1)
                if j < J_POOL:
                    v.wait_ge(sq_ready, j + 1)
                    v.tensor_reduce(ssq[:, KN + j * HEADS:KN + (j + 1) * HEADS],
                                    sq_tmp[j % 2][:, 0:HEADS * NOPE].rearrange("p (h c) -> p h c", h=HEADS),
                                    AX.X, ALU.add).then_inc(ssq_added, 1)
                elif j >= J_Q:
                    t = j - J_Q
                    v.wait_ge(q_sq_ready, t + 1)
                    squares = sq_tmp[t % 2][:, :].rearrange("p (h c) -> p h c", h=HEADS)
                    v.tensor_reduce(ssq[:, QN + t * HEADS:QN + (t + 1) * HEADS], squares[:, :, 0:NOPE],
                                    AX.X, ALU.add)
                    v.tensor_reduce(ssq[:, QR + t * HEADS:QR + (t + 1) * HEADS], squares[:, :, NOPE:HD],
                                    AX.X, ALU.add).then_inc(ssq_added, 1)
            v.wait_ge(root_ready, 4)
            v.reciprocal(rs[:, QN:N_SS], ssq[:, QN:N_SS]).then_inc(rs_ready, 1)
            v.wait_ge(rs_ready, 1)

            def stat(at):
                return rs[:, at:at + NT * HEADS].rearrange("p (t h) -> p t h", h=HEADS)[:, :, 0:1]

            H = ROPE // 2
            v.wait_ge(tables_ready, 1)
            v.wait_ge(w_used, N_POOL + 1)
            link(v.tensor_tensor(rope_v[:, :, :], qn[:, :, NOPE:HD], stat(QR).to_broadcast([P, NT, ROPE]),
                                 ALU.mult))
            v.tensor_tensor(rope_a[:, :, :], rope_v[:, :, :], q_cos[:, :, :], ALU.mult)
            v.tensor_tensor(rope_b[:, :, 0:H], rope_v[:, :, H:ROPE], q_sin[:, :, 0:H], ALU.mult)
            link(v.tensor_tensor(rope_b[:, :, H:ROPE], rope_v[:, :, 0:H], q_sin[:, :, H:ROPE], ALU.mult))
            v.tensor_tensor(qs[:, :, NOPE:HD], rope_a[:, :, :], rope_b[:, :, :], ALU.add)
            v.tensor_tensor(qs[:, :, 0:NOPE], qn[:, :, 0:NOPE], stat(QN).to_broadcast([P, NT, NOPE]), ALU.mult)\
                .then_inc(head0_ready, 1)

            def take_fills(head, fills):
                b = head[1] % 2
                for x, fill in fills:
                    bank = 6 + x % 2
                    if fill[0] in "qk":
                        hi, gain = prep_out(qT_hi, kT_hi, b, *fill)
                        lo, _ = prep_out(qT_lo, kT_lo, b, *fill)
                        v.wait_ge(prep_hi_ready, count(head, N_PREP, x + 1))
                        v.scalar_tensor_tensor(out=lo, in0=ps[0:HD, bank, 0:lo.shape[1]], scalar=gain[0:HD, :],
                                               in1=hi.bitcast(F32), op0=ALU.mult, op1=ALU.subtract)\
                            .then_inc(misc_free, 1)
                    elif fill[0] == "n":
                        _, i, m, parts, width = fill
                        v.wait_ge(misc_filled, count(head, N_FILLS, x + 1))
                        if m == parts - 1:
                            diagonal = ps[:, bank, width - P:width]
                            v.tensor_tensor(diagonal, diagonal, causal[:, :], ALU.add).then_inc(nat_masked, 1)
                            v.wait_ge(nat_masked, count(head, NT, i + 1))
                        v.tensor_reduce(max_parts[:, i, m:m + 1], ps[:, bank, 0:width], AX.X, ALU.max)\
                            .then_inc(misc_free, 1)
                        if x == N_FILLS - 2:
                            v.wait_ge(misc_free, count(head, N_FILLS, x + 1))
                            v.tensor_reduce(neg_max[:, :], max_parts[:, :, :], AX.X, ALU.max, negate=True)\
                                .then_inc(neg_max_ready, 1)
                    else:
                        v.wait_ge(misc_filled, count(head, N_FILLS, x + 1))
                        if not is_first(head):
                            v.wait_ge(m_landed, count(head, 16, 0))
                        v.tensor_copy(neg_max8[:, :], ps[0:NT, bank, 0:P]).then_inc(misc_free, 1)

            def invert_sums(head):
                v.wait_ge(l_landed, count(head, 16, 16))
                v.reciprocal(inv_denom[:, :], denom[:, :]).then_inc(inv_denom_ready, 1)

            def y_low(k):
                src, hi, lo = (yp, yp_hi, yp_lo) if k < POOL_GROUPS else (ya, ya_hi, ya_lo)
                at = k % POOL_GROUPS
                v.wait_ge(y_hi_ready, Y_ORDER.index(k) + 1)
                v.tensor_tensor(lo[:, at, :], src[:, at, :], hi[:, at, :].bitcast(F32), ALU.subtract)\
                    .then_inc(y_lo_ready, 1)

            def mask(head, j):
                first = P * j - META
                lo, hi = P_FROM[j], min(first + P, SEQ)
                rows_ = min(P, L - key0(j))
                at = ps[0:rows_, st_bank(head, j), lo - S_FROM[j]:hi - S_FROM[j]]
                m = lo - first + AHEAD
                v.wait_ge(st_done, count(head, KEY_TILES, j + 1))
                v.tensor_tensor(at, at, causal_t[0:rows_, m:m + hi - lo], ALU.add).then_inc(st_masked, 1)

            def attend(head, steps, previous=None, last=False, fills=True):
                for j in steps:
                    if fills:
                        take_fills(filled_in(head, j), fills_at(j, 0))
                    if j < KEY_TILES - 2:
                        mask(head, j + 2)
                    elif not last:
                        mask(next_head(head), j + 2 - KEY_TILES)
                    if fills and j == TAIL + 1:
                        take_fills(filled_in(head, j - 1), fills_at(j - 1, 1, 2, 3))
                    if fills and j != TAIL:
                        take_fills(filled_in(head, j), fills_at(j, 1, 2, 3))
                    if previous is not None:
                        if j == 1:
                            invert_sums(previous)
                    if last and j < 2:
                        split_lo(N_OUT + j)
                    elif last and j < 5:
                        y_low(Y_ORDER[j - 2])

            v.wait_ge(proj_act, N_JOBS)
            v.wait_ge(kr_ready, 1)
            for b in range(2):
                v.memset(kT_hi[b][HD:HD + 1, :].bitcast(F32), 1.0).then_inc(ones_ready, 1)
                v.memset(vs[b][:, :, VDIM:VDIM + 1], 1.0).then_inc(ones_ready, 1)
            v.memset(max_parts[:, :, :], MASKED).then_inc(ones_ready, 1)
            v.wait_ge(ones_ready, 5)
            take_fills((None, 0), list(enumerate(FILLS)))
            mask((None, 0), 0)
            mask((None, 0), 1)
            take_fills((None, 1), FILLS_AHEAD)
            attend((None, 0), BODY)
            with v.Fori(0, HEADS // 2 - 1) as i:
                for n in (1, 2):
                    attend((i, n - 1), END)
                    attend((i, n), BODY, previous=(i, n - 1))
            attend((None, HEADS - 2), END, fills=False)
            attend((None, HEADS - 1), BODY, previous=(None, HEADS - 2), last=True, fills=False)
            attend((None, HEADS - 1), END, last=True, fills=False)
            for k in Y_ORDER[3:7]:
                y_low(k)
            invert_sums((None, HEADS - 1))
            divide(v, (None, HEADS - 1))
            y_low(Y_ORDER[7])

            for d in range(KT):
                split_lo(N_OUT + d + 2)
                v.wait_ge(w_used, N_OUT + d + 1)
                v.wait_ge(resid_landed, 16 * KT)
                b = 2 * (d % 2)
                v.tensor_tensor(resid[:, d, :], psf[:, b * 512:b * 512 + SEQ], resid[:, d, :], ALU.add)\
                    .then_inc(h2_ready, 1)
                v.wait_ge(g_hi_ready, d + 1)
                v.scalar_tensor_tensor(out=g_lo[:, d, :], in0=resid[:, d, :],
                                       scalar=cols[:, C_FFN + d:C_FFN + d + 1],
                                       in1=g_hi[:, d, :].bitcast(F32), op0=ALU.mult, op1=ALU.subtract)\
                    .then_inc(g_lo_ready, 1)
                if d >= 1:
                    v.wait_ge(g_sq_ready, d + 1)
                    if d >= 2:
                        v.wait_ge(g_sq_added, d - 1)
                    v.tensor_tensor(r_sq[:, :], r_sq[:, :], r_sq_tmp[:, :], ALU.add)\
                        .then_inc(g_sq_added, 1)

            def gate_up(g, c, i, s):
                for j in range(2):
                    first = i is None and g == 0 and j == 0
                    t = in_loop(i, 4, 2 * g + j)
                    after = in_loop(i, 4, 2 * g + j + 1)
                    split_lo(c + 2 * j + 2, i)
                    if first:
                        v.wait_ge(r2_root_ready, 1)
                        v.reciprocal(r2[:, :], r2_root[:, :]).then_inc(r2_ready, 1)
                        v.wait_ge(r2_ready, 1)
                        v.sem_inc(down_bank_free, 4)
                    else:
                        v.wait_ge(silu_ready, t)
                    v.wait_ge(w_used, in_loop(i, PER, c + 2 * j + 1))
                    v.tensor_tensor(gate_in[:, :], psf[:, 0:SEQ], r2[:, :], ALU.mult)\
                        .then_inc(gate_in_ready, 1)
                    split_lo(c + 2 * j + 3, i)
                    v.wait_ge(w_used, in_loop(i, PER, c + 2 * j + 2))
                    v.tensor_tensor(up[:, :], psf[:, SEQ:2 * SEQ], r2[:, :], ALU.mult).then_inc(up_ready, 1)
                    v.wait_ge(up_ready, after)
                    v.wait_ge(silu_ready, after)
                    v.tensor_tensor(act[:, :], gate[:, :], up[:, :], ALU.mult).then_inc(act_ready, 1)
                    v.wait_ge(act_hi_ready, after)
                    v.tensor_tensor(act_lo[s][j][:, :], act[:, :], act_hi[s][j][:, :].bitcast(F32),
                                    ALU.subtract).then_inc(act_lo_ready, 1)

            def down(g, c, i):
                for x in range(2 * KT):
                    if x == 5 and c + 2 < N_ALL:
                        split_lo(c + 2, i)
                    d, half = x // 2, x % 2
                    out = resid[:, d, 512 * half:512 * (half + 1)]
                    if x < 2 * KT - 1:
                        v.wait_ge(down_done, in_loop(i, 2 * (2 * KT - 1), (2 * KT - 1) * g + x + 1))
                    else:
                        v.wait_ge(w_used, in_loop(i, PER, c + 2))
                    v.tensor_tensor(out, ps[:, 4 + x % 4, :], out, ALU.add).then_inc(down_bank_free, 1)
                if c + 3 < N_ALL:
                    split_lo(c + 3, i)

            gate_up(0, N_F, None, 0)
            with v.Fori(0, LOOPS) as i:
                gate_up(1, N_L, i, 1)
                down(0, N_L + 4, i)
                gate_up(2, N_L + 6, i, 0)
                down(1, N_L + 10, i)
            down(GROUPS - 1, N_ALL - 2, None)

        @block.tensor
        def _(pe):
            def passes(out, w_h, w_l, x_h, x_l, first, last):
                pe.matmul(out, w_h, x_h, start=first, stop=False)
                pe.matmul(out, w_h, x_l, start=False, stop=False)
                return pe.matmul(out, w_l, x_h, start=False, stop=last)

            def weights(c, k, width, m):
                s = c % N_SPLIT
                return (w_hi[s][:, k * width:k * width + m], w_lo[s][:, k * width:k * width + m])

            def z_step(s, k):
                w = IN_COLS[s][1]
                w_h, w_l = weights(s, k, w, w)
                for b in range(3):
                    x = slice(b * ZW, (b + 1) * ZW)
                    last = passes(ps[0:w, z_banks(s) + b, 0:ZW], w_h, w_l, h_hi[k][:, x], h_lo[k][:, x],
                                  k == 0, k == KT - 1)
                return last

            def transpose_tiles(src, starts, col):
                for n, start in enumerate(starts):
                    last = pe.transpose(psf[:, col + n * P:col + (n + 1) * P], src[:, start:start + P],
                                        ident[:, :])
                return last

            def transpose_last(src, col):
                return pe.transpose(psf[0:META, col:col + P], src[:, key0(NT):L], ident[:, :])

            pe.wait_ge(w_lo_ready, 2)
            for k in range(KT):
                pe.wait_ge(h_lo_ready, k + 1)
                for s in range(2):
                    last = z_step(s, k)
                    if k == KT - 1:
                        last.then_inc(w_used, 1)
            for s in range(2, N_STEPS):
                pe.wait_ge(w_lo_ready, s + 1)
                pe.wait_ge(z_act_done, ACT_READS[s - 2])
                pe.wait_ge(z_dve_done, DVE_READS[s - 2])
                for k in range(KT):
                    last = z_step(s, k)
                last.then_inc(w_used, 1)
                if s == 2:
                    pe.wait_ge(const_ready, 5)
                    pe.wait_ge(h_sq_added, KT - 1)
                    transpose_tiles(h_sq, [key0(t) for t in range(NT)], 6 * 512).then_inc(aux_done, 1)
                if s == 3:
                    pe.wait_ge(aux_dve, 1)
                    transpose_last(h_sq, 6 * 512)
                    pe.wait_ge(z_act_done, 3)
                    for t in range(NT + 1):
                        n = min(P, L - key0(t))
                        pe.transpose(psf[0:n, 6 * 512 + P + t * ROPE:6 * 512 + P + (t + 1) * ROPE],
                                     zr[:, key0(t):key0(t) + n], ident[0:ROPE, 0:ROPE])
                    pe.wait_ge(z_sq_added, 1)
                    transpose_tiles(z_sq, [key0(t) for t in range(4)], 7 * 512).then_inc(aux_done, 1)
                if s == 4:
                    pe.wait_ge(r_h_ready, 1)
                    pe.wait_ge(aux_dve, 2)
                    for t in range(6):
                        last = pe.matmul(psf[:, 6 * 512 + t * P:6 * 512 + (t + 1) * P],
                                         r_h[:, t:t + 1].to_broadcast([P, P]), ident[:, :],
                                         start=True, stop=True)
                    last.then_inc(aux_done, 1)
                if s == 5:
                    pe.wait_ge(aux_act, 2)
                    for t in range(6, NT):
                        pe.matmul(ps[:, 6, (t - 6) * P:(t - 5) * P], r_h[:, t:t + 1].to_broadcast([P, P]),
                                  ident[:, :], start=True, stop=True)
                    pe.matmul(ps[:, 6, 2 * P:2 * P + META], r_h[0:META, NT:NT + 1].to_broadcast([META, P]),
                              ident[0:META, 0:META], start=True, stop=True)
                    transpose_last(z_sq, 6 * 512 + 3 * P)
                    transpose_tiles(z_sq, [key0(t) for t in range(4, NT)], 7 * 512).then_inc(aux_done, 1)
                if s == 6:
                    pe.wait_ge(aux_dve, 3)
                    pe.wait_ge(z_sq_added, 3)
                    transpose_tiles(h_sq, [token0(t) for t in range(1, NT + 1)], 6 * 512).then_inc(aux_done, 1)
                if s == 7:
                    pe.wait_ge(aux_act, 3)
                    pe.wait_ge(aux_dve, 4)
                    for t in range(NT):
                        last = pe.transpose(psf[:, 6 * 512 + t * 32:6 * 512 + (t + 1) * 32],
                                            r_bcast[0:32, token0(t + 1):token0(t + 1) + P], ident[0:32, 0:32])
                    last.then_inc(aux_done, 1)

            def open_job(j):
                if j == 0:
                    pe.wait_ge(q_ms_ready, 1)
                elif j <= 3:
                    pe.wait_ge(z_dve_done, DVE_READS[-1])
                if j >= 4:
                    pe.wait_ge(proj_act, j - 3)
                return job_bank(j)

            def token_major(j, start, rows_, z0, n_k, tile, width):
                b = open_job(j)
                x = slice(start, start + rows_)
                for k in range(n_k):
                    pe.wait_ge(w_lo_ready, tile + k + 1)
                    w_h, w_l = w_hi[(tile + k) % N_SPLIT], w_lo[(tile + k) % N_SPLIT]
                    z_h, z_l = z_hi[z0 + k], z_lo[z0 + k]
                    for half in range(2):
                        c = slice(half * width, (half + 1) * width)
                        last = passes(ps[0:rows_, b + half, 0:width], z_h[:, x], z_l[:, x], w_h[:, c], w_l[:, c],
                                      k == 0, k == n_k - 1)
                    if k < n_k - 1 and j in JOB_ENDS:
                        last.then_inc(w_used, 1)
                return last.then_inc(w_used if j in JOB_ENDS else proj_done, 1)

            pe.wait_ge(z_dve_done, DVE_READS[5])
            for t in range(NT + 1):
                token_major(t, key0(t), min(P, L - key0(t)), 0, 2, N_KV, KVW // 2)
            pe.wait_ge(w_lo_ready, N_POOL + 1)
            for g in range(POOL_GROUPS):
                j = J_POOL + g
                b = open_job(j)
                pe.wait_ge(p_lo_ready, g + 1)
                w_h, w_l = weights(N_POOL, g, P, P)
                for half in range(2):
                    x = slice(512 * half, 512 * (half + 1))
                    last = passes(ps[:, b + half, :], w_h, w_l, p_hi[:, g, x], p_lo[:, g, x], True, True)
                last.then_inc(w_used if j in JOB_ENDS else proj_done, 1)
            for t in range(NT):
                token_major(J_Q + t, token0(t + 1), P, 2, 3, N_Q, QW // 2)

            def fill(head, fills):
                for x, f in fills:
                    b = head[1] % 2
                    bank = 6 + x % 2
                    if not is_first(head) or x >= 2:
                        pe.wait_ge(misc_free, count(head, N_FILLS, x - 1))
                    if f[0] in "qk":
                        if x == 0 and is_first(head):
                            pe.wait_ge(head0_ready, 1)
                        elif x == 0:
                            pe.wait_ge(qs_ready, count(head, 1, 0))
                        if x == 2:
                            pe.wait_ge(ks_ready, count(head, 1, 1))
                        src = qs if f[0] == "q" else ks
                        for n, t in enumerate(f[1]):
                            rows_ = P if f[0] == "q" else min(P, L - key0(t))
                            last = pe.transpose(ps[0:HD, bank, n * P:n * P + rows_], src[0:rows_, t, :],
                                                ident[0:rows_, 0:rows_])
                    elif f[0] == "n":
                        _, i, m, parts, width = f
                        if x == N_PREP:
                            pe.wait_ge(prep_hi_ready, count(head, N_PREP, N_PREP))
                        start = m * (META + P * (i + 1)) // parts if parts < 3 else m * 352
                        last = pe.matmul(ps[:, bank, 0:width], qT_hi[b][0:HD, i * P:(i + 1) * P],
                                         kT_hi[b][0:HD, start:start + width], start=True, stop=True)
                    else:
                        pe.wait_ge(neg_max_ready, count(head, 1, 1))
                        last = pe.transpose(ps[0:NT, bank, 0:P], neg_max[:, :], ident[:, :])
                    last.then_inc(misc_filled, 1)

            def key_tile(head, j, amid=(None, [])):
                b, bank = head[1] % 2, st_bank(head, j)
                rows_ = min(P, L - key0(j))
                n = SEQ - S_FROM[j]
                parts = 2 if n > 512 else 1
                width = n // parts
                k = slice(key0(j), key0(j) + rows_)
                if j == 0:
                    pe.wait_ge(m_landed, count(head, 16, 16))
                for m in range(parts):
                    c = slice(S_FROM[j] + m * width, S_FROM[j] + (m + 1) * width)
                    out = ps[0:rows_, bank + m, 0:width]
                    pe.matmul(out, kT_hi[b][0:HD + 1, k], qT_hi[b][0:HD + 1, c], start=True, stop=False)
                    pe.matmul(out, kT_hi[b][0:HD, k], qT_lo[b][0:HD, c], start=False, stop=False)
                    last = pe.matmul(out, kT_lo[b][0:HD, k], qT_hi[b][0:HD, c], start=False, stop=True)
                    if m == parts - 1:
                        last.then_inc(st_done, 1)
                    if m == 0:
                        fill(*amid)

            def values(head, j, amid=(None, [])):
                b = head[1] % 2
                rows_ = min(P, L - key0(j))
                if j == 0:
                    pe.wait_ge(vs_ready, count(head, 1, 1))
                    pe.wait_ge(y_taken, count(head, 2, 1))
                for half in range(2):
                    lo, hi = max(P_FROM[j], 512 * half), 512 * (half + 1)
                    if lo < hi:
                        last = pe.matmul(ps[0:VDIM + 1, 4 + half, lo - 512 * half:512], vs[b][0:rows_, j, :],
                                         probT[j % 3][0:rows_, lo - P_FROM[j]:hi - P_FROM[j]],
                                         start=j == 0, stop=j == (4 if half == 0 else KEY_TILES - 1))
                    if half == 0:
                        fill(*amid)
                last.then_inc(pv_done, 1)

            def attend(head, steps, last=False, fills=True):
                for j in steps:
                    pe.wait_ge(exp_done, count(head, KEY_TILES, j + 1))

                    def fills_now(place):
                        return filled_in(head, j), fills_at(j, place) if fills else []

                    if j < KEY_TILES - 2:
                        key_tile(head, j + 2, fills_now(0))
                    elif not last:
                        key_tile(next_head(head), j + 2 - KEY_TILES, fills_now(0))
                    fill(*fills_now(1))
                    values(head, j, fills_now(2))
                    fill(*fills_now(3))

            pe.wait_ge(proj_act, N_JOBS)
            pe.wait_ge(ones_ready, 5)
            fill((None, 0), list(enumerate(FILLS)))
            key_tile((None, 0), 0)
            key_tile((None, 0), 1)
            fill((None, 1), FILLS_AHEAD)
            attend((None, 0), BODY)
            with pe.Fori(0, HEADS // 2 - 1) as i:
                for n in (1, 2):
                    attend((i, n - 1), END)
                    attend((i, n), BODY)
            attend((None, HEADS - 2), END, fills=False)
            attend((None, HEADS - 1), BODY, last=True, fills=False)
            attend((None, HEADS - 1), END, last=True, fills=False)

            y_of = [(yp_hi, yp_lo, k) for k in range(POOL_GROUPS)] + \
                   [(ya_hi, ya_lo, k) for k in range(HEADS // 2)]
            parts = [(0, Y_ORDER[:-1]), (1, Y_ORDER[:-1]), (0, Y_ORDER[-1:]), (1, Y_ORDER[-1:])] + \
                    [(d, Y_ORDER) for d in range(2, KT)]
            for d, blocks in parts:
                n = N_OUT + d
                pe.wait_ge(w_lo_ready, n + 1)
                if d >= 2:
                    pe.wait_ge(h2_ready, d - 1)
                for k in blocks:
                    if d == 0:
                        pe.wait_ge(y_lo_ready, Y_ORDER.index(k) + 1)
                    y_h, y_l, at_k = y_of[k]
                    w_h, w_l = weights(n, k, P, P)
                    for half in range(2):
                        x = slice(512 * half, 512 * (half + 1))
                        last = passes(ps[:, 2 * (d % 2) + half, :], w_h, w_l, y_h[:, at_k, x],
                                      y_l[:, at_k, x], k == Y_ORDER[0], k == Y_ORDER[-1])
                if blocks[-1] == Y_ORDER[-1]:
                    last.then_inc(w_used, 1)

            def ffn_in(c, i, bank, t, first):
                pe.wait_ge(w_lo_ready, in_loop(i, PER, c + 1))
                for k in range(KT):
                    if first:
                        pe.wait_ge(g_lo_ready, k + 1)
                    w_h, w_l = weights(c, k, P, P)
                    for half in range(2):
                        x = slice(512 * half, 512 * (half + 1))
                        last = passes(ps[:, bank + half, :], w_h, w_l, g_hi[:, k, x], g_lo[:, k, x],
                                      k == 0, k == KT - 1)
                last.then_inc(w_used, 1)

            def gate_up(g, c, i):
                for j in range(2):
                    first = i is None and g == 0 and j == 0
                    t = in_loop(i, 4, 2 * g + j)
                    if first:
                        pe.wait_ge(h2_ready, KT - 1)
                    else:
                        pe.wait_ge(gate_in_ready, t)
                    ffn_in(c + 2 * j, i, 0, t, first)
                    if first:
                        pe.wait_ge(g_sq_added, KT - 1)
                        for half in range(2):
                            last = pe.matmul(ps[:, 4 + half, :], ones[:, :],
                                             r_sq[:, 512 * half:512 * (half + 1)], start=True, stop=True)
                        last.then_inc(ms2_done, 1)
                        pe.wait_ge(h2_ready, KT)
                    else:
                        pe.wait_ge(up_ready, t)
                    ffn_in(c + 2 * j + 1, i, 2, t, False)

            def down(g, c, i, s):
                pe.wait_ge(w_lo_ready, in_loop(i, PER, c + 2))
                pe.wait_ge(act_lo_ready, in_loop(i, 4, 2 * g + 2))
                for x in range(2 * KT):
                    d, half = x // 2, x % 2
                    pe.wait_ge(down_bank_free, in_loop(i, 4 * KT, 2 * KT * g + x + 1))
                    tok = slice(512 * half, 512 * (half + 1))
                    for j in range(2):
                        w_h, w_l = weights(c + j, d, P, P)
                        last = passes(ps[:, 4 + x % 4, :], w_h, w_l, act_hi[s][j][:, tok],
                                      act_lo[s][j][:, tok], j == 0, j == 1)
                        if j == 0 and x == 2 * KT - 1:
                            last.then_inc(w_used, 1)
                    last.then_inc(down_done if x < 2 * KT - 1 else w_used, 1)

            gate_up(0, N_F, None)
            with pe.Fori(0, LOOPS) as i:
                gate_up(1, N_L, i)
                down(0, N_L + 4, i, 0)
                gate_up(2, N_L + 6, i)
                down(1, N_L + 10, i, 1)
            down(GROUPS - 1, N_ALL - 2, None, 0)


def kernel(x, meta_tokens, attn_norm_g, w_in, w_pool, pool_scale, q_a_norm_g, w_q_b, kv_a_norm_g, w_kv_b,
           q_norm_g, k_norm_g, w_out, ffn_norm_g, w_gate, w_up, w_down):
    import numpy as np
    from concourse import bacc
    from concourse.bass_utils import run_bass_kernel_spmd

    x, meta_tokens = np.asarray(x), np.asarray(meta_tokens)
    length = meta_tokens.shape[0] + x.shape[1]
    n_tiles = x.shape[1] // P

    xT = np.ascontiguousarray(np.concatenate([meta_tokens, x[0]], axis=0).T)

    def blocks(g):
        return np.asarray(g)[0].reshape(-1, P).T

    def head_gain(g):
        return np.concatenate([np.asarray(g)[0, :NOPE], np.ones(P - NOPE, np.float32)])[:, None]

    columns = np.ascontiguousarray(np.concatenate(
        [blocks(attn_norm_g), blocks(ffn_norm_g), blocks(kv_a_norm_g), blocks(q_a_norm_g),
         blocks(pool_scale), head_gain(q_norm_g), head_gain(k_norm_g)], axis=1))
    rows = np.ascontiguousarray(np.broadcast_to(
        np.concatenate([np.asarray(q_norm_g)[0, NOPE:], np.asarray(k_norm_g)[0, NOPE:]]), (P, 2 * ROPE)))

    inv = 1.0 / (np.float32(10000.0) ** (np.arange(0, ROPE, 2, dtype=np.float32) / np.float32(ROPE)))
    starts = [token0(t + 1) for t in range(n_tiles)] + [key0(t) for t in range(n_tiles + 1)]
    token = np.stack([start + np.arange(P) for start in starts], axis=1)
    angle = token.astype(np.float32)[:, :, None] * inv[None, None, :].astype(np.float32)
    cos, sin = np.cos(angle).astype(np.float32), np.sin(angle).astype(np.float32)
    rope_cos = np.ascontiguousarray(np.concatenate([cos, cos], axis=2))
    rope_sin = np.ascontiguousarray(np.concatenate([-sin, sin], axis=2))

    nc = bacc.Bacc("TRN2", target_bir_lowering=False, num_devices=1)
    arrays, args = {}, []
    for name, a in [("xT", xT), ("w_in", w_in), ("w_pool", w_pool), ("w_q_b", w_q_b), ("w_kv_b", w_kv_b),
                    ("w_out", w_out), ("w_gate", w_gate), ("w_up", w_up), ("w_down", w_down),
                    ("columns", columns), ("rows", rows), ("rope_cos", rope_cos), ("rope_sin", rope_sin)]:
        arrays[f"in_{name}"] = np.ascontiguousarray(a)
        args.append(nc.dram_tensor(f"in_{name}", arrays[f"in_{name}"].shape, F32, kind="ExternalInput").ap())
    outT = nc.dram_tensor("outT", (x.shape[2], x.shape[1]), F32, kind="ExternalOutput").ap()
    inverses = nc.dram_tensor("inverses", (n_tiles * P // 16, 16), F32, kind="Internal").ap()
    build(nc, *args, inverses, outT)
    got = run_bass_kernel_spmd(nc, [arrays], core_ids=[0]).results[0]["outT"]
    return np.ascontiguousarray(np.asarray(got).T)[None]
```

```python
from contextlib import ExitStack

import concourse.bass as bass
from concourse import mybir

F32 = mybir.dt.float32
F32R = mybir.dt.float32r
ALU = mybir.AluOpType
ACT = mybir.ActivationFunctionType
AX = mybir.AxisListType

P = 128
META = 16
EPS = 1e-6
MASKED = -1e30
N_RAW, N_SPLIT, N_H = 2, 3, 4
POOL_GROUPS = 4
EARLY = 2
HEADS = 8
NOPE, ROPE, VDIM = 64, 32, 64
HD = NOPE + ROPE
C_ATTN, C_FFN, C_Z, C_POOL, C_QN, C_KN = 0, 8, 16, 21, 25, 26
N_COLS = 27


def token0(t):
    return 0 if t == 0 else META + P * (t - 1)


def key0(t):
    return P * t


def misc_fills():
    fills = [("q", [0, 1, 2, 3]), ("q", [4, 5, 6, 7]), ("k", [0, 1, 2, 3]), ("k", [4, 5, 6]), ("k", [7, 8])]
    for i in range(8):
        n = META + P * (i + 1)
        parts = -(-n // 512)
        width = n // parts if parts < 3 else 352
        fills += [("n", i, m, parts, min(width, n - m * width)) for m in range(parts)]
    return fills + [("m",)]


FILLS = misc_fills()
N_FILLS = len(FILLS)
N_PREP = 5
FIRST = FILLS[2:N_PREP]
for tile in range(8):
    FIRST = FIRST + [("q", [tile])] + [f for f in FILLS if f[0] == "n" and f[1] == tile]
FIRST = FIRST + [("m",)]
FIRST_MORE = len(FIRST) - N_FILLS
FILL_AT = [(7, 0), (7, 1), (8, 1), (8, 3), (0, 1), (0, 2), (0, 3), (0, 3), (1, 1), (1, 2), (1, 2), (1, 3),
           (2, 1), (2, 2), (2, 3), (2, 3), (2, 3), (3, 2), (3, 2), (4, 1)]
TAIL = 7
KEY_TILES = 9
S_FROM = [0, 112, 240, 368, 416, 624, 752, 768, 768]
AHEAD = 80
P_FROM = [0, 112, 240, 368, 416, 624, 752, 880, 928]


def build(nc, xT, w_in, w_pool, w_q_b, w_kv_b, w_out, w_gate, w_up, w_down, columns, rows, rope_cos,
          rope_sin, inverses, outT):
    D = w_in.shape[1]
    L = xT.shape[1]
    SEQ = L - META
    KT = D // P
    ZW = (L + 2) // 3 + ((L + 2) // 3) % 2
    LP = 3 * ZW
    NT = SEQ // P
    N_FFN = w_gate.shape[2]
    FT = N_FFN // P
    GROUPS = FT // 2
    LOOPS = (GROUPS - 1) // 2
    QW, KVW = w_q_b.shape[2], w_kv_b.shape[2]
    POOLW = POOL_GROUPS * P
    SCALE = float(HD) ** -0.5
    assert len(FILL_AT) == N_FILLS == 20 and SEQ + META == P * (KEY_TILES - 1) + META
    assert GROUPS % 2 == 1 and KT == 8 and NT == 8 and SEQ == 1024 and HEADS == 8

    Q0, KV0 = POOLW, POOLW + 3 * P
    R0 = KV0 + 2 * P
    IN_COLS = [(KV0, P), (KV0 + P, P), (R0, ROPE), (Q0, P), (Q0 + P, P), (Q0 + 2 * P, P)] + \
              [(g * P, P) for g in range(POOL_GROUPS)]
    in_cols = w_in[0].rearrange("(k p) c -> p k c", p=P)
    early = [(in_cols[:, :, c:c + w], KT, w) for c, w in IN_COLS]
    N_KV = len(early)
    early += [(w_kv_b[0, k * P:(k + 1) * P, :], 1, KVW) for k in range(2)]
    N_POOL = len(early)
    early += [(w_pool[0].rearrange("g c d -> c g d"), POOL_GROUPS, P)]
    N_Q = len(early)
    early += [(w_q_b[0, k * P:(k + 1) * P, :], 1, QW) for k in range(3)]
    N_OUT = len(early)
    out_cols = w_out[0].rearrange("(k p) c -> p k c", p=P)
    early += [(out_cols[:, :, d * P:(d + 1) * P], KT, P) for d in range(KT)]
    N_F = len(early)
    assert N_F % N_SPLIT == 0 and N_F % N_RAW == 0
    gate_t = w_gate[0].rearrange("(k p) (f c) -> f p k c", p=P, c=P)
    up_t = w_up[0].rearrange("(k p) (f c) -> f p k c", p=P, c=P)
    down_t = w_down[0].rearrange("(f p) c -> f p c", p=P)
    N_ALL = N_F + 3 * FT
    PER = 12
    N_L = N_F + 4

    with ExitStack() as ctx:
        def sem(name):
            return ctx.enter_context(nc.semaphore(name))

        cursor = [nc.sbuf_base + (-nc.sbuf_base) % 32]

        def size(shape):
            n = 4
            for s in shape[1:]:
                n *= s
            return n + (-n) % 32

        def take(name, shape, dt=F32):
            t = nc.alloc_sbuf_tensor_at(name, shape, dt, offset=cursor[0])
            cursor[0] += size(shape)
            assert cursor[0] <= nc.sbuf_top, (name, cursor[0] - nc.sbuf_top)
            return t

        w_raw = [take(f"w_raw{i}", [P, 1024]) for i in range(N_RAW)]
        w_hi = [take(f"w_hi{i}", [P, 1024], F32R) for i in range(N_SPLIT)]
        w_lo = [take(f"w_lo{i}", [P, 1024], F32R) for i in range(N_SPLIT)]
        ident = take("ident", [P, P])
        ones = take("ones", [P, P])
        causal = take("causal", [P, P])
        causal_t = take("causal_t", [P, AHEAD + P])
        cols = take("cols", [P, N_COLS])
        gains = take("gains", [P, 2 * ROPE])
        eps = take("eps", [P, 1])
        q_scale_col = take("q_scale_col", [P, 1])
        h_ms = take("h_ms", [P, NT + 1])
        h_root = take("h_root", [P, NT + 1])
        r_h = take("r_h", [P, NT + 1])
        r_h2 = take("r_h2", [P, NT + 1])
        r_hq = take("r_hq", [P, NT])
        r_hq2 = take("r_hq2", [P, NT])
        kv_sum = take("kv_sum", [P, NT + 1])
        q_sum = take("q_sum", [P, NT])
        kv_ms = take("kv_ms", [P, NT + 1])
        kv_root = take("kv_root", [P, NT + 1])
        kv_inv = take("kv_inv", [P, NT + 1])
        s_kv = take("s_kv", [P, NT + 1])
        q_ms = take("q_ms", [P, NT])
        q_root = take("q_root", [P, NT])
        q_inv = take("q_inv", [P, NT])
        s_q = take("s_q", [P, NT])
        max_parts = take("max_parts", [P, NT, 3])
        neg_max = take("neg_max", [P, NT])
        KN, KR = 0, (NT + 1) * HEADS
        QS = KR + NT + 1
        N_SS = QS + NT * 2 * HEADS
        scratch_at = cursor[0]
        q_cos = take("q_cos", [P, NT, ROPE])
        q_sin = take("q_sin", [P, NT, ROPE])
        krn = take("krn", [P, NT + 1, ROPE])
        ssq = take("ssq", [P, N_SS])
        rs = take("rs", [P, N_SS])
        yp_at = cursor[0]
        p_hi = take("p_hi", [P, POOL_GROUPS, SEQ], F32R)
        r1_at = cursor[0]
        p_lo = take("p_lo", [P, POOL_GROUPS, SEQ], F32R)
        base = cursor[0]

        h_hi = [take(f"h_hi{k}", [P, LP], F32R) for k in range(KT)]
        h_lo = [take(f"h_lo{k}", [P, LP], F32R) for k in range(KT)]
        z_hi = [take(f"z_hi{k}", [P, LP], F32R) for k in range(5)]
        z_lo = [take(f"z_lo{k}", [P, LP], F32R) for k in range(5)]
        late = cursor[0]
        h_raw = [take(f"h_raw{i}", [P, LP]) for i in range(2)]
        square = take("square", [P, LP])
        h_sq = take("h_sq", [P, LP])
        z_sq = take("z_sq", [P, LP])
        r_bcast = take("r_bcast", [P, LP])
        zr = take("zr", [ROPE, LP])
        u, win = h_raw[0], [h_raw[1], square]
        h_raw += [z_sq, r_bcast]

        y_space = HEADS // 2 * size([P, SEQ])
        ya_at = nc.sbuf_top - y_space - 32
        ya_at -= ya_at % 32
        ya_hi_at = ya_at - y_space

        cursor[0] = base
        kvn = take("kvn", [P, NT + 1, KVW])
        qn = take("qn", [P, NT, QW])
        attn_at = cursor[0]
        cos2 = take("cos2", [P, 2 * NT + 1, ROPE])
        sin2 = take("sin2", [P, 2 * NT + 1, ROPE])
        cursor[0] = ya_at
        sq_tmp = [take(f"sq_tmp{i}", [P, QW]) for i in range(2)]
        kr_b = take("kr_b", [P, NT + 1, ROPE])
        k_cos = take("k_cos", [P, NT + 1, ROPE])
        k_sin = take("k_sin", [P, NT + 1, ROPE])
        kr_a = take("kr_a", [P, NT + 1, ROPE])

        yp = nc.alloc_sbuf_tensor_at("yp", [P, POOL_GROUPS, SEQ], F32, offset=yp_at)
        yp_lo = nc.alloc_sbuf_tensor_at("yp_lo", [P, POOL_GROUPS, SEQ], F32R, offset=yp_at)
        yp_hi = nc.alloc_sbuf_tensor_at("yp_hi", [P, POOL_GROUPS, SEQ], F32R, offset=r1_at)
        ya = nc.alloc_sbuf_tensor_at("ya", [P, HEADS // 2, SEQ], F32, offset=ya_at)
        ya_lo = nc.alloc_sbuf_tensor_at("ya_lo", [P, HEADS // 2, SEQ], F32R, offset=ya_at)
        ya_hi = nc.alloc_sbuf_tensor_at("ya_hi", [P, HEADS // 2, SEQ], F32R, offset=ya_hi_at)

        qT_hi, qT_lo, kT_hi, kT_lo = [None, None], [None, None], [None, None], [None, None]
        cursor[0] = r1_at
        qs = take("qs", [P, NT, HD])
        ks = take("ks", [P, NT + 1, HD])
        rope_v = take("rope_v", [P, NT, ROPE])
        rope_a = take("rope_a", [P, NT, ROPE])
        rope_b = take("rope_b", [P, NT, ROPE])
        assert cursor[0] <= r1_at + 3 * size([P, SEQ])
        cursor[0] = r1_at + 3 * size([P, SEQ])
        y_raw = [take("y_raw0", [P, SEQ]), None]
        assert cursor[0] <= base
        cursor[0] = ya_hi_at
        vs = [take("vs0", [P, NT + 1, VDIM + 1]), None]
        cursor[0] = max(cursor[0], late)
        qT_hi[0] = take("qT_hi0", [P, SEQ], F32R)
        kT_hi[0] = take("kT_hi0", [P, L], F32R)
        kT_lo[0] = take("kT_lo0", [P, L], F32R)
        neg_max8 = take("neg_max8", [NT, P], F32R)
        denom = take("denom", [SEQ // 16, 16])
        inv_denom = take("inv_denom", [SEQ // 16, 16])
        assert cursor[0] <= ya_at
        cursor[0] = attn_at
        qT_lo[0] = take("qT_lo0", [P, SEQ], F32R)
        assert cursor[0] <= base + 2 * KT * size([P, LP])
        qT_hi[1] = take("qT_hi1", [P, SEQ], F32R)
        qT_lo[1] = take("qT_lo1", [P, SEQ], F32R)
        kT_hi[1] = take("kT_hi1", [P, L], F32R)
        kT_lo[1] = take("kT_lo1", [P, L], F32R)
        probT = [take(f"probT{j}", [P, SEQ - P_FROM[j]]) for j in range(3)]
        vs[1] = take("vs1", [P, NT + 1, VDIM + 1])
        y_raw[1] = take("y_raw1", [P, SEQ])
        inv_l = take("inv_l", [P, SEQ])
        assert cursor[0] <= ya_hi_at

        cursor[0] = base
        resid = take("resid", [P, KT, SEQ])
        g_hi = take("g_hi", [P, KT, SEQ], F32R)
        g_lo = take("g_lo", [P, KT, SEQ], F32R)
        r_sq = take("r_sq", [P, SEQ])
        r_sq_tmp = nc.alloc_sbuf_tensor_at("r_sq_tmp", [P, SEQ], F32, offset=scratch_at)
        assert scratch_at + size([P, SEQ]) <= yp_at
        assert cursor[0] <= ya_hi_at

        cursor[0] = yp_at
        r2 = take("r2", [P, SEQ])
        r2_root = take("r2_root", [P, SEQ])
        gate_in = take("gate_in", [P, SEQ])
        gate = take("gate", [P, SEQ])
        up = take("up", [P, SEQ])
        act = take("act", [P, SEQ])
        assert cursor[0] <= base
        cursor[0] = ya_hi_at
        act_hi = [[take(f"act_hi{s}{j}", [P, SEQ], F32R) for j in range(2)] for s in range(2)]
        act_lo = [[take(f"act_lo{s}{j}", [P, SEQ], F32R) for j in range(2)] for s in range(2)]

        ps = ctx.enter_context(nc.psum_tensor("ps", [P, 8, 512], F32))
        psf = ps[:, :, :].rearrange("p b c -> p (b c)")

        columns_landed = sem("columns_landed")
        rope_landed = sem("rope_landed")
        raw_landed = [sem(f"raw_landed{i}") for i in range(N_RAW)]
        w_hi_ready = sem("w_hi_ready")
        w_lo_ready = sem("w_lo_ready")
        w_used = sem("w_used")
        h_landed = [sem(f"h_landed{i}") for i in range(N_H)]
        pad_ready = sem("pad_ready")
        h_hi_ready = sem("h_hi_ready")
        h_sq_ready = sem("h_sq_ready")
        h_lo_ready = sem("h_lo_ready")
        h_sq_added = sem("h_sq_added")
        const_ready = sem("const_ready")
        z_hi_ready = sem("z_hi_ready")
        z_act_done = sem("z_act_done")
        z_dve_done = sem("z_dve_done")
        z_sq_added = sem("z_sq_added")
        aux_done = sem("aux_done")
        aux_act = sem("aux_act")
        aux_dve = sem("aux_dve")
        dve_step = sem("dve_step")
        pool_step = sem("pool_step")
        h_ms_ready = sem("h_ms_ready")
        h_root_ready = sem("h_root_ready")
        r_h_ready = sem("r_h_ready")
        kv_ms_ready = sem("kv_ms_ready")
        kv_root_ready = sem("kv_root_ready")
        s_kv_ready = sem("s_kv_ready")
        q_ms_ready = sem("q_ms_ready")
        q_root_ready = sem("q_root_ready")
        s_q_ready = sem("s_q_ready")
        p_ready = sem("p_ready")
        p_hi_ready = sem("p_hi_ready")
        p_lo_ready = sem("p_lo_ready")
        proj_done = sem("proj_done")
        proj_act = sem("proj_act")
        kv_pad_ready = sem("kv_pad_ready")
        sq_ready = sem("sq_ready")
        ssq_added = sem("ssq_added")
        root_ready = sem("root_ready")
        rs_k_ready = sem("rs_k_ready")
        rs_ready = sem("rs_ready")
        q_sq_ready = sem("q_sq_ready")
        q_scale_ready = sem("q_scale_ready")
        kr_ready = sem("kr_ready")
        head0_ready = sem("head0_ready")
        qs_ready = sem("qs_ready")
        ks_ready = sem("ks_ready")
        vs_ready = sem("vs_ready")
        ones_ready = sem("ones_ready")
        misc_filled = sem("misc_filled")
        prep_hi_ready = sem("prep_hi_ready")
        misc_free = sem("misc_free")
        nat_masked = sem("nat_masked")
        neg_max_ready = sem("neg_max_ready")
        m_landed = sem("m_landed")
        st_done = sem("st_done")
        st_masked = sem("st_masked")
        exp_done = sem("exp_done")
        pv_done = sem("pv_done")
        y_taken = sem("y_taken")
        l_landed = sem("l_landed")
        inv_denom_ready = sem("inv_denom_ready")
        inv_row_landed = sem("inv_row_landed")
        inv_l_landed = sem("inv_l_landed")
        ya_ready = sem("ya_ready")
        y_hi_ready = sem("y_hi_ready")
        y_lo_ready = sem("y_lo_ready")
        resid_landed = sem("resid_landed")
        h2_ready = sem("h2_ready")
        g_hi_ready = sem("g_hi_ready")
        g_sq_ready = sem("g_sq_ready")
        g_lo_ready = sem("g_lo_ready")
        g_sq_added = sem("g_sq_added")
        ms2_done = sem("ms2_done")
        r2_root_ready = sem("r2_root_ready")
        r2_ready = sem("r2_ready")
        gate_in_ready = sem("gate_in_ready")
        silu_ready = sem("silu_ready")
        up_ready = sem("up_ready")
        act_ready = sem("act_ready")
        act_hi_ready = sem("act_hi_ready")
        act_lo_ready = sem("act_lo_ready")
        down_done = sem("down_done")
        down_bank_free = sem("down_bank_free")
        out_landed = sem("out_landed")

        Z_OF_STEP = {0: 0, 1: 1, 3: 2, 4: 3, 5: 4}
        ACT_READS = [1, 2, 3, 4, 5, 6, 6, 6, 6, 6]
        DVE_READS = [1, 2, 2, 3, 4, 5, 6, 7, 8, 9]
        N_STEPS = len(IN_COLS)
        J_POOL, J_Q, N_JOBS = NT + 1, NT + 1 + POOL_GROUPS, 2 * NT + 1 + POOL_GROUPS

        JOB_ENDS = {J_POOL - 1: N_POOL, J_Q - 1: N_Q, N_JOBS - 1: N_OUT}

        def z_banks(step):
            return 3 * (step % 2)

        def job_bank(job):
            return 2 * ((job + 3) % 4) if job < J_Q else 2 * ((job - J_Q) % 3)

        def wait_for_job(engine, j):
            if j in JOB_ENDS:
                engine.wait_ge(w_used, JOB_ENDS[j])
            else:
                engine.wait_ge(proj_done, j + 1 - sum(1 for e in JOB_ENDS if e < j))

        def count(head, per, c):
            i, n = head
            return n * per + c if i is None else i * (2 * per) + (n * per + c)

        def next_head(head):
            return head[0], head[1] + 1

        Y_ORDER = [0, 1, 2, 4, 5, 3, 6, 7]

        def is_first(head):
            return head[0] is None and head[1] == 0

        def first_fills(*what):
            return [(x, f) for x, f in enumerate(FIRST)
                    if (f[0] if f[0] in "km" else f[1] if f[0] == "n" else f[1][0]) in what]

        def fill_count(head, c):
            return c if is_first(head) else count(head, N_FILLS, c) + FIRST_MORE

        def prep_count(head, x):
            if is_first(head):
                return sum(1 for f in FIRST[:x + 1] if f[0] in "qk")
            return count(head, N_PREP, min(x + 1, N_PREP)) + FIRST_MORE

        def last_prep(i):
            return next(x for x, f in enumerate(FILLS) if f[0] == "k" and
                        min(key0(f[1][-1] + 1), L) >= META + P * (i + 1))

        def fills_at(j, *places):
            return [(x, FILLS[x]) for x in range(N_FILLS) for place in places if FILL_AT[x] == (j, place)]

        FIRST_IN = [(), ("k",), (0,), (1,), (2,), (3,), (4,), (5,)]
        FIRST_END = (6, 7, "m")

        FILLS_AHEAD = [(x, FILLS[x]) for x in range(N_FILLS) if FILL_AT[x][0] >= TAIL]
        BODY, END = range(TAIL), range(TAIL, KEY_TILES)

        def divide(engine, head):
            i, n = head
            e, pair = n % 2, (n // 2 if i is None else i + n // 2)
            rows_ = slice(VDIM * e, VDIM * (e + 1))
            engine.wait_ge(inv_l_landed, count(head, 16, 16))
            engine.tensor_tensor(ya[rows_, bass.ds(pair, 1), :].rearrange("p a c -> p (a c)"),
                                 y_raw[e][0:VDIM, :], inv_l[0:VDIM, :], ALU.mult).then_inc(ya_ready, 1)

        def filled_in(head, j):
            return next_head(next_head(head)) if j >= TAIL else next_head(head)

        def in_loop(i, per, c):
            return c if i is None else i * per + c

        def raw_count(n):
            return 16 * (n // N_RAW + 1)

        def transposed(q, k, b, kind, tiles):
            if kind == "q":
                return q[b][0:HD, tiles[0] * P:(tiles[-1] + 1) * P], q_scale_col
            return k[b][0:HD, key0(tiles[0]):min(key0(tiles[-1] + 1), L)], cols[:, C_KN:C_KN + 1]

        def st_bank(head, j):
            return 2 * ((KEY_TILES * head[1] + j) % 2)

        block = ctx.enter_context(nc.Block())

        @block.sync
        def _(sp):
            def load_weights(n):
                src, k, w = early[n]
                if n >= N_RAW:
                    sp.wait_ge(w_lo_ready, n - N_RAW + 1)
                dst = w_raw[n % N_RAW][:, 0:k * w]
                if k > 1:
                    dst = dst.rearrange("p (k c) -> p k c", k=k)
                sp.dma_start(dst, src).then_inc(raw_landed[n % N_RAW], 16)

            def load_h(k):
                if k >= N_H:
                    sp.wait_ge(h_sq_ready, k - N_H + 1)
                    sp.wait_ge(h_lo_ready, k - N_H + 1)
                sp.dma_start(h_raw[k % N_H][:, 0:L], xT[k * P:(k + 1) * P, :])\
                  .then_inc(h_landed[k % N_H], 16)

            sp.dma_start(cols[:, :], columns).then_inc(columns_landed, 16)
            load_h(0)
            load_weights(0)
            load_weights(1)
            for k in range(1, N_H):
                load_h(k)
            load_weights(2)
            load_weights(3)
            for k in range(N_H, KT):
                load_h(k)
            sp.dma_start(gains[:, :], rows).then_inc(columns_landed, 16)
            for n in range(4, N_STEPS + 2):
                load_weights(n)
            sp.wait_ge(w_used, N_STEPS)
            sp.dma_start(cos2[:, :, :], rope_cos).then_inc(rope_landed, 16)
            sp.dma_start(sin2[:, :, :], rope_sin).then_inc(rope_landed, 16)
            for n in range(N_STEPS + 2, N_OUT + 2):
                load_weights(n)

            def send_max(head):
                sp.wait_ge(misc_free, count(head, N_FILLS, N_FILLS) + FIRST_MORE)
                sp.dma_start(qT_hi[head[1] % 2][HD:HD + 1, :].bitcast(F32), neg_max8[:, :].bitcast(F32))\
                  .then_inc(m_landed, 16)

            def send_sums(head):
                sp.wait_ge(y_taken, count(head, 2, 3))
                sp.dma_start(denom[:, :], y_raw[head[1] % 2][VDIM:VDIM + 1, :]).then_inc(l_landed, 16)

            def send_inverses(head):
                sp.wait_ge(inv_denom_ready, count(head, 1, 1))
                sp.dma_start(inverses, inv_denom[:, :]).then_inc(inv_row_landed, 16)
                sp.wait_ge(inv_row_landed, count(head, 16, 16))
                sp.wait_ge(ya_ready, count(head, 1, 1))
                sp.dma_start(inv_l[0:VDIM, :].rearrange("p (r c) -> p r c", r=SEQ // 16),
                             inverses[None, :, :].to_broadcast([VDIM, SEQ // 16, 16]))\
                  .then_inc(inv_l_landed, 16)

            def send(head):
                send_sums(head)
                send_inverses(head)
                send_max(next_head(next_head(head)))

            send_max((None, 0))
            send_max((None, 1))
            send((None, 0))
            with sp.Fori(0, HEADS // 2 - 2) as i:
                send((i, 1))
                send((i, 2))
            send((None, HEADS - 3))
            send_sums((None, HEADS - 2))
            send_inverses((None, HEADS - 2))
            sp.wait_ge(ks_ready, HEADS)
            sp.wait_ge(vs_ready, HEADS)
            for d in range(KT):
                sp.dma_start(resid[:, d, :], xT[d * P:(d + 1) * P, META:L]).then_inc(resid_landed, 16)
            send_sums((None, HEADS - 1))
            send_inverses((None, HEADS - 1))
            for n in range(N_OUT + 2, N_F):
                load_weights(n)

            def load_ffn(src, c, i):
                sp.wait_ge(w_lo_ready, in_loop(i, PER, c - N_RAW + 1))
                dst = w_raw[c % N_RAW][:, :]
                if len(src.shape) == 3:
                    dst = dst.rearrange("p (k c) -> p k c", k=KT)
                sp.dma_start(dst, src).then_inc(raw_landed[c % N_RAW], 16)

            def load_gate_up(f, c, i):
                for j in range(2):
                    load_ffn(gate_t[f + j], c + 2 * j, i)
                    load_ffn(up_t[f + j], c + 2 * j + 1, i)

            def load_down(f, c, i):
                for j in range(2):
                    load_ffn(down_t[f + j], c + j, i)

            load_gate_up(0, N_F, None)
            with sp.Fori(0, LOOPS) as i:
                load_gate_up(i * 4 + 2, N_L, i)
                load_down(i * 4, N_L + 4, i)
                load_gate_up(i * 4 + 4, N_L + 6, i)
                load_down(i * 4 + 2, N_L + 10, i)
            load_down(FT - 2, N_ALL - 2, None)
            for d in range(KT):
                sp.wait_ge(down_bank_free, 4 + 16 * (GROUPS - 1) + 2 * (d + 1))
                sp.dma_start(outT[d * P:(d + 1) * P, :], resid[:, d, :]).then_inc(out_landed, 16)
            sp.wait_ge(out_landed, 16 * KT)

        @block.gpsimd
        def _(pool):
            steps = [0]

            def link(ins):
                steps[0] += 1
                ins.then_inc(pool_step, 1)
                pool.wait_ge(pool_step, steps[0])

            pool.memset(ident[:, :], 0.0).then_inc(pool_step, 1)
            pool.memset(causal[:, :], 0.0).then_inc(pool_step, 1)
            pool.memset(causal_t[:, :], 0.0).then_inc(pool_step, 1)
            pool.memset(ones[:, :], 1.0).then_inc(const_ready, 1)
            pool.memset(eps[:, :], EPS).then_inc(const_ready, 1)
            steps[0] = 3
            pool.wait_ge(pool_step, 3)
            pool.affine_select(out=ident[:, :], in_=ident[:, :], compare_op=ALU.not_equal, fill=1.0,
                               base=0, pattern=[[-1, P]], channel_multiplier=1).then_inc(const_ready, 1)
            pool.affine_select(out=causal[:, :], in_=causal[:, :], compare_op=ALU.is_ge, fill=MASKED,
                               base=0, pattern=[[-1, P]], channel_multiplier=1).then_inc(const_ready, 1)
            pool.affine_select(out=causal_t[:, :], in_=causal_t[:, :], compare_op=ALU.is_ge, fill=MASKED,
                               base=-AHEAD, pattern=[[1, AHEAD + P]], channel_multiplier=-1)\
                .then_inc(const_ready, 1)

            pool.wait_ge(columns_landed, 32)
            pool.wait_ge(rope_landed, 32)
            pool.wait_ge(p_lo_ready, POOL_GROUPS)
            H = ROPE // 2

            def table(out, trig, n, g, swapped):
                for a in range(2):
                    b = 1 - a if swapped else a
                    last = pool.tensor_tensor(
                        out[:, :, a * H:(a + 1) * H],
                        trig[:, 0 if n == NT else NT:n if n == NT else NT + n, a * H:(a + 1) * H],
                        gains[:, None, g + b * H:g + (b + 1) * H].to_broadcast([P, n, H]), ALU.mult)
                return last

            table(q_cos, cos2, NT, 0, False)
            table(q_sin, sin2, NT, 0, True)
            table(k_cos, cos2, NT + 1, ROPE, False)
            link(table(k_sin, sin2, NT + 1, ROPE, True))

            def squares(job, src, out):
                pool.wait_ge(proj_act, job + 1)
                pool.tensor_tensor(out, src, src, ALU.mult).then_inc(sq_ready, 1)

            for t in range(NT + 1):
                if t >= 2:
                    pool.wait_ge(ssq_added, t - 1)
                squares(t, kvn[:, t, :].rearrange("p (h c) -> p h c", h=HEADS)[:, :, 0:NOPE],
                        sq_tmp[t % 2][:, 0:HEADS * NOPE].rearrange("p (h c) -> p h c", h=HEADS))
            def rope(v, cos, sin, a, b, n):
                pool.tensor_tensor(a, v, cos[:, :, :], ALU.mult)
                pool.tensor_tensor(b[:, :, 0:H], v[:, :, H:ROPE], sin[:, :, 0:H], ALU.mult)
                return pool.tensor_tensor(b[:, :, H:ROPE], v[:, :, 0:H], sin[:, :, H:ROPE], ALU.mult)

            pool.wait_ge(rs_k_ready, 1)
            pool.wait_ge(w_used, N_POOL + 1)
            link(pool.tensor_tensor(krn[:, :, :], krn[:, :, :],
                                    rs[:, KR:KR + NT + 1, None].to_broadcast([P, NT + 1, ROPE]), ALU.mult))
            link(rope(krn[:, :, :], k_cos, k_sin, kr_a[:, :, :], kr_b[:, :, :], NT + 1))
            pool.tensor_tensor(ks[:, :, NOPE:HD], kr_a[:, :, :], kr_b[:, :, :], ALU.add).then_inc(kr_ready, 1)
            before = steps[0]

            def stat_k(h):
                return rs[:, KN:KN + (NT + 1) * HEADS].rearrange("p (t h) -> p t h", h=HEADS)[:, :, bass.ds(h, 1)]

            def stat_q(part, h):
                return rs[:, QS:N_SS].rearrange("p (t h) -> p t h", h=2 * HEADS)[:, :, bass.ds(h + part * HEADS, 1)]

            def queries(h):
                pool.tensor_tensor(rope_v[:, :, :], qn[:, :, bass.ds(h * HD + NOPE, ROPE)],
                                   stat_q(1, h).to_broadcast([P, NT, ROPE]), ALU.mult)\
                    .then_inc(pool_step, 1)
                pool.tensor_tensor(qs[:, :, 0:NOPE], qn[:, :, bass.ds(h * HD, NOPE)],
                                   stat_q(0, h).to_broadcast([P, NT, NOPE]), ALU.mult)
                pool.wait_ge(pool_step, h * 2 + (before - 1))
                rope(rope_v[:, :, :], q_cos, q_sin, rope_a[:, :, :], rope_b[:, :, :], NT)\
                    .then_inc(pool_step, 1)
                pool.wait_ge(pool_step, h * 2 + before)
                pool.tensor_tensor(qs[:, :, NOPE:HD], rope_a[:, :, :], rope_b[:, :, :], ALU.add)\
                    .then_inc(qs_ready, 1)

            def keys(h):
                pool.tensor_tensor(ks[:, :, 0:NOPE], kvn[:, :, bass.ds(h * (NOPE + VDIM), NOPE)],
                                   stat_k(h).to_broadcast([P, NT + 1, NOPE]), ALU.mult)\
                    .then_inc(ks_ready, 1)

            def prepare(head):
                i, n = head
                h = n if i is None else i * 2 + n
                if i is None and n == 1:
                    pool.wait_ge(misc_filled, first_fills(7)[0][0] + 1)
                else:
                    pool.wait_ge(misc_filled, count(head, N_FILLS, N_PREP - N_FILLS) + FIRST_MORE)
                queries(h)
                keys(h)

            def divide_after(head, ahead):
                pool.wait_ge(ks_ready, count(head, 1, ahead + 1))
                divide(pool, head)
                pool.wait_ge(ya_ready, count(head, 1, 2))

            keys(0)
            for t in range(NT):
                pool.wait_ge(rs_ready, t + 1)
                v0 = rope_v[:, t, :]
                link(pool.tensor_tensor(v0, qn[:, t, NOPE:HD],
                                        stat_q(1, 0)[:, t, :].to_broadcast([P, ROPE]), ALU.mult))
                pool.tensor_tensor(rope_a[:, t, :], v0, q_cos[:, t, :], ALU.mult)
                pool.tensor_tensor(rope_b[:, t, 0:H], rope_v[:, t, H:ROPE], q_sin[:, t, 0:H], ALU.mult)
                link(pool.tensor_tensor(rope_b[:, t, H:ROPE], rope_v[:, t, 0:H], q_sin[:, t, H:ROPE], ALU.mult))
                pool.tensor_tensor(qs[:, t, NOPE:HD], rope_a[:, t, :], rope_b[:, t, :], ALU.add)
                pool.tensor_tensor(qs[:, t, 0:NOPE], qn[:, t, 0:NOPE],
                                   stat_q(0, 0)[:, t, :].to_broadcast([P, NOPE]), ALU.mult)\
                    .then_inc(head0_ready, 1)
            before = steps[0]
            pool.sem_inc(ya_ready, 1)
            prepare((None, 1))
            prepare((None, 2))
            prepare((None, 3))
            with pool.Fori(0, HEADS // 2 - 2) as i:
                for n in (0, 1):
                    divide_after((i, n), 3)
                    prepare((i, n + 4))
            for h in range(HEADS - 4, HEADS - 1):
                divide_after((None, h), HEADS - 1 - h)

        @block.scalar
        def _(act_e):
            a = act_e

            def split_hi(c, i=None):
                w = 1024 if c >= N_F else early[c][1] * early[c][2]
                a.wait_ge(raw_landed[c % N_RAW], in_loop(i, 16 * PER // N_RAW, raw_count(c)))
                if c >= N_SPLIT:
                    a.wait_ge(w_used, in_loop(i, PER, c - N_SPLIT + 1))
                a.activation(w_hi[c % N_SPLIT][:, 0:w], w_raw[c % N_RAW][:, 0:w], ACT.Copy)\
                    .then_inc(w_hi_ready, 1)

            a.wait_ge(pad_ready, N_H + 1)
            a.activation(h_root[:, NT:], h_ms[:, NT:], ACT.Identity)
            a.wait_ge(columns_landed, 16)
            for k in range(KT):
                a.wait_ge(h_landed[k % N_H], 16 * (k // N_H + 1))
                a.activation(h_hi[k][:, :], h_raw[k % N_H][:, :], ACT.Identity,
                             scale=cols[:, C_ATTN + k:C_ATTN + k + 1]).then_inc(h_hi_ready, 1)
                if k == 0:
                    split_hi(0)
                    split_hi(1)
                if k >= 2:
                    a.wait_ge(h_sq_added, k - 1)
                a.activation((square if k else h_sq)[:, :], h_raw[k % N_H][:, :], ACT.Square)\
                    .then_inc(h_sq_ready, 1)

            def z_view(step, rows=P):
                b = z_banks(step)
                return ps[0:rows, b:b + 3, 0:ZW]

            def tiles3(t, rows=P):
                return t[0:rows, :].rearrange("p (b c) -> p b c", b=3)

            for s in range(N_STEPS):
                split_hi(s + 2)
                if s in Z_OF_STEP:
                    z = Z_OF_STEP[s]
                    a.wait_ge(w_used, s + 1)
                    a.activation(tiles3(z_hi[z]), z_view(s), ACT.Identity,
                                 scale=cols[:, C_Z + z:C_Z + z + 1]).then_inc(z_hi_ready, 1)
                    if s == 1:
                        a.wait_ge(h_sq_added, KT - 1)
                    if s == 3:
                        a.wait_ge(aux_done, 2)
                    if s == 4:
                        a.wait_ge(z_sq_added, 1)
                    if s == 5:
                        a.wait_ge(z_sq_added, 2)
                    dst = {0: z_sq, 1: square, 3: h_sq, 4: square, 5: square}[s]
                    a.activation(tiles3(dst), z_view(s), ACT.Square).then_inc(z_act_done, 1)
                if s == 2:
                    a.wait_ge(w_used, 3)
                    a.activation(tiles3(zr, ROPE), z_view(2, ROPE), ACT.Copy).then_inc(z_act_done, 1)
                if s == 3:
                    a.wait_ge(h_ms_ready, 1)
                    a.wait_ge(const_ready, 5)
                    a.activation(h_root[:, :], h_ms[:, :], ACT.Sqrt, bias=eps[:, :], scale=1.0 / D)\
                        .then_inc(h_root_ready, 1)
                if s == 4:
                    a.wait_ge(aux_done, 3)
                    a.activation(r_bcast[:, 0:512], ps[:, 6, :], ACT.Copy).then_inc(aux_act, 1)
                    a.activation(r_bcast[:, 512:768], ps[:, 7, 0:256], ACT.Copy).then_inc(aux_act, 1)
                if s == 5:
                    a.wait_ge(aux_done, 4)
                    a.activation(r_bcast[:, 768:L], ps[:, 6, 0:L - 768], ACT.Copy).then_inc(aux_act, 1)
                if s == 6:
                    a.wait_ge(kv_ms_ready, 1)
                    a.activation(kv_root[:, :], kv_ms[:, :], ACT.Sqrt, bias=eps[:, :])\
                        .then_inc(kv_root_ready, 1)
                if s == 8:
                    a.wait_ge(q_ms_ready, 1)
                    a.activation(q_root[:, :], q_ms[:, :], ACT.Sqrt, bias=eps[:, :])\
                        .then_inc(q_root_ready, 1)
                if s >= 6:
                    g = s - 6
                    a.wait_ge(p_ready, g + 1)
                    a.activation(p_hi[:, g, :], win[g % 2][:, META:L], ACT.Copy).then_inc(p_hi_ready, 1)

            def high_parts(head, fills):
                for x, fill in fills:
                    if fill[0] in "qk":
                        a.wait_ge(misc_filled, fill_count(head, x + 1))
                        out, gain = transposed(qT_hi, kT_hi, head[1] % 2, *fill)
                        a.activation(out, ps[0:HD, 6 + x % 2, 0:out.shape[1]], ACT.Copy, scale=gain[0:HD, :])\
                            .then_inc(prep_hi_ready, 1)

            def roots(lo, hi, n):
                a.activation(ssq[:, lo:hi], ssq[:, lo:hi], ACT.Sqrt, bias=eps[:, :], scale=1.0 / n)\
                    .then_inc(root_ready, 1)

            for j in range(N_JOBS):
                b = job_bank(j)
                if j == 0:
                    split_hi(N_POOL)
                    a.wait_ge(s_kv_ready, 1)
                    a.wait_ge(q_scale_ready, 1)
                if j == J_POOL:
                    split_hi(N_Q + 1)
                if j == J_Q - 2:
                    split_hi(N_Q + 2)
                if j == J_Q:
                    a.wait_ge(s_q_ready, 1)
                if j == J_POOL + 1:
                    a.wait_ge(ssq_added, NT + 2)
                    roots(KN, KR, NOPE)
                    roots(KR, QS, ROPE)
                if j == J_Q + 1:
                    high_parts((None, 0), first_fills(*FIRST_IN[1]))
                wait_for_job(a, j)
                if j < J_POOL:
                    n = min(P, L - key0(j))
                    if n < P:
                        a.wait_ge(kv_pad_ready, 1)
                        split_hi(N_Q)
                    a.activation(kvn[0:n, j, :], psf[0:n, b * 512:b * 512 + KVW], ACT.Copy,
                                 scale=s_kv[0:n, j:j + 1]).then_inc(proj_act, 1)
                elif j < J_Q:
                    g = j - J_POOL
                    a.activation(yp[:, g, :], psf[:, b * 512:b * 512 + SEQ], ACT.Copy,
                                 scale=cols[:, C_POOL + g:C_POOL + g + 1]).then_inc(proj_act, 1)
                else:
                    t = j - J_Q
                    a.wait_ge(ssq_added, NT + 2 + max(t - 1, 0))
                    a.activation(sq_tmp[t % 2][:, :].rearrange("p (b c) -> p b c", b=2),
                                 ps[:, b:b + 2, 0:QW // 2], ACT.Square, scale=s_q[:, t:t + 1])\
                        .then_inc(q_sq_ready, 1)
                    a.activation(qn[:, t, :].rearrange("p (b c) -> p b c", b=2),
                                 ps[:, b:b + 2, 0:QW // 2], ACT.Copy,
                                 scale=s_q[:, t:t + 1]).then_inc(proj_act, 1)
                    if 1 <= t < NT - 1:
                        high_parts((None, 0), first_fills(*FIRST_IN[t + 1]))
                    a.wait_ge(ssq_added, NT + 2 + t + 1)
                    at = QS + t * 2 * HEADS
                    roots(at, at + HEADS, NOPE)
                    roots(at + HEADS, at + 2 * HEADS, ROPE)
            high_parts((None, 0), first_fills(*FIRST_END))
            split_hi(N_OUT)
            split_hi(N_OUT + 1)

            def take_values(h, b):
                a.activation(vs[b][:, :, 0:VDIM], kvn[:, :, bass.ds(h * (NOPE + VDIM) + NOPE, VDIM)],
                             ACT.Copy).then_inc(vs_ready, 1)

            def exponentials(head, j):
                n = SEQ - P_FROM[j]
                rows_ = min(P, L - key0(j))
                bank = st_bank(head, j)
                a.wait_ge(st_masked, count(head, KEY_TILES, j + 1))
                if not is_first(head) or j >= 3:
                    a.wait_ge(pv_done, count(head, KEY_TILES, j - 2))
                out = probT[j % 3][0:rows_, 0:n]
                skip = P_FROM[j] - S_FROM[j]
                if n > 512:
                    a.activation(out.rearrange("p (b c) -> p b c", b=2), ps[0:rows_, bank:bank + 2, 0:n // 2],
                                 ACT.Exp).then_inc(exp_done, 1)
                else:
                    a.activation(out, ps[0:rows_, bank, skip:skip + n], ACT.Exp).then_inc(exp_done, 1)

            def take_y(head, half):
                a.wait_ge(pv_done, count(head, KEY_TILES, 5 if half == 0 else KEY_TILES))
                if half == 0:
                    a.wait_ge(ya_ready, count(head, 1, 0))
                a.activation(y_raw[head[1] % 2][0:VDIM + 1, 512 * half:512 * (half + 1)],
                             ps[0:VDIM + 1, 4 + half, :], ACT.Copy).then_inc(y_taken, 1)

            def y_high(k):
                src, dst = (yp, yp_hi) if k < POOL_GROUPS else (ya, ya_hi)
                a.activation(dst[:, k % POOL_GROUPS, :], src[:, k % POOL_GROUPS, :], ACT.Copy)\
                    .then_inc(y_hi_ready, 1)

            def attend(head, steps, last=False, fills=True):
                for j in steps:
                    places = ((0, 1), (2, 3)) if j == KEY_TILES - 1 else ((0,), (1, 2, 3))
                    if fills:
                        high_parts(filled_in(head, j), fills_at(j, *places[0]))
                    if j < KEY_TILES - 2:
                        exponentials(head, j + 2)
                    elif not last:
                        exponentials(next_head(head), j + 2 - KEY_TILES)
                    if fills:
                        high_parts(filled_in(head, j), fills_at(j, *places[1]))
                    if j == 3 and not last:
                        n = next_head(head)
                        take_values(n[1] if n[0] is None else n[0] * 2 + n[1], n[1] % 2)
                    if j == 4:
                        take_y(head, 0)
                    if last and j < 5:
                        y_high(Y_ORDER[j])
                    if j == KEY_TILES - 1:
                        take_y(head, 1)
                        if last:
                            a.wait_ge(ya_ready, 1 + HEADS - 1)
                            y_high(Y_ORDER[5])
                            y_high(Y_ORDER[6])

            a.sem_inc(y_taken, 1)
            take_values(0, 0)
            exponentials((None, 0), 0)
            high_parts((None, 1), FILLS_AHEAD[:2])
            exponentials((None, 0), 1)
            high_parts((None, 1), FILLS_AHEAD[2:])
            attend((None, 0), BODY)
            with a.Fori(0, HEADS // 2 - 1) as i:
                for n in (1, 2):
                    attend((i, n - 1), END)
                    attend((i, n), BODY)
            attend((None, HEADS - 2), END, fills=False)
            attend((None, HEADS - 1), BODY, last=True, fills=False)
            attend((None, HEADS - 1), END, last=True, fills=False)
            a.wait_ge(ya_ready, 1 + HEADS)
            y_high(Y_ORDER[7])

            for d in range(KT):
                split_hi(N_OUT + d + 2)
                a.wait_ge(h2_ready, d + 1)
                a.activation(g_hi[:, d, :], resid[:, d, :], ACT.Copy,
                             scale=cols[:, C_FFN + d:C_FFN + d + 1]).then_inc(g_hi_ready, 1)
                if d >= 2:
                    a.wait_ge(g_sq_added, d - 1)
                a.activation((r_sq_tmp if d else r_sq)[:, :], resid[:, d, :], ACT.Square)\
                    .then_inc(g_sq_ready, 1)

            def gate_up(g, c, i, s):
                for j in range(2):
                    t = in_loop(i, 4, 2 * g + j)
                    split_hi(c + 2 * j + 2, i)
                    if i is None and g == 0 and j == 0:
                        a.wait_ge(ms2_done, 1)
                        a.activation(r2_root[:, :], psf[:, 4 * 512:4 * 512 + SEQ], ACT.Sqrt,
                                     bias=eps[:, :], scale=1.0 / D).then_inc(r2_root_ready, 1)
                    a.wait_ge(gate_in_ready, t + 1)
                    if not (i is None and g == 0 and j == 0):
                        a.wait_ge(act_ready, t)
                    a.activation(gate[:, :], gate_in[:, :], ACT.Silu).then_inc(silu_ready, 1)
                    split_hi(c + 2 * j + 3, i)
                    a.wait_ge(act_ready, t + 1)
                    a.activation(act_hi[s][j][:, :], act[:, :], ACT.Copy).then_inc(act_hi_ready, 1)

            def down(c, i):
                for j in range(2):
                    if c + j + 2 < N_ALL:
                        split_hi(c + j + 2, i)

            gate_up(0, N_F, None, 0)
            with a.Fori(0, LOOPS) as i:
                gate_up(1, N_L, i, 1)
                down(N_L + 4, i)
                gate_up(2, N_L + 6, i, 0)
                down(N_L + 10, i)

        @block.vector
        def _(v):
            steps = [0]

            def link(ins):
                steps[0] += 1
                ins.then_inc(dve_step, 1)
                v.wait_ge(dve_step, steps[0])

            def split_lo(c, i=None):
                w = 1024 if c >= N_F else early[c][1] * early[c][2]
                v.wait_ge(w_hi_ready, in_loop(i, PER, c + 1))
                v.tensor_tensor(w_lo[c % N_SPLIT][:, 0:w], w_raw[c % N_RAW][:, 0:w],
                                w_hi[c % N_SPLIT][:, 0:w].bitcast(F32), ALU.subtract)\
                    .then_inc(w_lo_ready, 1)

            for t in h_raw:
                v.memset(t[:, L:LP], 0.0).then_inc(pad_ready, 1)
            for t in (h_ms[:, NT:], kv_sum[:, NT:], krn[:, NT, :]):
                v.memset(t, 1.0).then_inc(pad_ready, 1)
            v.wait_ge(columns_landed, 16)
            for k in range(KT):
                v.wait_ge(h_hi_ready, k + 1)
                v.scalar_tensor_tensor(out=h_lo[k][:, :], in0=h_raw[k % N_H][:, :],
                                       scalar=cols[:, C_ATTN + k:C_ATTN + k + 1],
                                       in1=h_hi[k][:, :].bitcast(F32), op0=ALU.mult, op1=ALU.subtract)\
                    .then_inc(h_lo_ready, 1)
                if k == 0:
                    split_lo(0)
                    split_lo(1)
                else:
                    v.wait_ge(h_sq_ready, k + 1)
                    if k >= 2:
                        v.wait_ge(h_sq_added, k - 1)
                    v.tensor_tensor(h_sq[:, :], h_sq[:, :], square[:, :], ALU.add).then_inc(h_sq_added, 1)

            def z_view(step):
                b = z_banks(step)
                return ps[:, b:b + 3, 0:ZW]

            def tiles3(t):
                return t[:, :].rearrange("p (b c) -> p b c", b=3)

            def column_sums(out, col, n):
                return v.tensor_reduce(out, psf[:, col:col + n * P].rearrange("p (t c) -> p t c", c=P),
                                       AX.X, ALU.add)

            def last_sum(out, col):
                return v.tensor_reduce(out[0:META, NT:NT + 1], psf[0:META, col:col + P], AX.X, ALU.add)

            for s in range(N_STEPS):
                split_lo(s + 2)
                if s in Z_OF_STEP:
                    z = Z_OF_STEP[s]
                    v.wait_ge(z_hi_ready, z + 1)
                    v.wait_ge(z_act_done, ACT_READS[s])
                    v.scalar_tensor_tensor(out=tiles3(z_lo[z]), in0=z_view(s),
                                           scalar=cols[:, C_Z + z:C_Z + z + 1],
                                           in1=tiles3(z_hi[z]).bitcast(F32), op0=ALU.mult,
                                           op1=ALU.subtract).then_inc(z_dve_done, 1)
                    if s in (1, 4, 5):
                        acc = z_sq if s == 1 else h_sq
                        if s == 5:
                            v.wait_ge(z_sq_added, 2)
                        v.tensor_tensor(acc[:, :], acc[:, :], square[:, :], ALU.add)\
                            .then_inc(z_sq_added, 1)
                if s == 2:
                    v.wait_ge(aux_done, 1)
                    column_sums(h_ms[:, 0:NT], 6 * 512, NT).then_inc(aux_dve, 1)
                if s == 3:
                    v.wait_ge(aux_done, 2)
                    v.wait_ge(pad_ready, N_H + 3)
                    last_sum(h_ms, 6 * 512).then_inc(h_ms_ready, 1)
                    v.tensor_reduce(kv_sum[:, 0:4], ps[:, 7, :].rearrange("p (t c) -> p t c", c=P),
                                    AX.X, ALU.add)
                    v.wait_ge(h_root_ready, 1)
                    v.reciprocal(r_h[:, :], h_root[:, :]).then_inc(r_h_ready, 1)
                    v.wait_ge(r_h_ready, 1)
                    v.tensor_tensor(krn[:, 0:NT, :],
                                    ps[:, 6, P:P + NT * ROPE].rearrange("p (t c) -> p t c", c=ROPE),
                                    r_h[:, 0:NT, None].to_broadcast([P, NT, ROPE]), ALU.mult)
                    v.tensor_tensor(krn[0:META, NT, :], ps[0:META, 6, P + NT * ROPE:P + (NT + 1) * ROPE],
                                    r_h[0:META, NT:NT + 1].to_broadcast([META, ROPE]), ALU.mult)\
                        .then_inc(aux_dve, 1)
                if s == 5:
                    v.wait_ge(aux_done, 4)
                    v.wait_ge(aux_act, 3)
                    last_sum(kv_sum, 6 * 512 + 3 * P)
                    link(column_sums(kv_sum[:, 4:NT], 7 * 512, 4))
                    aux_read = v.tensor_tensor(r_h2[:, :], r_h[:, :], r_h[:, :], ALU.mult)
                    aux_read.then_inc(aux_dve, 1)
                    v.wait_ge(aux_dve, 3)
                    v.scalar_tensor_tensor(out=kv_ms[:, :], in0=kv_sum[:, :], scalar=1.0 / (2 * P),
                                           in1=r_h2[:, :], op0=ALU.mult, op1=ALU.mult)\
                        .then_inc(kv_ms_ready, 1)
                if s >= 6:
                    g = s - 6
                    v.wait_ge(w_used, s + 1)
                    if g == 0:
                        v.wait_ge(aux_act, 3)
                        v.wait_ge(pad_ready, N_H)
                    else:
                        v.wait_ge(p_hi_ready, g)
                    ub = u[:, :].rearrange("p (b c) -> p b c", b=3)
                    rb = r_bcast[:, :].rearrange("p (b c) -> p b c", b=3)
                    v.tensor_tensor(ub, z_view(s), rb, ALU.mult).then_inc(z_dve_done, 1)
                    v.wait_ge(z_dve_done, DVE_READS[s])
                    src, start = u, 0
                    for j in range(g + 1):
                        shift = 2 ** j
                        dst = win[(1 + g + g - j) % 2]
                        start += shift
                        link(v.tensor_tensor(dst[:, start:L], src[:, start:L],
                                             src[:, start - shift:L - shift], ALU.add))
                        src = dst
                    v.scalar_tensor_tensor(out=win[g % 2][:, META:L], in0=src[:, META:L],
                                           scalar=1.0 / 2 ** (g + 1), in1=u[:, META:L],
                                           op0=ALU.mult, op1=ALU.subtract).then_inc(p_ready, 1)
                    v.wait_ge(p_hi_ready, g + 1)
                    v.tensor_tensor(p_lo[:, g, :], win[g % 2][:, META:L],
                                    p_hi[:, g, :].bitcast(F32), ALU.subtract).then_inc(p_lo_ready, 1)
                if s == 6:
                    v.wait_ge(kv_root_ready, 1)
                    link(v.reciprocal(kv_inv[:, :], kv_root[:, :]))
                    v.tensor_tensor(s_kv[:, :], kv_inv[:, :], r_h[:, :], ALU.mult).then_inc(s_kv_ready, 1)
                    v.wait_ge(aux_done, 5)
                    column_sums(q_sum[:, :], 6 * 512, NT).then_inc(aux_dve, 1)
                if s == 7:
                    v.wait_ge(aux_done, 6)
                    link(v.tensor_copy(r_hq[:, :], psf[:, 6 * 512:6 * 512 + NT * 32]
                                       .rearrange("p (t c) -> p t c", c=32)[:, :, 0:1]
                                       .rearrange("p t c -> p (t c)")))
                    link(v.tensor_tensor(r_hq2[:, :], r_hq[:, :], r_hq[:, :], ALU.mult))
                    v.wait_ge(aux_dve, 4)
                    v.scalar_tensor_tensor(out=q_ms[:, :], in0=q_sum[:, :], scalar=1.0 / (3 * P),
                                           in1=r_hq2[:, :], op0=ALU.mult, op1=ALU.mult)\
                        .then_inc(q_ms_ready, 1)
                if s == 8:
                    v.wait_ge(q_root_ready, 1)
                    link(v.reciprocal(q_inv[:, :], q_root[:, :]))
                    v.tensor_tensor(s_q[:, :], q_inv[:, :], r_hq[:, :], ALU.mult).then_inc(s_q_ready, 1)
                    v.tensor_scalar(q_scale_col[:, :], cols[:, C_QN:C_QN + 1], SCALE, None, ALU.mult)\
                        .then_inc(q_scale_ready, 1)

            v.wait_ge(w_used, N_STEPS)
            v.memset(kvn[:, NT, :], 0.0).then_inc(kv_pad_ready, 1)
            v.memset(max_parts[:, :, :], MASKED).then_inc(ones_ready, 1)
            v.wait_ge(ones_ready, 1)

            def take_fills(head, fills):
                b = head[1] % 2
                for x, fill in fills:
                    bank = 6 + x % 2
                    if fill[0] in "qk":
                        hi, gain = transposed(qT_hi, kT_hi, b, *fill)
                        lo, _ = transposed(qT_lo, kT_lo, b, *fill)
                        v.wait_ge(prep_hi_ready, prep_count(head, x))
                        v.scalar_tensor_tensor(out=lo, in0=ps[0:HD, bank, 0:lo.shape[1]], scalar=gain[0:HD, :],
                                               in1=hi.bitcast(F32), op0=ALU.mult, op1=ALU.subtract)\
                            .then_inc(misc_free, 1)
                    elif fill[0] == "n":
                        _, i, m, parts, width = fill
                        v.wait_ge(misc_filled, fill_count(head, x + 1))
                        if m == parts - 1:
                            diagonal = ps[:, bank, width - P:width]
                            v.tensor_tensor(diagonal, diagonal, causal[:, :], ALU.add).then_inc(nat_masked, 1)
                            v.wait_ge(nat_masked, count(head, NT, i + 1))
                        v.tensor_reduce(max_parts[:, i, m:m + 1], ps[:, bank, 0:width], AX.X, ALU.max)\
                            .then_inc(misc_free, 1)
                        if i == NT - 1 and m == parts - 1:
                            v.wait_ge(misc_free, fill_count(head, x + 1))
                            v.tensor_reduce(neg_max[:, :], max_parts[:, :, :], AX.X, ALU.max, negate=True)\
                                .then_inc(neg_max_ready, 1)
                    else:
                        v.wait_ge(misc_filled, fill_count(head, x + 1))
                        if not is_first(head):
                            v.wait_ge(m_landed, count(head, 16, 0))
                        v.tensor_copy(neg_max8[:, :], ps[0:NT, bank, 0:P]).then_inc(misc_free, 1)

            for j in range(N_JOBS):
                if j == 0:
                    split_lo(N_POOL)
                if j == J_POOL - 1:
                    split_lo(N_Q)
                if j == J_POOL:
                    v.wait_ge(aux_dve, 3)
                    link(v.tensor_tensor(kr_b[:, :, :], krn[:, :, :], krn[:, :, :], ALU.mult))
                    v.tensor_reduce(ssq[:, KR:QS], kr_b[:, :, :], AX.X, ALU.add).then_inc(ssq_added, 1)
                    split_lo(N_Q + 1)
                    v.wait_ge(root_ready, 2)
                    v.reciprocal(rs[:, 0:QS], ssq[:, 0:QS]).then_inc(rs_k_ready, 1)
                if j == J_Q:
                    split_lo(N_Q + 2)
                    v.memset(kT_hi[0][HD:HD + 1, :].bitcast(F32), 1.0).then_inc(ones_ready, 1)
                if j < J_POOL:
                    v.wait_ge(sq_ready, j + 1)
                    v.tensor_reduce(ssq[:, KN + j * HEADS:KN + (j + 1) * HEADS],
                                    sq_tmp[j % 2][:, 0:HEADS * NOPE].rearrange("p (h c) -> p h c", h=HEADS),
                                    AX.X, ALU.add).then_inc(ssq_added, 1)
                elif j >= J_Q:
                    t = j - J_Q
                    take_fills((None, 0), first_fills(*FIRST_IN[t]))
                    v.wait_ge(q_sq_ready, t + 1)
                    squares = sq_tmp[t % 2][:, :].rearrange("p (h c) -> p h c", h=HEADS)
                    at = QS + t * 2 * HEADS
                    v.tensor_reduce(ssq[:, at:at + HEADS], squares[:, :, 0:NOPE], AX.X, ALU.add)
                    v.tensor_reduce(ssq[:, at + HEADS:at + 2 * HEADS], squares[:, :, NOPE:HD], AX.X, ALU.add)\
                        .then_inc(ssq_added, 1)
                    v.wait_ge(root_ready, 2 + 2 * (t + 1))
                    v.reciprocal(rs[:, at:at + 2 * HEADS], ssq[:, at:at + 2 * HEADS]).then_inc(rs_ready, 1)
            take_fills((None, 0), first_fills(*FIRST_END))

            def invert_sums(head):
                v.wait_ge(l_landed, count(head, 16, 16))
                v.reciprocal(inv_denom[:, :], denom[:, :]).then_inc(inv_denom_ready, 1)

            def y_low(k):
                src, hi, lo = (yp, yp_hi, yp_lo) if k < POOL_GROUPS else (ya, ya_hi, ya_lo)
                at = k % POOL_GROUPS
                v.wait_ge(y_hi_ready, Y_ORDER.index(k) + 1)
                v.tensor_tensor(lo[:, at, :], src[:, at, :], hi[:, at, :].bitcast(F32), ALU.subtract)\
                    .then_inc(y_lo_ready, 1)

            def mask(head, j):
                first = P * j - META
                lo, hi = P_FROM[j], min(first + P, SEQ)
                rows_ = min(P, L - key0(j))
                at = ps[0:rows_, st_bank(head, j), lo - S_FROM[j]:hi - S_FROM[j]]
                m = lo - first + AHEAD
                v.wait_ge(st_done, count(head, KEY_TILES, j + 1))
                v.tensor_tensor(at, at, causal_t[0:rows_, m:m + hi - lo], ALU.add).then_inc(st_masked, 1)

            def attend(head, steps, previous=None, last=False, fills=True):
                for j in steps:
                    if j < KEY_TILES - 2:
                        mask(head, j + 2)
                    elif not last:
                        mask(next_head(head), j + 2 - KEY_TILES)
                    if fills:
                        take_fills(filled_in(head, j), fills_at(j, 0))
                    if fills and j == TAIL + 1:
                        take_fills(filled_in(head, j - 1), fills_at(j - 1, 1, 2, 3))
                    if fills and j != TAIL:
                        take_fills(filled_in(head, j), fills_at(j, 1, 2, 3))
                    if previous is not None and j == 1:
                        invert_sums(previous)
                    if last and j < 2:
                        split_lo(N_OUT + j)
                    elif last and j < 5:
                        y_low(Y_ORDER[j - 2])

            v.wait_ge(proj_act, N_JOBS)
            v.wait_ge(kr_ready, 1)
            v.memset(kT_hi[1][HD:HD + 1, :].bitcast(F32), 1.0).then_inc(ones_ready, 1)
            for b in range(2):
                v.memset(vs[b][:, :, VDIM:VDIM + 1], 1.0).then_inc(ones_ready, 1)
            mask((None, 0), 0)
            mask((None, 0), 1)
            take_fills((None, 1), FILLS_AHEAD)
            attend((None, 0), BODY)
            with v.Fori(0, HEADS // 2 - 1) as i:
                for n in (1, 2):
                    attend((i, n - 1), END)
                    attend((i, n), BODY, previous=(i, n - 1))
            attend((None, HEADS - 2), END, fills=False)
            attend((None, HEADS - 1), BODY, previous=(None, HEADS - 2), last=True, fills=False)
            attend((None, HEADS - 1), END, last=True, fills=False)
            for k in Y_ORDER[3:7]:
                y_low(k)
            invert_sums((None, HEADS - 1))
            divide(v, (None, HEADS - 1))
            y_low(Y_ORDER[7])

            for d in range(KT):
                split_lo(N_OUT + d + 2)
                v.wait_ge(w_used, N_OUT + d + 1)
                v.wait_ge(resid_landed, 16 * KT)
                b = 2 * (d % 2)
                v.tensor_tensor(resid[:, d, :], psf[:, b * 512:b * 512 + SEQ], resid[:, d, :], ALU.add)\
                    .then_inc(h2_ready, 1)
                v.wait_ge(g_hi_ready, d + 1)
                v.scalar_tensor_tensor(out=g_lo[:, d, :], in0=resid[:, d, :],
                                       scalar=cols[:, C_FFN + d:C_FFN + d + 1],
                                       in1=g_hi[:, d, :].bitcast(F32), op0=ALU.mult, op1=ALU.subtract)\
                    .then_inc(g_lo_ready, 1)
                if d >= 1:
                    v.wait_ge(g_sq_ready, d + 1)
                    if d >= 2:
                        v.wait_ge(g_sq_added, d - 1)
                    v.tensor_tensor(r_sq[:, :], r_sq[:, :], r_sq_tmp[:, :], ALU.add)\
                        .then_inc(g_sq_added, 1)

            def gate_up(g, c, i, s, down_next=True):
                for j in range(2):
                    first = i is None and g == 0 and j == 0
                    t = in_loop(i, 4, 2 * g + j)
                    after = in_loop(i, 4, 2 * g + j + 1)
                    split_lo(c + 2 * j + 2, i)
                    if first:
                        v.wait_ge(r2_root_ready, 1)
                        v.reciprocal(r2[:, :], r2_root[:, :]).then_inc(r2_ready, 1)
                        v.wait_ge(r2_ready, 1)
                        v.sem_inc(down_bank_free, 4)
                    else:
                        v.wait_ge(silu_ready, t)
                    v.wait_ge(w_used, in_loop(i, PER, c + 2 * j + 1))
                    v.tensor_tensor(gate_in[:, :], psf[:, 0:SEQ], r2[:, :], ALU.mult)\
                        .then_inc(gate_in_ready, 1)
                    split_lo(c + 2 * j + 3, i)
                    v.wait_ge(w_used, in_loop(i, PER, c + 2 * j + 2))
                    v.tensor_tensor(up[:, :], psf[:, SEQ:2 * SEQ], r2[:, :], ALU.mult).then_inc(up_ready, 1)
                    v.wait_ge(up_ready, after)
                    v.wait_ge(silu_ready, after)
                    v.tensor_tensor(act[:, :], gate[:, :], up[:, :], ALU.mult).then_inc(act_ready, 1)
                    if j == 0 or not down_next:
                        act_low(g, i, s, j)

            def act_low(g, i, s, j):
                v.wait_ge(act_hi_ready, in_loop(i, 4, 2 * g + j + 1))
                v.tensor_tensor(act_lo[s][j][:, :], act[:, :], act_hi[s][j][:, :].bitcast(F32),
                                ALU.subtract).then_inc(act_lo_ready, 1)

            def down(g, c, i, s):
                for x in range(2 * KT):
                    if x == 2 and s is not None:
                        act_low(g + 1, i, s, 1)
                    if x == 5 and c + 2 < N_ALL:
                        split_lo(c + 2, i)
                    d, half = x // 2, x % 2
                    out = resid[:, d, 512 * half:512 * (half + 1)]
                    if x < 2 * KT - 1:
                        v.wait_ge(down_done, in_loop(i, 2 * (2 * KT - 1), (2 * KT - 1) * g + x + 1))
                    else:
                        v.wait_ge(w_used, in_loop(i, PER, c + 2))
                    v.tensor_tensor(out, ps[:, 4 + x % 4, :], out, ALU.add).then_inc(down_bank_free, 1)
                if c + 3 < N_ALL:
                    split_lo(c + 3, i)

            gate_up(0, N_F, None, 0, down_next=False)
            with v.Fori(0, LOOPS) as i:
                gate_up(1, N_L, i, 1)
                down(0, N_L + 4, i, 1)
                gate_up(2, N_L + 6, i, 0)
                down(1, N_L + 10, i, 0)
            down(GROUPS - 1, N_ALL - 2, None, None)

        @block.tensor
        def _(pe):
            def passes(out, w_h, w_l, x_h, x_l, first, last):
                pe.matmul(out, w_h, x_h, start=first, stop=False)
                pe.matmul(out, w_h, x_l, start=False, stop=False)
                return pe.matmul(out, w_l, x_h, start=False, stop=last)

            def weights(c, k, width, m):
                s = c % N_SPLIT
                return (w_hi[s][:, k * width:k * width + m], w_lo[s][:, k * width:k * width + m])

            def z_step(s, k):
                w = IN_COLS[s][1]
                w_h, w_l = weights(s, k, w, w)
                for b in range(3):
                    x = slice(b * ZW, (b + 1) * ZW)
                    last = passes(ps[0:w, z_banks(s) + b, 0:ZW], w_h, w_l, h_hi[k][:, x], h_lo[k][:, x],
                                  k == 0, k == KT - 1)
                return last

            def transpose_tiles(src, starts, col):
                for n, start in enumerate(starts):
                    last = pe.transpose(psf[:, col + n * P:col + (n + 1) * P], src[:, start:start + P],
                                        ident[:, :])
                return last

            def transpose_last(src, col):
                return pe.transpose(psf[0:META, col:col + P], src[:, key0(NT):L], ident[:, :])

            for s, k in [(s, k) for k in range(KT - EARLY) for s in range(2)] + \
                        [(s, k) for s in range(2) for k in range(KT - EARLY, KT)]:
                if s == 0:
                    pe.wait_ge(h_lo_ready, k + 1)
                if k == 0:
                    pe.wait_ge(w_lo_ready, s + 1)
                last = z_step(s, k)
                if k == KT - 1:
                    last.then_inc(w_used, 1)
            for s in range(2, N_STEPS):
                pe.wait_ge(w_lo_ready, s + 1)
                pe.wait_ge(z_act_done, ACT_READS[s - 2])
                pe.wait_ge(z_dve_done, DVE_READS[s - 2])
                for k in range(KT):
                    last = z_step(s, k)
                last.then_inc(w_used, 1)
                if s == 2:
                    pe.wait_ge(const_ready, 5)
                    pe.wait_ge(h_sq_added, KT - 1)
                    transpose_tiles(h_sq, [key0(t) for t in range(NT)], 6 * 512).then_inc(aux_done, 1)
                if s == 3:
                    pe.wait_ge(aux_dve, 1)
                    transpose_last(h_sq, 6 * 512)
                    pe.wait_ge(z_act_done, 3)
                    for t in range(NT + 1):
                        n = min(P, L - key0(t))
                        pe.transpose(psf[0:n, 6 * 512 + P + t * ROPE:6 * 512 + P + (t + 1) * ROPE],
                                     zr[:, key0(t):key0(t) + n], ident[0:ROPE, 0:ROPE])
                    pe.wait_ge(z_sq_added, 1)
                    transpose_tiles(z_sq, [key0(t) for t in range(4)], 7 * 512).then_inc(aux_done, 1)
                if s == 4:
                    pe.wait_ge(r_h_ready, 1)
                    pe.wait_ge(aux_dve, 2)
                    for t in range(6):
                        last = pe.matmul(psf[:, 6 * 512 + t * P:6 * 512 + (t + 1) * P],
                                         r_h[:, t:t + 1].to_broadcast([P, P]), ident[:, :],
                                         start=True, stop=True)
                    last.then_inc(aux_done, 1)
                if s == 5:
                    pe.wait_ge(aux_act, 2)
                    for t in range(6, NT):
                        pe.matmul(ps[:, 6, (t - 6) * P:(t - 5) * P], r_h[:, t:t + 1].to_broadcast([P, P]),
                                  ident[:, :], start=True, stop=True)
                    pe.matmul(ps[:, 6, 2 * P:2 * P + META], r_h[0:META, NT:NT + 1].to_broadcast([META, P]),
                              ident[0:META, 0:META], start=True, stop=True)
                    transpose_last(z_sq, 6 * 512 + 3 * P)
                    transpose_tiles(z_sq, [key0(t) for t in range(4, NT)], 7 * 512).then_inc(aux_done, 1)
                if s == 6:
                    pe.wait_ge(aux_dve, 3)
                    pe.wait_ge(z_sq_added, 3)
                    transpose_tiles(h_sq, [token0(t) for t in range(1, NT + 1)], 6 * 512).then_inc(aux_done, 1)
                if s == 7:
                    pe.wait_ge(aux_act, 3)
                    pe.wait_ge(aux_dve, 4)
                    for t in range(NT):
                        last = pe.transpose(psf[:, 6 * 512 + t * 32:6 * 512 + (t + 1) * 32],
                                            r_bcast[0:32, token0(t + 1):token0(t + 1) + P], ident[0:32, 0:32])
                    last.then_inc(aux_done, 1)

            def open_job(j):
                if j == 0:
                    pe.wait_ge(q_ms_ready, 1)
                elif j <= 3:
                    pe.wait_ge(z_dve_done, DVE_READS[-1])
                if j >= J_Q + 3:
                    pe.wait_ge(proj_act, j - 2)
                elif j >= J_Q:
                    pe.wait_ge(proj_act, J_POOL + j - J_Q + 1)
                elif j >= 4:
                    pe.wait_ge(proj_act, j - 3)
                return job_bank(j)

            def token_major(j, start, rows_, z0, n_k, tile, width, fills=()):
                b = open_job(j)
                x = slice(start, start + rows_)
                for k in range(n_k):
                    pe.wait_ge(w_lo_ready, tile + k + 1)
                    w_h, w_l = w_hi[(tile + k) % N_SPLIT], w_lo[(tile + k) % N_SPLIT]
                    z_h, z_l = z_hi[z0 + k], z_lo[z0 + k]
                    for half in range(2):
                        c = slice(half * width, (half + 1) * width)
                        last = passes(ps[0:rows_, b + half, 0:width], z_h[:, x], z_l[:, x], w_h[:, c], w_l[:, c],
                                      k == 0, k == n_k - 1)
                    if j in JOB_ENDS or k == n_k - 1:
                        last.then_inc(w_used if j in JOB_ENDS else proj_done, 1)
                    if fills:
                        cuts = [0, 1, 1 + len(fills) // 2, len(fills)]
                        fill((None, 0), fills[cuts[k]:cuts[k + 1]])

            def fill(head, fills):
                for x, f in fills:
                    b = head[1] % 2
                    bank = 6 + x % 2
                    if not is_first(head) or x >= 2:
                        pe.wait_ge(misc_free, fill_count(head, x - 1))
                    if f[0] in "qk":
                        if is_first(head) and f[0] == "q":
                            pe.wait_ge(head0_ready, f[1][0] + 1)
                        elif f[0] == "q" and x == 0:
                            pe.wait_ge(qs_ready, count(head, 1, 0))
                        if f[0] == "k" and f[1][0] == 0:
                            pe.wait_ge(ks_ready, count(head, 1, 1))
                        src = qs if f[0] == "q" else ks
                        for n, t in enumerate(f[1]):
                            rows_ = P if f[0] == "q" else min(P, L - key0(t))
                            last = pe.transpose(ps[0:HD, bank, n * P:n * P + rows_], src[0:rows_, t, :],
                                                ident[0:rows_, 0:rows_])
                    elif f[0] == "n":
                        _, i, m, parts, width = f
                        if is_first(head):
                            pe.wait_ge(prep_hi_ready, prep_count(head, x))
                        elif m == 0 and (i == 0 or last_prep(i) > last_prep(i - 1)):
                            pe.wait_ge(prep_hi_ready, prep_count(head, last_prep(i)))
                        start = m * (META + P * (i + 1)) // parts if parts < 3 else m * 352
                        last = pe.matmul(ps[:, bank, 0:width], qT_hi[b][0:HD, i * P:(i + 1) * P],
                                         kT_hi[b][0:HD, start:start + width], start=True, stop=True)
                    else:
                        pe.wait_ge(neg_max_ready, count(head, 1, 1))
                        last = pe.transpose(ps[0:NT, bank, 0:P], neg_max[:, :], ident[:, :])
                    last.then_inc(misc_filled, 1)

            pe.wait_ge(z_dve_done, DVE_READS[5])
            for t in range(NT + 1):
                token_major(t, key0(t), min(P, L - key0(t)), 0, 2, N_KV, KVW // 2)
            pe.wait_ge(w_lo_ready, N_POOL + 1)
            for g in range(POOL_GROUPS):
                j = J_POOL + g
                b = open_job(j)
                pe.wait_ge(p_lo_ready, g + 1)
                w_h, w_l = weights(N_POOL, g, P, P)
                for half in range(2):
                    x = slice(512 * half, 512 * (half + 1))
                    last = passes(ps[:, b + half, :], w_h, w_l, p_hi[:, g, x], p_lo[:, g, x], True, True)
                last.then_inc(w_used if j in JOB_ENDS else proj_done, 1)
            for t in range(NT):
                if t == 1:
                    pe.wait_ge(proj_act, J_Q)
                token_major(J_Q + t, token0(t + 1), P, 2, 3, N_Q, QW // 2, first_fills(*FIRST_IN[t]))
            fill((None, 0), first_fills(*FIRST_END))

            def key_tile(head, j, amid=(None, []), low=True, high=True):
                b, bank = head[1] % 2, st_bank(head, j)
                rows_ = min(P, L - key0(j))
                n = SEQ - S_FROM[j]
                parts = 2 if n > 512 else 1
                width = n // parts
                k = slice(key0(j), key0(j) + rows_)
                if high and j == 0:
                    pe.wait_ge(m_landed, count(head, 16, 16))
                for m in range(parts):
                    c = slice(S_FROM[j] + m * width, S_FROM[j] + (m + 1) * width)
                    out = ps[0:rows_, bank + m, 0:width]
                    if low:
                        pe.matmul(out, kT_hi[b][0:HD, k], qT_lo[b][0:HD, c], start=True, stop=False)
                        pe.matmul(out, kT_lo[b][0:HD, k], qT_hi[b][0:HD, c], start=False, stop=False)
                    if high:
                        last = pe.matmul(out, kT_hi[b][0:HD + 1, k], qT_hi[b][0:HD + 1, c],
                                         start=False, stop=True)
                        if m == parts - 1:
                            last.then_inc(st_done, 1)
                    if m == 0:
                        fill(*amid)

            def values(head, j, amid=(None, [])):
                b = head[1] % 2
                rows_ = min(P, L - key0(j))
                if j == 0:
                    pe.wait_ge(vs_ready, count(head, 1, 1))
                    pe.wait_ge(y_taken, count(head, 2, 1))
                for half in range(2):
                    lo, hi = max(P_FROM[j], 512 * half), 512 * (half + 1)
                    if lo < hi:
                        last = pe.matmul(ps[0:VDIM + 1, 4 + half, lo - 512 * half:512], vs[b][0:rows_, j, :],
                                         probT[j % 3][0:rows_, lo - P_FROM[j]:hi - P_FROM[j]],
                                         start=j == 0, stop=j == (4 if half == 0 else KEY_TILES - 1))
                    if half == 0:
                        fill(*amid)
                last.then_inc(pv_done, 1)

            def attend(head, steps, last=False, fills=True):
                for j in steps:
                    pe.wait_ge(exp_done, count(head, KEY_TILES, j + 1))

                    def fills_now(place):
                        return filled_in(head, j), fills_at(j, place) if fills else []

                    if j < KEY_TILES - 2:
                        key_tile(head, j + 2, fills_now(0))
                    elif not last:
                        key_tile(next_head(head), j + 2 - KEY_TILES, fills_now(0))
                    fill(*fills_now(1))
                    values(head, j, fills_now(2))
                    fill(*fills_now(3))

            pe.wait_ge(proj_act, N_JOBS)
            for j in (0, 1):
                key_tile((None, 0), j, high=False)
            pe.wait_ge(ones_ready, 5)
            for j in (0, 1):
                key_tile((None, 0), j, low=False)
            fill((None, 1), FILLS_AHEAD)
            attend((None, 0), BODY)
            with pe.Fori(0, HEADS // 2 - 1) as i:
                for n in (1, 2):
                    attend((i, n - 1), END)
                    attend((i, n), BODY)
            attend((None, HEADS - 2), END, fills=False)
            attend((None, HEADS - 1), BODY, last=True, fills=False)
            attend((None, HEADS - 1), END, last=True, fills=False)

            y_of = [(yp_hi, yp_lo, k) for k in range(POOL_GROUPS)] + \
                   [(ya_hi, ya_lo, k) for k in range(HEADS // 2)]
            parts = [(0, Y_ORDER[:-1]), (1, Y_ORDER[:-1]), (0, Y_ORDER[-1:]), (1, Y_ORDER[-1:])] + \
                    [(d, Y_ORDER) for d in range(2, KT)]
            for d, blocks in parts:
                n = N_OUT + d
                pe.wait_ge(w_lo_ready, n + 1)
                if d >= 2:
                    pe.wait_ge(h2_ready, d - 1)
                for k in blocks:
                    if d == 0:
                        pe.wait_ge(y_lo_ready, Y_ORDER.index(k) + 1)
                    y_h, y_l, at_k = y_of[k]
                    w_h, w_l = weights(n, k, P, P)
                    for half in range(2):
                        x = slice(512 * half, 512 * (half + 1))
                        last = passes(ps[:, 2 * (d % 2) + half, :], w_h, w_l, y_h[:, at_k, x],
                                      y_l[:, at_k, x], k == Y_ORDER[0], k == Y_ORDER[-1])
                if blocks[-1] == Y_ORDER[-1]:
                    last.then_inc(w_used, 1)

            def ffn_in(c, i, bank, t, first):
                pe.wait_ge(w_lo_ready, in_loop(i, PER, c + 1))
                for k in range(KT):
                    if first:
                        pe.wait_ge(g_lo_ready, k + 1)
                    w_h, w_l = weights(c, k, P, P)
                    for half in range(2):
                        x = slice(512 * half, 512 * (half + 1))
                        last = passes(ps[:, bank + half, :], w_h, w_l, g_hi[:, k, x], g_lo[:, k, x],
                                      k == 0, k == KT - 1)
                last.then_inc(w_used, 1)

            def gate_up(g, c, i):
                for j in range(2):
                    first = i is None and g == 0 and j == 0
                    t = in_loop(i, 4, 2 * g + j)
                    if first:
                        pe.wait_ge(h2_ready, KT - 1)
                    else:
                        pe.wait_ge(gate_in_ready, t)
                    ffn_in(c + 2 * j, i, 0, t, first)
                    if first:
                        pe.wait_ge(g_sq_added, KT - 1)
                        for half in range(2):
                            last = pe.matmul(ps[:, 4 + half, :], ones[:, :],
                                             r_sq[:, 512 * half:512 * (half + 1)], start=True, stop=True)
                        last.then_inc(ms2_done, 1)
                        pe.wait_ge(h2_ready, KT)
                    else:
                        pe.wait_ge(up_ready, t)
                    ffn_in(c + 2 * j + 1, i, 2, t, False)

            def down(g, c, i, s):
                pe.wait_ge(act_lo_ready, in_loop(i, 4, 2 * g + 2))
                banks = 4 if i is None else 1
                order = [(x + b, j) for x in range(0, 2 * KT, banks) for j in range(2) for b in range(banks)]
                for x, j in order:
                    d, half = x // 2, x % 2
                    tok = slice(512 * half, 512 * (half + 1))
                    if x == 0:
                        pe.wait_ge(w_lo_ready, in_loop(i, PER, c + j + 1))
                    if j == 0:
                        pe.wait_ge(down_bank_free, in_loop(i, 4 * KT, 2 * KT * g + x + 1))
                    w_h, w_l = weights(c + j, d, P, P)
                    last = passes(ps[:, 4 + x % 4, :], w_h, w_l, act_hi[s][j][:, tok], act_lo[s][j][:, tok],
                                  j == 0, j == 1)
                    if x == 2 * KT - 1:
                        last.then_inc(w_used, 1)
                    elif j == 1:
                        last.then_inc(down_done, 1)

            gate_up(0, N_F, None)
            with pe.Fori(0, LOOPS) as i:
                gate_up(1, N_L, i)
                down(0, N_L + 4, i, 0)
                gate_up(2, N_L + 6, i)
                down(1, N_L + 10, i, 1)
            down(GROUPS - 1, N_ALL - 2, None, 0)


def kernel(x, meta_tokens, attn_norm_g, w_in, w_pool, pool_scale, q_a_norm_g, w_q_b, kv_a_norm_g, w_kv_b,
           q_norm_g, k_norm_g, w_out, ffn_norm_g, w_gate, w_up, w_down):
    import numpy as np
    from concourse import bacc
    from concourse.bass_utils import run_bass_kernel_spmd

    x, meta_tokens = np.asarray(x), np.asarray(meta_tokens)
    length = meta_tokens.shape[0] + x.shape[1]
    n_tiles = x.shape[1] // P

    xT = np.ascontiguousarray(np.concatenate([meta_tokens, x[0]], axis=0).T)

    def blocks(g):
        return np.asarray(g)[0].reshape(-1, P).T

    def head_gain(g):
        return np.concatenate([np.asarray(g)[0, :NOPE], np.ones(P - NOPE, np.float32)])[:, None]

    columns = np.ascontiguousarray(np.concatenate(
        [blocks(attn_norm_g), blocks(ffn_norm_g), blocks(kv_a_norm_g), blocks(q_a_norm_g),
         blocks(pool_scale), head_gain(q_norm_g), head_gain(k_norm_g)], axis=1))
    rows = np.ascontiguousarray(np.broadcast_to(
        np.concatenate([np.asarray(q_norm_g)[0, NOPE:], np.asarray(k_norm_g)[0, NOPE:]]), (P, 2 * ROPE)))

    inv = 1.0 / (np.float32(10000.0) ** (np.arange(0, ROPE, 2, dtype=np.float32) / np.float32(ROPE)))
    starts = [token0(t + 1) for t in range(n_tiles)] + [key0(t) for t in range(n_tiles + 1)]
    token = np.stack([start + np.arange(P) for start in starts], axis=1)
    angle = token.astype(np.float32)[:, :, None] * inv[None, None, :].astype(np.float32)
    cos, sin = np.cos(angle).astype(np.float32), np.sin(angle).astype(np.float32)
    rope_cos = np.ascontiguousarray(np.concatenate([cos, cos], axis=2))
    rope_sin = np.ascontiguousarray(np.concatenate([-sin, sin], axis=2))

    nc = bacc.Bacc("TRN2", target_bir_lowering=False, num_devices=1)
    arrays, args = {}, []
    for name, a in [("xT", xT), ("w_in", w_in), ("w_pool", w_pool), ("w_q_b", w_q_b), ("w_kv_b", w_kv_b),
                    ("w_out", w_out), ("w_gate", w_gate), ("w_up", w_up), ("w_down", w_down),
                    ("columns", columns), ("rows", rows), ("rope_cos", rope_cos), ("rope_sin", rope_sin)]:
        arrays[f"in_{name}"] = np.ascontiguousarray(a)
        args.append(nc.dram_tensor(f"in_{name}", arrays[f"in_{name}"].shape, F32, kind="ExternalInput").ap())
    outT = nc.dram_tensor("outT", (x.shape[2], x.shape[1]), F32, kind="ExternalOutput").ap()
    inverses = nc.dram_tensor("inverses", (n_tiles * P // 16, 16), F32, kind="Internal").ap()
    build(nc, *args, inverses, outT)
    got = run_bass_kernel_spmd(nc, [arrays], core_ids=[0]).results[0]["outT"]
    return np.ascontiguousarray(np.asarray(got).T)[None]
```
